# Optimizing a Trainium2 kernel written in Bass

```python
import jax, jax.numpy as jnp
from jax import lax
import numpy as np

D_MODEL = 1024
BATCH = 1
SEQ = 512
DEPTH = 2

N_MIXERS = 2
RWKV_HEAD_SIZE = 64
RWKV_HEADS = D_MODEL // RWKV_HEAD_SIZE
DECAY_LORA = 64
AAA_LORA = 64
GATE_LORA = 160
GN_EPS = 64e-5
N_SHIFT_BRANCHES = 6
POOL_WINDOWS = (2, 4, 8, 16)
POOL_GROUPS = 4
POOL_GROUP_WIDTH = D_MODEL // POOL_GROUPS
PEER_HEADS = 8
N_KEYS = 128
N_EXPERTS = N_KEYS * N_KEYS
PEER_TOPK = 16
PEER_DK = 256
PEER_DK_HALF = PEER_DK // 2
PEER_BLOCK = 128
ALPHA = (2 * DEPTH) ** 0.25
BETA = (8 * DEPTH) ** -0.25
LN_EPS = 1e-5
N_MOD = 6

kernel_name = 'hybrid_rwkv7_pool_peer_deepnorm_adaln'

def layer_norm(x, g, b):
    xf = x.astype(jnp.float32)
    mu = jnp.mean(xf, axis=-1, keepdims=True)
    var = jnp.mean(jnp.square(xf - mu), axis=-1, keepdims=True)
    return ((xf - mu) * lax.rsqrt(var + LN_EPS)).astype(x.dtype) * g + b

def wkv7_scan(r, decay, k, v, a_vec, b_vec):
    B, S, H, N = r.shape

    def step(state, inp):
        r_t, w_t, k_t, v_t, a_t, b_t = inp
        sa = jnp.einsum('bhvk,bhk->bhv', state, a_t)
        state = (state * w_t[:, :, None, :] + sa[..., None] * b_t[:, :, None, :]
                 + v_t[..., None] * k_t[:, :, None, :])
        y = jnp.einsum('bhvk,bhk->bhv', state, r_t)
        return state, y

    xs = tuple(jnp.moveaxis(t, 1, 0) for t in (r, decay, k, v, a_vec, b_vec))
    s0 = jnp.zeros((B, H, N, N), jnp.float32)
    _, ys = lax.scan(step, s0, xs)
    return jnp.moveaxis(ys, 0, 1)

def rwkv7_time_mix(h, mu, w_rkv, w0, w1, w2, a0, a1, a2, g1, g2, k_k, k_a, r_k, lnx_g, lnx_b, w_o):
    B, S, D = h.shape
    H, N = RWKV_HEADS, RWKV_HEAD_SIZE
    f32 = jnp.float32
    xx = jnp.pad(h, ((0, 0), (1, 0), (0, 0)))[:, :-1] - h
    xs = h[None] + xx[None] * mu[:, None, None, :]
    r, k, v = jnp.einsum('nbsd,nde->nbse', xs[:3], w_rkv)
    w = -jax.nn.softplus(-(w0 + jnp.tanh(xs[3] @ w1) @ w2).astype(f32)) - 0.5
    decay = jnp.exp(-jnp.exp(w))
    a = jax.nn.sigmoid(a0 + (xs[4] @ a1) @ a2)
    g = jax.nn.sigmoid(xs[5] @ g1) @ g2
    kk = (k * k_k).astype(f32).reshape(B, S, H, N)
    kk = kk * lax.rsqrt(jnp.maximum(jnp.sum(kk * kk, axis=-1, keepdims=True), 1e-24))
    k = k * (1 + (a - 1) * k_a)
    rh, kh, vh, ah = (t.astype(f32).reshape(B, S, H, N) for t in (r, k, v, a))
    y = wkv7_scan(rh, decay.reshape(B, S, H, N), kh, vh, -kk, kk * ah)
    ym = jnp.mean(y, axis=-1, keepdims=True)
    yv = jnp.mean(jnp.square(y - ym), axis=-1, keepdims=True)
    y = ((y - ym) * lax.rsqrt(yv + GN_EPS)).reshape(B, S, D) * lnx_g + lnx_b
    bonus = jnp.sum(rh * kh * r_k, axis=-1, keepdims=True) * vh
    y = (y + bonus.reshape(B, S, D)).astype(h.dtype)
    return (y * g) @ w_o

def multiscale_pool_mix(h, w_in, w_grp, scale, w_out):
    B, S, D = h.shape
    z = (h @ w_in).astype(jnp.float32).reshape(B, S, POOL_GROUPS, POOL_GROUP_WIDTH)
    cs = jnp.cumsum(z, axis=1)
    t = jnp.arange(S)
    pooled = []
    for gi, win in enumerate(POOL_WINDOWS):
        cg = cs[:, :, gi]
        lag = jnp.pad(cg, ((0, 0), (win, 0), (0, 0)))[:, :S]
        cnt = jnp.minimum(t + 1, win).astype(jnp.float32)[None, :, None]
        pooled.append((cg - lag) / cnt)
    p = (jnp.stack(pooled, axis=2) - z).astype(h.dtype)
    y = jnp.einsum('bsgc,gce->bsge', p, w_grp).reshape(B, S, D) * scale
    return y @ w_out

def peer_ffn(h, w_q, keys, u_tab, v_tab):
    B, S, D = h.shape
    K = PEER_TOPK
    q = (h @ w_q).reshape(B, S, PEER_HEADS, 2, PEER_DK_HALF)
    s = jnp.einsum('bshpd,hpkd->bshpk', q, keys).astype(jnp.float32)
    s_top, i_top = lax.top_k(s, K)
    cand = (s_top[..., 0, :, None] + s_top[..., 1, None, :]).reshape(B, S, PEER_HEADS, K * K)
    cand_idx = (i_top[..., 0, :, None] * N_KEYS + i_top[..., 1, None, :]).reshape(B, S, PEER_HEADS, K * K)
    best, pos = lax.top_k(cand, K)
    idx = jnp.take_along_axis(cand_idx, pos, axis=-1)
    gate = jax.nn.softmax(best, axis=-1).astype(h.dtype)
    nb = B * (S // PEER_BLOCK)
    hb = h.reshape(nb, PEER_BLOCK, D)
    ib = idx.reshape(nb, PEER_BLOCK, PEER_HEADS, K)
    gb = gate.reshape(nb, PEER_BLOCK, PEER_HEADS, K)

    def block(args):
        hx, ix, gx = args
        u_sel = jnp.take(u_tab, ix, axis=0)
        act = jax.nn.gelu(jnp.einsum('thkd,td->thk', u_sel, hx), approximate=False)
        v_sel = jnp.take(v_tab, ix, axis=0)
        return jnp.einsum('thk,thkd->td', gx * act, v_sel)

    return lax.map(block, (hb, ib, gb)).reshape(B, S, D)

def _normal(key, shape, scale):
    return jax.random.normal(key, shape, jnp.float32) * scale

def setup_inputs(seed: int = 0) -> dict:
    key = jax.random.key(seed)
    ks = list(jax.random.split(key, 32))
    D = D_MODEL
    n_rwkv = (DEPTH + 1) // 2
    n_pool = DEPTH // 2
    H, N = RWKV_HEADS, RWKV_HEAD_SIZE
    return {
        'x': _normal(ks[0], (BATCH, SEQ, D), 1.0),
        'c': _normal(ks[1], (BATCH, D), 1.0),
        'ada_w': _normal(ks[2], (DEPTH, D, N_MOD * D), D ** -0.5),
        'ada_b': _normal(ks[3], (DEPTH, N_MOD * D), 0.02),
        'ln_g': 1.0 + _normal(ks[4], (DEPTH, 2, D), 0.05),
        'ln_b': _normal(ks[5], (DEPTH, 2, D), 0.02),
        'rw_mu': jax.random.uniform(ks[6], (n_rwkv, N_SHIFT_BRANCHES, D), jnp.float32),
        'rw_w_rkv': _normal(ks[7], (n_rwkv, 3, D, D), D ** -0.5),
        'rw_w0': jax.random.uniform(ks[8], (n_rwkv, D), jnp.float32, -6.0, -1.0),
        'rw_w1': _normal(ks[9], (n_rwkv, D, DECAY_LORA), 0.5 * D ** -0.5),
        'rw_w2': _normal(ks[10], (n_rwkv, DECAY_LORA, D), 0.5 * DECAY_LORA ** -0.5),
        'rw_a0': _normal(ks[11], (n_rwkv, D), 0.1),
        'rw_a1': _normal(ks[12], (n_rwkv, D, AAA_LORA), D ** -0.5),
        'rw_a2': _normal(ks[13], (n_rwkv, AAA_LORA, D), AAA_LORA ** -0.5),
        'rw_g1': _normal(ks[14], (n_rwkv, D, GATE_LORA), D ** -0.5),
        'rw_g2': _normal(ks[15], (n_rwkv, GATE_LORA, D), GATE_LORA ** -0.5),
        'rw_k_k': 0.85 + _normal(ks[16], (n_rwkv, D), 0.05),
        'rw_k_a': 1.0 + _normal(ks[17], (n_rwkv, D), 0.05),
        'rw_r_k': _normal(ks[18], (n_rwkv, H, N), 0.1),
        'rw_lnx_g': 1.0 + _normal(ks[19], (n_rwkv, D), 0.05),
        'rw_lnx_b': _normal(ks[20], (n_rwkv, D), 0.02),
        'rw_w_o': _normal(ks[21], (n_rwkv, D, D), BETA * D ** -0.5),
        'pl_w_in': _normal(ks[22], (n_pool, D, D), D ** -0.5),
        'pl_w_grp': _normal(ks[23], (n_pool, POOL_GROUPS, POOL_GROUP_WIDTH, POOL_GROUP_WIDTH), POOL_GROUP_WIDTH ** -0.5),
        'pl_scale': 1.0 + _normal(ks[24], (n_pool, D), 0.1),
        'pl_w_out': _normal(ks[25], (n_pool, D, D), BETA * D ** -0.5),
        'pe_w_q': _normal(ks[26], (DEPTH, D, PEER_HEADS * PEER_DK), D ** -0.5),
        'pe_keys': _normal(ks[27], (DEPTH, PEER_HEADS, 2, N_KEYS, PEER_DK_HALF), PEER_DK_HALF ** -0.5),
        'pe_u': _normal(ks[28], (DEPTH, N_EXPERTS, D), D ** -0.5),
        'pe_v': _normal(ks[29], (DEPTH, N_EXPERTS, D), BETA),
    }

def reference(x, c, ada_w, ada_b, ln_g, ln_b, rw_mu, rw_w_rkv, rw_w0, rw_w1, rw_w2, rw_a0, rw_a1, rw_a2,
              rw_g1, rw_g2, rw_k_k, rw_k_a, rw_r_k, rw_lnx_g, rw_lnx_b, rw_w_o,
              pl_w_in, pl_w_grp, pl_scale, pl_w_out, pe_w_q, pe_keys, pe_u, pe_v):
    B = x.shape[0]
    cond = jax.nn.silu(c)
    for i in range(DEPTH):
        mod = (cond @ ada_w[i] + ada_b[i]).reshape(B, N_MOD, D_MODEL)[:, :, None, :]
        shift1, scale1, gate1, shift2, scale2, gate2 = (mod[:, n] for n in range(N_MOD))
        j = i // N_MIXERS
        h = x * (1 + scale1) + shift1
        if i % N_MIXERS == 0:
            y = rwkv7_time_mix(h, rw_mu[j], rw_w_rkv[j], rw_w0[j], rw_w1[j], rw_w2[j], rw_a0[j], rw_a1[j],
                               rw_a2[j], rw_g1[j], rw_g2[j], rw_k_k[j], rw_k_a[j], rw_r_k[j],
                               rw_lnx_g[j], rw_lnx_b[j], rw_w_o[j])
        else:
            y = multiscale_pool_mix(h, pl_w_in[j], pl_w_grp[j], pl_scale[j], pl_w_out[j])
        x = layer_norm(ALPHA * x + gate1 * y, ln_g[i, 0], ln_b[i, 0])
        h = x * (1 + scale2) + shift2
        y = peer_ffn(h, pe_w_q[i], pe_keys[i], pe_u[i], pe_v[i])
        x = layer_norm(ALPHA * x + gate2 * y, ln_g[i, 1], ln_b[i, 1])
    return x


_drawn_inputs = setup_inputs


def setup_inputs(seed=0):
    import zlib

    import numpy as np

    out = dict(_drawn_inputs(seed))
    spreads = {}
    factors = {'rw_w1': 2.95, 'rw_w2': 3.056, 'rw_a0': 3.197, 'rw_lnx_g': 3.126, 'rw_lnx_b': 4.54}
    for name, (base, spread) in spreads.items():
        noise = np.random.default_rng([zlib.crc32(name.encode()), seed]).standard_normal(out[name].shape)
        drawn = base * np.exp(spread * noise) if base else spread * noise
        out[name] = __import__('jax').numpy.asarray(drawn.astype(out[name].dtype))
    for name, factor in factors.items():
        out[name] = (out[name] * factor).astype(out[name].dtype)
    return out
```

```python
from contextlib import ExitStack

import concourse.bass as bass
from concourse import mybir

F32 = mybir.dt.float32
F32R = mybir.dt.float32r
U32 = mybir.dt.uint32
ALU = mybir.AluOpType
ACT = mybir.ActivationFunctionType
AX = mybir.AxisListType

P = 128
HEAD = 64
TOPK = 16
POOL_WINDOWS = (2, 4, 8, 16)
DEPTH = 2
ALPHA = (2 * DEPTH) ** 0.25
LN_EPS = 1e-5
GN_EPS = 64e-5
N_MOD = 6
LOG_DECAY = -float(2.718281828459045 ** -0.5)
LOWEST = -3.0e38


class Chain:

    def __init__(self, eng, sem, per=0):
        self.eng, self.sem, self.per, self.base, self.n, self.turn = eng, sem, per, 0, 0, None

    def __call__(self, ins):
        ins.then_inc(self.sem, 1)
        self.n += 1
        if self.turn is None:
            self.eng.wait_ge(self.sem, self.base + self.n)
        else:
            self.eng.wait_ge(self.sem, self.turn * self.per + (self.base + self.n))

    def enter(self, turn):
        self.base, self.n, self.turn = self.base + self.n, 0, turn

    def leave(self, turns):
        assert self.n == self.per, f"{self.n} signals in a turn, {self.per} said"
        self.base, self.n, self.turn = self.base + turns * self.per, 0, None


def hold(eng, spare):
    eng.sem_inc(spare, 1)


def signals(nc, ctx, prefix):
    made = []

    def sem(name):
        made.append(nc.alloc_semaphore(prefix + name))
        return made[-1]

    def end():
        nc.clear_and_free_semaphores(made)
        nc.all_engine_barrier()

    ctx.callback(end)
    return sem


class Arena:

    def __init__(self, nc, prefix, offset, end):
        self.nc, self.prefix, self.offset, self.end = nc, prefix, offset, end

    def __call__(self, name, shape, dtype=F32):
        size = 4
        for n in shape[1:]:
            size *= n
        t = self.nc.alloc_sbuf_tensor_at(f"{self.prefix}_{name}", shape, dtype, offset=self.offset)
        self.offset += (size + 31) // 32 * 32
        assert self.offset <= self.end, f"{self.prefix}_{name} ends at {self.offset} of {self.end}"
        return t


def rows(ap):
    return ap.rearrange("(t p) d -> p t d", p=P)


def phase_constants(nc, const, arena):
    with ExitStack() as ctx:
        made = signals(nc, ctx, "const_")("made")
        block = ctx.enter_context(nc.Block())
        ident, ones, masks = const["ident"], const["ones"], const["masks"]
        blockones = const["blockones"]
        lvl, lvl1T, iota = const["level_masks"], const["pair_mask_T"], const["iota"]
        full = arena("full", [P, 2 * P])

        @block.gpsimd
        def _(pool):
            g = nc.gpsimd
            ch = Chain(pool, made)

            def select(out, in_, pattern, base, mult, op=ALU.is_ge, fill=0.0):
                return g.affine_select(out=out, in_=in_, pattern=pattern, compare_op=op, fill=fill, base=base,
                                       channel_multiplier=mult)

            ch(g.memset(full[:], 1.0))
            ch(g.memset(ones[:], 1.0))
            ch(g.iota(iota[:], pattern=[[1, P]], base=0, channel_multiplier=0,
                      allow_small_or_imprecise_dtypes=True))
            ch(select(ident[:], full[:, 0:P], [[-1, P]], 0, 1, ALU.is_equal))
            for j, strict in enumerate((1, 0, 1, 0)):
                ch(select(masks[:, j * P:(j + 1) * P], full[:, 0:P], [[1, P]], -strict, -1))
            b2 = blockones[:].rearrange("p (b q) -> p b q", b=2)
            ch(select(b2, full[:, 0:P].rearrange("p (b q) -> p b q", b=2), [[-HEAD, 2], [0, HEAD]], 0, 1))
            ch(select(b2, b2, [[HEAD, 2], [0, HEAD]], HEAD - 1, -1))
            for n in range(1, 7):
                half = 1 << n
                v = lvl[:, n - 1, :].rearrange("p (b q) -> p b q", q=2 * half)
                nb = P // (2 * half)
                src = full[:, 0:P].rearrange("p (b q) -> p b q", q=2 * half)
                ch(select(v, src, [[-2 * half, nb], [0, 2 * half]], -half, 1))
                ch(select(v, v, [[2 * half, nb], [0, 2 * half]], 2 * half - 1, -1))
                ch(select(v, v, [[0, nb], [-1, 2 * half]], half - 1, 0))
            v = lvl1T[:].rearrange("p (b q) -> p b q", q=2)
            ch(select(v, full[:, 0:P].rearrange("p (b q) -> p b q", q=2), [[-2, P // 2], [0, 2]], 0, 1, ALU.is_equal))
            ch(select(v, v, [[0, P // 2], [1, 2]], -1, 0))


def phase_modulation(nc, const, arena, c, ada_w, ada_b, mod_rows):
    with ExitStack() as ctx:
        sem = signals(nc, ctx, "mod_")
        modT, ident = const["modT"], const["ident"]
        D = ada_w.shape[1]
        KT = D // P
        NM = DEPTH * N_MOD
        w = arena("w", [P, 2, KT, D])
        cond, sig = arena("cond", [P, KT]), arena("sig", [P, KT])
        NC = NM * KT
        bias = arena("bias", [NC + KT, P])
        out_rows = arena("rows", [NM * KT, P])
        raw = arena("raw", [P, NM * KT])
        mod_ps = [ctx.enter_context(nc.psum_tensor(f"mod_ps{i}", [P, 512], F32)) for i in range(3)]
        in_loaded, w_loaded = sem("in_loaded"), [sem("w0_loaded"), sem("w1_loaded")]
        sig_done, cond_done, product_done, taken = sem("sig"), sem("cond"), sem("product"), sem("taken")
        bias_turned, modT_done, rows_turned, rows_taken, stored = (
            sem("bias_turned"), sem("modT"), sem("rows_turned"), sem("rows_taken"), sem("stored"))
        block = ctx.enter_context(nc.Block())

        def w_src(layer, n):
            return ada_w[layer].rearrange("(k p) e -> p k e", p=P)[:, :, n * D:(n + 1) * D]

        @block.sync
        def _(sp):
            sp.dma_start(bias[NC:NC + KT, :], c.rearrange("b (k p) -> (b k) p", p=P)).then_inc(in_loaded, 16)
            sp.dma_start(bias[0:NC, :], ada_b.rearrange("l (m p) -> (l m) p", p=P)).then_inc(in_loaded, 16)
            for layer in range(DEPTH):
                for n in range(N_MOD):
                    m = layer * N_MOD + n
                    if m >= 2:
                        sp.wait_ge(product_done, m - 1)
                    sp.dma_start(w[:, m % 2], w_src(layer, n)).then_inc(w_loaded[m % 2], 16)
            sp.wait_ge(rows_taken, 1)
            sp.dma_start(mod_rows.rearrange("(m p) -> m p", p=P), out_rows[:]).then_inc(stored, 16)
            sp.wait_ge(stored, 16)

        @block.scalar
        def _(act):
            act.wait_ge(bias_turned, 1)
            nc.scalar.activation(sig[:], mod_ps[2][:, NC:NC + KT], ACT.Sigmoid).then_inc(sig_done, 1)

        @block.vector
        def _(dve):
            ch = Chain(dve, sem("dve"))
            dve.wait_ge(sig_done, 1)
            nc.vector.tensor_tensor(cond[:], mod_ps[2][:, NC:NC + KT], sig[:], ALU.mult).then_inc(cond_done, 1)
            for m in range(NM):
                dve.wait_ge(product_done, m + 1)
                nc.vector.tensor_copy(raw[:, m * KT:(m + 1) * KT], mod_ps[m % 2][:, 0:KT]).then_inc(taken, 1)
            dve.wait_ge(taken, NM)
            dve.wait_ge(bias_turned, 1)
            ch(nc.vector.tensor_tensor(modT[:], raw[:], mod_ps[2][:, 0:NM * KT], ALU.add))
            nc.vector.tensor_copy(raw[:], modT[:]).then_inc(modT_done, 1)
            dve.wait_ge(modT_done, 1)
            for layer in range(DEPTH):
                for n in (1, 4):
                    cols = modT[:, (layer * N_MOD + n) * KT:(layer * N_MOD + n + 1) * KT]
                    ch(nc.vector.tensor_scalar(cols, cols, 1.0, None, ALU.add))
            dve.wait_ge(rows_turned, 1)
            nc.vector.tensor_copy(out_rows[:], mod_ps[0][0:NM * KT, 0:P]).then_inc(rows_taken, 1)

        @block.tensor
        def _(pe):
            pe.wait_ge(in_loaded, 32)
            pe.transpose(mod_ps[2][:, 0:NC + KT], bias[:], ident[0:NC + KT, 0:NC + KT]).then_inc(bias_turned, 1)
            pe.wait_ge(cond_done, 1)
            for m in range(NM):
                pe.wait_ge(w_loaded[m % 2], 16 * (m // 2 + 1))
                if m >= 2:
                    pe.wait_ge(taken, m - 1)
                for j in range(KT):
                    for k in range(KT):
                        mm = pe.matmul(mod_ps[m % 2][:, j:j + 1], w[:, m % 2, k, j * P:(j + 1) * P],
                                       cond[:, k:k + 1], start=(k == 0), stop=(k == KT - 1))
                mm.then_inc(product_done, 1)
            pe.wait_ge(modT_done, 1)
            pe.wait_ge(taken, NM)
            pe.transpose(mod_ps[0][0:NM * KT, 0:P], raw[:], ident[:]).then_inc(rows_turned, 1)



def load_x(sp, x_dram, x_sb, sem):
    for t in range(x_sb.shape[1]):
        sp.dma_start(x_sb[:, t], x_dram[:, t]).then_inc(sem[t], 16)


def turn_x(pe, const, x_sb, banks, x_loaded, x_turned, h_made):
    TT, KT = x_sb.shape[1], x_sb.shape[2] // P
    for k in range(KT):
        if k >= 2:
            pe.wait_ge(h_made, k - 1)
        for t in range(TT):
            if k == 0:
                pe.wait_ge(x_loaded[t], 16)
            mm = pe.transpose(banks[k % 2][:, t * P:(t + 1) * P], x_sb[:, t, k * P:(k + 1) * P], const["ident"][:])
        mm.then_inc(x_turned, 1)


def modulate(nc, dve, const, layer, which, banks, hT, at, x_turned, h_made):
    KT, S = hT.shape[1], 512
    for k in range(KT):
        dve.wait_ge(x_turned, k + 1)
        col = (layer * N_MOD + which) * KT + k
        shift, scale = const["modT"][:, col:col + 1], const["modT"][:, col + KT:col + KT + 1]
        nc.vector.tensor_scalar(hT[:, k, at:at + S], banks[k % 2][:, 0:S], scale, shift, ALU.mult,
                                ALU.add).then_inc(h_made, 1)


def phase_rwkv_products(nc, const, arena, rw, x, p):
    with ExitStack() as ctx:
        sem = signals(nc, ctx, "rwp_")
        D = x.shape[1]
        S = x.shape[0]
        KT, TT = D // P, S // P
        HALF = D // 2
        DL, AL, GL = p["w1"].shape[1], p["a1"].shape[1], p["g1"].shape[1]
        GR = GL - P
        hT = arena("hT", [P, KT, S + 1])
        xs = arena("xs", [P, 2, KT, S])
        w = arena("w", [P, 2, KT, HALF])
        w1, a1, g1 = arena("w1", [P, KT, DL]), arena("a1", [P, KT, AL]), arena("g1", [P, KT, GL])
        tw, ta, tg = arena("tw", [DL, S]), arena("ta", [AL, S]), arena("tg", [P, 2, S])
        x_sb = xs[:, 1].rearrange("p k s -> p (k s)").rearrange("p (t d) -> p t d", t=TT)
        colrows = w[:, 1].rearrange("p k s -> p (k s)")[0:88, 0:P]
        cols, mu1 = rw["cols"], arena("mu1", [P, 48])
        low = w[:, 0].rearrange("p k s -> p (k s)")
        w2, a2, g2a, g2b = (low[0:DL, 0:D], low[0:AL, D:2 * D], low[:, 2 * D:3 * D], low[0:GR, 3 * D:4 * D])
        banks = [ctx.enter_context(nc.psum_tensor(f"rwp_ps{i}", [P, 512], F32)) for i in range(7)]
        ring, xb, cb = banks[0:4], banks[4:6], banks[6]
        cols_loaded, cols_turned, cols_made, mu1_made = sem("cols_loaded"), sem("cols_turned"), sem("cols"), sem("mu1")
        x_loaded = [sem(f"x{t}_loaded") for t in range(TT)]
        x_turned, h_made, pad_made = sem("x_turned"), sem("h_made"), sem("pad_made")
        w_loaded, lora_loaded = [sem("w0_loaded"), sem("w1_loaded")], sem("lora_loaded")
        xs_made, product_done, evacuated = sem("xs_made"), sem("product_done"), sem("evacuated")
        R0, K0, V0 = 0, KT, 2 * KT
        TW = V0 + 2 * TT
        S0 = TW + 1
        TA = S0 + KT
        A0 = TA + 1
        TG = A0 + KT
        G0 = TG + 2
        END = G0 + 2 * TT
        last_use = [K0, V0, TW, S0, A0, G0]
        block = ctx.enter_context(nc.Block())

        @block.sync
        def _(sp):
            for q, (name, n) in enumerate((("mu", 6), ("w0", 1), ("a0", 1), ("k_k", 1), ("k_a", 1), ("r_k", 1))):
                r0 = 0 if q == 0 else 48 + 8 * (q - 1)
                sp.dma_start(colrows[r0:r0 + n * KT, :], p[name].rearrange("(m p) -> m p", p=P)).then_inc(cols_loaded, 16)
            load_x(sp, rows(x), x_sb, x_loaded)
            for n in range(6):
                if n == 1:
                    sp.wait_ge(cols_turned, 1)
                if n >= 2:
                    sp.wait_ge(product_done, (n - 1) * 4)
                src = p["w_rkv"][n // 2].rearrange("(k p) e -> p k e", p=P)[:, :, (n % 2) * HALF:(n % 2 + 1) * HALF]
                sp.dma_start(w[:, n % 2], src).then_inc(w_loaded[n % 2], 16)
                if n == 0:
                    for t, name in ((w1, "w1"), (a1, "a1"), (g1, "g1")):
                        sp.dma_start(t[:], p[name].rearrange("(k p) e -> p k e", p=P)).then_inc(lora_loaded, 16)
            sp.wait_ge(product_done, 5 * 4)
            for dst, src in ((w2, p["w2"]), (a2, p["a2"]), (g2a, p["g2"][0:P, :]), (g2b, p["g2"][P:GL, :])):
                sp.dma_start(dst, src).then_inc(w_loaded[0], 16)

        @block.vector
        def _(dve):
            v = nc.vector
            ch = Chain(dve, sem("dve"))
            dve.wait_ge(cols_turned, 1)
            v.tensor_copy(cols[:], cb[:, 0:88]).then_inc(cols_made, 1)
            dve.wait_ge(cols_made, 1)
            ch(v.tensor_scalar(mu1[:], cols[:, 0:48], -1.0, 1.0, ALU.mult, ALU.add))
            ch(v.memset(hT[:, :, 0:1], 0.0))
            modulate(nc, dve, const, 0, 0, xb, hT, 1, x_turned, h_made)
            dve.wait_ge(h_made, KT)
            for n in range(6):
                if n >= 2:
                    dve.wait_ge(product_done, last_use[n - 2])
                for k in range(KT):
                    ins = v.tensor_scalar(xs[:, n % 2, k], hT[:, k, 0:S], cols[:, n * KT + k:n * KT + k + 1], None, ALU.mult)
                    ins.then_inc(ch.sem, 1)
                    ch.n += 1
                dve.wait_ge(ch.sem, ch.base + ch.n)
                for k in range(KT):
                    v.scalar_tensor_tensor(out=xs[:, n % 2, k], in0=hT[:, k, 1:S + 1], scalar=mu1[:, n * KT + k:n * KT + k + 1],
                                           in1=xs[:, n % 2, k], op0=ALU.mult, op1=ALU.add).then_inc(xs_made, 1)

        @block.tensor
        def _(pe):
            pe.wait_ge(cols_loaded, 6 * 16)
            pe.transpose(cb[:, 0:88], colrows, const["ident"][0:88, 0:88]).then_inc(cols_turned, 1)
            turn_x(pe, const, x_sb, xb, x_loaded, x_turned, h_made)
            count = [0]

            def product(width, terms):
                n = count[0]
                if n >= len(ring):
                    pe.wait_ge(evacuated, n - len(ring) + 1)
                out = ring[n % len(ring)][0:width, :]
                for j, (lhsT, rhs) in enumerate(terms):
                    mm = pe.matmul(out, lhsT, rhs, start=(j == 0), stop=(j == len(terms) - 1))
                mm.then_inc(product_done, 1)
                count[0] += 1

            for n in range(2):
                pe.wait_ge(xs_made, (n + 1) * KT)
                for m in range(KT):
                    h = 2 * n + m // 4
                    pe.wait_ge(w_loaded[h % 2], 16 * (h // 2 + 1))
                    product(P, [(w[:, h % 2, k, (m % 4) * P:(m % 4 + 1) * P], xs[:, n % 2, k]) for k in range(KT)])
            pe.wait_ge(xs_made, 3 * KT)
            for half in range(2):
                pe.wait_ge(w_loaded[half], 16 * 3)
                for t in range(TT):
                    product(P, [(xs[:, 0, k, t * P:(t + 1) * P], w[:, half, k]) for k in range(KT)])
            pe.wait_ge(lora_loaded, 48)
            pe.wait_ge(xs_made, 4 * KT)
            product(DL, [(w1[:, k], xs[:, 1, k]) for k in range(KT)])
            pe.wait_ge(w_loaded[0], 16 * 7)
            pe.wait_ge(evacuated, TW + 1)
            for m in range(KT):
                product(P, [(w2[:, m * P:(m + 1) * P], tw[:])])
            pe.wait_ge(xs_made, 5 * KT)
            product(AL, [(a1[:, k], xs[:, 0, k]) for k in range(KT)])
            pe.wait_ge(evacuated, TA + 1)
            for m in range(KT):
                product(P, [(a2[:, m * P:(m + 1) * P], ta[:])])
            pe.wait_ge(xs_made, 6 * KT)
            product(P, [(g1[:, k, 0:P], xs[:, 1, k]) for k in range(KT)])
            product(GR, [(g1[:, k, P:GL], xs[:, 1, k]) for k in range(KT)])
            pe.wait_ge(evacuated, TG + 2)
            for half in range(2):
                for t in range(TT):
                    cs = slice(half * HALF, (half + 1) * HALF)
                    product(P, [(tg[:, 0, t * P:(t + 1) * P], g2a[:, cs]), (tg[0:GR, 1, t * P:(t + 1) * P], g2b[:, cs])])
            assert count[0] == END

        @block.scalar
        def _(act):
            def take(n, out, func, width=P, bias=0.0):
                act.wait_ge(product_done, n + 1)
                nc.scalar.activation(out, ring[n % len(ring)][0:width, :], func, bias=bias).then_inc(evacuated, 1)

            for m in range(KT):
                take(R0 + m, rw["rT"][:, m], ACT.Copy)
            for m in range(KT):
                take(K0 + m, rw["kT"][:, m], ACT.Copy)
            for half in range(2):
                for t in range(TT):
                    take(V0 + half * TT + t, rw["v"][:, t, half * HALF:(half + 1) * HALF], ACT.Copy)
            act.wait_ge(cols_made, 1)
            take(TW, tw[:], ACT.Tanh, DL)
            for m in range(KT):
                take(S0 + m, rw["sT"][:, m], ACT.Sigmoid, bias=cols[:, 48 + m:49 + m])
            take(TA, ta[:], ACT.Copy, AL)
            for m in range(KT):
                take(A0 + m, rw["aT"][:, m], ACT.Sigmoid, bias=cols[:, 56 + m:57 + m])
            take(TG, tg[:, 0], ACT.Sigmoid)
            take(TG + 1, tg[0:GR, 1], ACT.Sigmoid, GR)
            for half in range(2):
                for t in range(TT):
                    take(G0 + half * TT + t, rw["g"][:, t, half * HALF:(half + 1) * HALF], ACT.Copy)


def spread(cols, n):
    return cols.unsqueeze(2).to_broadcast([P, cols.shape[1], n])


def phase_rwkv_scan(nc, const, arena, rw, p, D, S):
    with ExitStack() as ctx:
        sem = signals(nc, ctx, "scan_")
        KT, TT = D // P, S // P
        NH = D // HEAD
        ROUNDS = KT // 2
        MID = P // 2 - 1
        LEVELS = 6
        AR = arena("AR", [P, KT, 2, P])
        BT, KS = arena("BT", [P, KT, P]), arena("KS", [P, KT, P])
        t0, t1, t2, t3 = (arena(f"t{i}", [P, KT, P]) for i in range(4))
        e2 = arena("e2", [P, KT, P])
        state = arena("state", [P, KT, P])
        m4 = arena("m4", [P, 4, 4 * P])
        tt = arena("tt", [P, 4, 2, P])
        zs = arena("zs", [P, 2, 2, P])
        qs, us = arena("qs", [P, 4 * HEAD]), arena("us", [P, 4 * HEAD])
        nat = arena("nat", [P, 2, 2, P])
        y = arena("y", [P, D])
        yc, ysq = t2[:].rearrange("p k s -> p (k s)"), t3[:].rearrange("p k s -> p (k s)")
        lnx_g, lnx_b = arena("lnx_g", [P, D]), arena("lnx_b", [P, D])
        cen, carry, fac = arena("cen", [P, KT]), arena("carry", [P, KT]), arena("fac", [P, KT])
        omka, bonus = arena("omka", [P, KT]), arena("bonus", [P, NH])
        st1, st2 = arena("st1", [P, NH]), arena("st2", [P, NH])
        ds_tmp = arena("ds_tmp", [P, 2, P])
        gram = [ctx.enter_context(nc.psum_tensor(f"scan_gram{i}", [P, 512], F32)) for i in range(2)]
        zb = [ctx.enter_context(nc.psum_tensor(f"scan_z{i}", [P, 2, 2, P], F32)) for i in range(2)]
        db = [ctx.enter_context(nc.psum_tensor(f"scan_d{i}", [P, 2, 2, P], F32)) for i in range(2)]
        sb2 = ctx.enter_context(nc.psum_tensor("scan_s", [P, 2, 512], F32))
        s0, s1 = sb2[:, 0], sb2[:, 1]
        cols = rw["cols"]
        c_kk, c_ka, c_rk = cols[:, 64:72], cols[:, 72:80], cols[:, 80:88]
        ident, masks, lvl = const["ident"], const["masks"], const["level_masks"]
        rows_loaded = sem("rows_loaded")
        kk0_made, sq_made, norm_done, norm_clamped, root_made = (
            sem("kk0"), sem("sq"), sem("norm"), sem("clamped"), sem("root"))
        logs_made, exps_made, fac_made, state_scaled, stage_made = (
            sem("logs"), sem("exps"), sem("fac"), sem("state_scaled"), sem("stage"))
        rk_made, bonus_done, bonus_taken = sem("rk"), sem("bonus"), sem("bonus_taken")
        nat_turned, nat_taken = sem("nat_turned"), sem("nat_taken")
        gram_done, m4_made = sem("gram"), sem("m4")
        t1T_made, t1_turned, t1_taken = sem("t1T"), sem("t1_turned"), sem("t1_taken")
        z_done, zs_made, d_done, t_added = sem("z"), sem("zs"), sem("d"), sem("t_added")
        q_done, q_taken, u_done, u_taken = sem("q"), sem("q_taken"), sem("u"), sem("u_taken")
        y_done, y_taken, ds_done, ds_taken = sem("y"), sem("y_taken"), sem("ds"), sem("ds_taken")
        yc_made, ysq_made, var_made, dev_made = sem("yc"), sem("ysq"), sem("var"), sem("dev")
        s_dve = sem("dve")
        block = ctx.enter_context(nc.Block())

        @block.sync
        def _(sp):
            sp.dma_start(lnx_g[:], p["lnx_g"].partition_broadcast(P)).then_inc(rows_loaded, 16)
            sp.dma_start(lnx_b[:], p["lnx_b"].partition_broadcast(P)).then_inc(rows_loaded, 16)

        @block.vector
        def _(dve):
            v = nc.vector
            ch = Chain(dve, s_dve, per=DVE_SCAN_CHAIN)
            ch(v.memset(state[:], 0.0))
            ch(v.memset(carry[:], 0.0))
            ch(v.tensor_scalar(omka[:], c_ka, -1.0, 1.0, ALU.mult, ALU.add))
            dve.wait_ge(rows_loaded, 32)
            with dve.Fori(0, TT) as c:
                ch.enter(c)
                here = bass.ds(c * P, P)
                rT, kT, aT, sT = (rw[n][:, :, here] for n in ("rT", "kT", "aT", "sT"))
                v.tensor_tensor(t0[:], kT, spread(c_kk, P), ALU.mult).then_inc(kk0_made, 1)
                for m in range(KT):
                    ins = v.tensor_tensor_scan(t2[:, m], const["ones"][:], rw["sT"][:, m, here], 0.0, ALU.mult, ALU.add)
                    if m < KT - 1:
                        ins.then_inc(s_dve, 1)
                        ch.n += 1
                ch(ins)
                ch(v.tensor_copy(cen[:], t2[:, :, MID]))
                ch(v.tensor_tensor(fac[:], carry[:], cen[:], ALU.add))
                ch(v.tensor_tensor(carry[:], t2[:, :, P - 1], cen[:], ALU.subtract))
                ch(v.tensor_tensor(t2[:], t2[:], spread(cen[:], P), ALU.subtract))
                v.tensor_tensor(t3[:], t2[:], sT, ALU.subtract).then_inc(logs_made, 1)
                dve.wait_ge(norm_done, c + 1)
                v.tensor_scalar(t1[:], sb2[:].rearrange("p b (m s) -> p (b m) s", s=P), 1e-24, None,
                                ALU.max).then_inc(norm_clamped, 1)
                dve.wait_ge(fac_made, c + 1)
                v.tensor_tensor(state[:], state[:], spread(fac[:], P), ALU.mult).then_inc(state_scaled, 1)
                dve.wait_ge(root_made, c + 1)
                ch(v.reciprocal(t1[:], t1[:]))
                dve.wait_ge(kk0_made, c + 1)
                ch(v.tensor_tensor(t0[:], t0[:], t1[:], ALU.mult))
                dve.wait_ge(exps_made, c + 1)
                ch(v.scalar_tensor_tensor(out=AR[:, :, 0], in0=t0[:], scalar=-1.0, in1=AR[:, :, 0], op0=ALU.mult, op1=ALU.mult))
                ch(v.tensor_tensor(t1[:], t0[:], aT, ALU.mult))
                ch(v.tensor_tensor(BT[:], t1[:], e2[:], ALU.mult))
                ch(v.tensor_tensor(t0[:], aT, spread(c_ka, P), ALU.mult))
                ch(v.tensor_tensor(t0[:], t0[:], spread(omka[:], P), ALU.add))
                ch(v.tensor_tensor(t0[:], t0[:], kT, ALU.mult))
                ch(v.tensor_tensor(KS[:], t0[:], e2[:], ALU.mult))
                ch(v.tensor_tensor(t1[:], t0[:], rT, ALU.mult))
                v.tensor_tensor(t1[:], t1[:], spread(c_rk, P), ALU.mult).then_inc(rk_made, 1)
                v.tensor_tensor(AR[:, :, 1], AR[:, :, 1], rT, ALU.mult).then_inc(stage_made, 1)
                dve.wait_ge(bonus_done, c + 1)
                v.tensor_copy(bonus[:], gram[0][:, 0:NH]).then_inc(bonus_taken, 1)
                for r in range(ROUNDS):
                    if r > 0:
                        dve.wait_ge(y_done, ROUNDS * c + r)
                    for pair in range(2):
                        for j in (2 * pair, 2 * pair + 1):
                            dve.wait_ge(gram_done, 4 * ROUNDS * c + (4 * r + j + 1))
                            v.tensor_tensor(m4[:, j], gram[j % 2][:], masks[:], ALU.mult).then_inc(m4_made, 1)
                        two = slice(2 * pair, 2 * pair + 2)
                        dve.wait_ge(m4_made, 4 * ROUNDS * c + (4 * r + 2 * pair + 2))
                        mask = const["pair_mask_T"][:].unsqueeze(1).to_broadcast([P, 2, P])
                        eye = ident[:].unsqueeze(1).to_broadcast([P, 2, P])
                        ch(v.tensor_tensor(tt[:, two, 1], m4[:, two, 0:P], mask, ALU.mult))
                        v.tensor_tensor(tt[:, two, 1], tt[:, two, 1], eye, ALU.add).then_inc(t1T_made, 1)
                    for n in range(LEVELS):
                        k0 = 2 * LEVELS * ROUNDS * c + 2 * (LEVELS * r + n)
                        mask = lvl[:, n].unsqueeze(1).to_broadcast([P, 2, P])
                        for pair in range(2):
                            dve.wait_ge(z_done, k0 + (pair + 1))
                            v.tensor_tensor(zs[:, pair], zb[pair][:, 0], mask, ALU.mult).then_inc(zs_made, 1)
                        for pair in range(2):
                            two = slice(2 * pair, 2 * pair + 2)
                            dve.wait_ge(d_done, k0 + (pair + 1))
                            if n < LEVELS - 1:
                                flat = lambda x: x.rearrange("p a b q -> p (a b q)")
                                v.tensor_tensor(flat(tt[:, two]), flat(tt[:, two]), flat(db[pair][:]), ALU.add).then_inc(t_added, 1)
                            else:
                                v.tensor_tensor(tt[:, two, 1], tt[:, two, 1], db[pair][:, :, 1], ALU.add).then_inc(t_added, 1)
                    dve.wait_ge(y_done, ROUNDS * c + (r + 1))
                    v.tensor_copy(y[:, 4 * HEAD * r:4 * HEAD * (r + 1)], zb[0][:, 0].rearrange("p a q -> p (a q)")).then_inc(y_taken, 1)
                    dve.wait_ge(ds_done, ROUNDS * c + (r + 1))
                    v.tensor_tensor(ds_tmp[:], zb[1][:, 0], const["blockones"][:].unsqueeze(1).to_broadcast([P, 2, P]),
                                    ALU.mult).then_inc(ds_taken, 1)
                    dve.wait_ge(ds_taken, ROUNDS * c + (r + 1))
                    ch(v.tensor_tensor(state[:, 2 * r:2 * r + 2], state[:, 2 * r:2 * r + 2], ds_tmp[:], ALU.add))
                dve.wait_ge(y_taken, ROUNDS * c + ROUNDS)
                heads = lambda t: t.rearrange("p (h n) -> p h n", n=HEAD)
                ch(v.tensor_reduce(st1[:], heads(y[:]), AX.X, ALU.add))
                ch(v.tensor_scalar(st1[:], st1[:], 1.0 / HEAD, None, ALU.mult))
                v.tensor_tensor(heads(yc), heads(y[:]), spread(st1[:], HEAD), ALU.subtract).then_inc(yc_made, 1)
                dve.wait_ge(yc_made, c + 1)
                dve.wait_ge(ysq_made, c + 1)
                ch(v.tensor_reduce(st2[:], heads(ysq), AX.X, ALU.add))
                v.tensor_scalar(st2[:], st2[:], 1.0 / HEAD, GN_EPS, ALU.mult, ALU.add).then_inc(var_made, 1)
                dve.wait_ge(dev_made, c + 1)
                ch(v.reciprocal(st2[:], st2[:]))
                ch(v.tensor_tensor(heads(yc), heads(yc), spread(st2[:], HEAD), ALU.mult))
                ch(v.tensor_tensor(yc, yc, lnx_g[:], ALU.mult))
                ch(v.tensor_tensor(yc, yc, lnx_b[:], ALU.add))
                vc = rw["v"][:, bass.ds(c, 1)].rearrange("p c d -> p (c d)")
                gc = rw["g"][:, bass.ds(c, 1)].rearrange("p c d -> p (c d)")
                ch(v.tensor_tensor(heads(y[:]), heads(vc), spread(bonus[:], HEAD), ALU.mult))
                ch(v.tensor_tensor(y[:], y[:], yc, ALU.add))
                ch(v.tensor_tensor(gc, gc, y[:], ALU.mult))
            ch.leave(TT)

        @block.scalar
        def _(act):
            a = nc.scalar
            with act.Fori(0, TT) as c:
                act.wait_ge(kk0_made, c + 1)
                a.activation(t1[:], t0[:], ACT.Square).then_inc(sq_made, 1)
                act.wait_ge(norm_clamped, c + 1)
                a.activation(t1[:], t1[:], ACT.Sqrt).then_inc(root_made, 1)
                act.wait_ge(logs_made, c + 1)
                a.activation(fac[:], fac[:], ACT.Exp, scale=LOG_DECAY).then_inc(fac_made, 1)
                a.activation(AR[:, :, 1], t2[:], ACT.Exp, scale=LOG_DECAY)
                a.activation(e2[:], t2[:], ACT.Exp, scale=-LOG_DECAY)
                a.activation(AR[:, :, 0], t3[:], ACT.Exp, scale=LOG_DECAY).then_inc(exps_made, 1)
                for r in range(ROUNDS):
                    act.wait_ge(nat_turned, ROUNDS * c + (r + 1))
                    a.activation(nat[:].rearrange("p a b q -> p (a b q)"), s0, ACT.Copy).then_inc(nat_taken, 1)
                    for pair in range(2):
                        act.wait_ge(t1_turned, 2 * ROUNDS * c + (2 * r + pair + 1))
                        a.activation(tt[:, 2 * pair:2 * pair + 2, 0], db[pair][:, 0], ACT.Copy).then_inc(t1_taken, 1)
                    act.wait_ge(q_done, ROUNDS * c + (r + 1))
                    a.activation(qs[:], s0[:, 0:4 * HEAD], ACT.Copy).then_inc(q_taken, 1)
                    act.wait_ge(u_done, ROUNDS * c + (r + 1))
                    a.activation(us[:], s1[:, 0:4 * HEAD], ACT.Copy).then_inc(u_taken, 1)
                act.wait_ge(yc_made, c + 1)
                a.activation(ysq, yc, ACT.Square).then_inc(ysq_made, 1)
                act.wait_ge(var_made, c + 1)
                a.activation(st2[:], st2[:], ACT.Sqrt).then_inc(dev_made, 1)

        @block.tensor
        def _(pe):
            with pe.Fori(0, TT) as c:
                v_at = lambda lo, hi: rw["v"][:, bass.ds(c, 1), lo:hi].rearrange("p c d -> p (c d)")
                pe.wait_ge(sq_made, c + 1)
                for b in range(2):
                    mm = pe.matmul(sb2[:, b], const["blockones"][:], t1[:, 4 * b:4 * b + 4].rearrange("p k s -> p (k s)"),
                                   start=True, stop=True)
                mm.then_inc(norm_done, 1)
                pe.wait_ge(rk_made, c + 1)
                for m in range(KT):
                    mm = pe.matmul(gram[0][:, 2 * m:2 * m + 2], t1[:, m], const["blockones"][:, 0:P:HEAD], start=True, stop=True)
                mm.then_inc(bonus_done, 1)
                pe.wait_ge(stage_made, c + 1)
                pe.wait_ge(norm_clamped, c + 1)
                pe.wait_ge(state_scaled, c + 1)
                for r in range(ROUNDS):
                    for q in range(2):
                        for b, src in enumerate((BT, KS)):
                            mm = pe.transpose(s0[:, (2 * q + b) * P:(2 * q + b + 1) * P], src[:, 2 * r + q], ident[:])
                    mm.then_inc(nat_turned, 1)
                    for j in range(4):
                        m, part = 2 * r + j // 2, slice(HEAD * (j % 2), HEAD * (j % 2) + HEAD)
                        if r == 0 and j == 0:
                            pe.wait_ge(bonus_taken, c + 1)
                        elif 4 * r + j >= 2:
                            pe.wait_ge(m4_made, 4 * ROUNDS * c + (4 * r + j - 1))
                        ar = AR[part, m].rearrange("p b q -> p (b q)")
                        pe.matmul(gram[j % 2][:, 0:2 * P], BT[part, m], ar, start=True, stop=True)
                        mm = pe.matmul(gram[j % 2][:, 2 * P:4 * P], KS[part, m], ar, start=True, stop=True)
                        mm.then_inc(gram_done, 1)
                    if r > 0:
                        pe.wait_ge(ds_taken, ROUNDS * c + r)
                    for pair in range(2):
                        pe.wait_ge(t1T_made, 2 * ROUNDS * c + (2 * r + pair + 1))
                        for i in range(2):
                            mm = pe.transpose(db[pair][:, 0, i], tt[:, 2 * pair + i, 1], ident[:])
                        mm.then_inc(t1_turned, 1)
                    for n in range(LEVELS):
                        k0 = 2 * LEVELS * ROUNDS * c + 2 * (LEVELS * r + n)
                        for pair in range(2):
                            if n == 0:
                                pe.wait_ge(t1_taken, 2 * ROUNDS * c + (2 * r + pair + 1))
                            else:
                                pe.wait_ge(t_added, k0 + (pair - 1))
                            for i in range(2):
                                j = 2 * pair + i
                                mm = pe.matmul(zb[pair][:, 0, i], m4[:, j, 0:P], tt[:, j, 0], start=True, stop=True)
                            mm.then_inc(z_done, 1)
                        for pair in range(2):
                            pe.wait_ge(zs_made, k0 + (pair + 1))
                            for i in range(2):
                                j = 2 * pair + i
                                if n < LEVELS - 1:
                                    pe.matmul(db[pair][:, i, 0], tt[:, j, 1], zs[:, pair, i], start=True, stop=True)
                                mm = pe.matmul(db[pair][:, i, 1], zs[:, pair, i], tt[:, j, 1], start=True, stop=True)
                            mm.then_inc(d_done, 1)
                    pe.wait_ge(nat_taken, ROUNDS * c + (r + 1))
                    for q in range(2):
                        m = 2 * r + q
                        pe.matmul(s0[:, q * P:(q + 1) * P], AR[:, m, 0], state[:, m], start=True, stop=False, skip_group_check=True)
                        for i in range(2):
                            j, lo = 2 * q + i, (2 * m + i) * HEAD
                            mm = pe.matmul(s0[:, j * HEAD:(j + 1) * HEAD], m4[:, j, 2 * P:3 * P], v_at(lo, lo + HEAD),
                                           start=False, stop=(i == 1), skip_group_check=True)
                    mm.then_inc(q_done, 1)
                    pe.wait_ge(t_added, 2 * LEVELS * ROUNDS * c + 2 * LEVELS * (r + 1))
                    pe.wait_ge(q_taken, ROUNDS * c + (r + 1))
                    for j in range(4):
                        mm = pe.matmul(s1[:, j * HEAD:(j + 1) * HEAD], tt[:, j, 1], qs[:, j * HEAD:(j + 1) * HEAD], start=True, stop=True)
                    mm.then_inc(u_done, 1)
                    pe.wait_ge(u_taken, ROUNDS * c + (r + 1))
                    for q in range(2):
                        m = 2 * r + q
                        pe.matmul(zb[0][:, 0, q], AR[:, m, 1], state[:, m], start=True, stop=False, skip_group_check=True)
                        for i in range(2):
                            j, lo = 2 * q + i, (2 * m + i) * HEAD
                            out = zb[0][:, 0, q, i * HEAD:(i + 1) * HEAD]
                            pe.matmul(out, m4[:, j, P:2 * P], us[:, j * HEAD:(j + 1) * HEAD], start=False, stop=False, skip_group_check=True)
                            mm = pe.matmul(out, m4[:, j, 3 * P:4 * P], v_at(lo, lo + HEAD), start=False, stop=(i == 1),
                                           skip_group_check=True)
                    mm.then_inc(y_done, 1)
                    for q in range(2):
                        m = 2 * r + q
                        pe.matmul(zb[1][:, 0, q], nat[:, q, 0], us[:, q * P:(q + 1) * P], start=True, stop=False)
                        mm = pe.matmul(zb[1][:, 0, q], nat[:, q, 1], v_at(m * P, (m + 1) * P), start=False, stop=True)
                    mm.then_inc(ds_done, 1)


DVE_SCAN_CHAIN = 44



def phase_mixer_out(nc, const, arena, name, layer, yT, y_rows, w_out, x, out, mod_rows, ln_g, ln_b, y_ready=None, which=0):
    with ExitStack() as ctx:
        sem = signals(nc, ctx, name + "_")
        D, S = x.shape[1], x.shape[0]
        KT, TT = D // P, S // P
        gate, g_row, b_row = arena("gate", [P, D]), arena("g_row", [P, D]), arena("b_row", [P, D])
        xt = arena("xt", [P, TT, D])
        t = arena("t", [P, 2, D])
        stats, mv, dev = arena("stats", [P, 2, 6]), arena("mv", [P, 2, 2]), arena("dev", [P, 2])
        w = arena("w", [P, KT, D]) if w_out is not None else None
        turned = yT is None and w_out is not None
        if turned:
            yT = arena("yT", [P, KT, S])
        tb = [ctx.enter_context(nc.psum_tensor(f"{name}_tb{i}", [P, 512], F32)) for i in range(2)] if turned else None
        yb = [ctx.enter_context(nc.psum_tensor(f"{name}_yb{i}", [P, 2, 512], F32)) for i in range(2)] if w is not None else None
        rows_loaded, w_loaded, x_loaded = sem("rows_loaded"), sem("w_loaded"), sem("x_loaded")
        turned_s, taken, y_done, y_used = sem("turned"), sem("taken"), sem("y_done"), sem("y_used")
        normed, var_made, dev_made, stored = sem("normed"), sem("var"), sem("dev"), sem("stored")
        block = ctx.enter_context(nc.Block())
        x_v, out_v = rows(x), rows(out)

        @block.sync
        def _(sp):
            g0 = (layer * N_MOD + 3 * which + 2) * D
            if w is not None:
                for k in range(KT):
                    sp.dma_start(w[:, k], w_out[k * P:(k + 1) * P, :]).then_inc(w_loaded, 16)
            sp.dma_start(gate[:], mod_rows[g0:g0 + D].partition_broadcast(P)).then_inc(rows_loaded, 16)
            sp.dma_start(g_row[:], ln_g.partition_broadcast(P)).then_inc(rows_loaded, 16)
            sp.dma_start(b_row[:], ln_b.partition_broadcast(P)).then_inc(rows_loaded, 16)
            sp.dma_start(xt[:], x_v).then_inc(x_loaded, 16)
            for i in range(TT):
                sp.wait_ge(normed, i + 1)
                sp.dma_start(out_v[:, i], xt[:, i]).then_inc(stored, 16)
            sp.wait_ge(stored, 16 * TT)

        @block.tensor
        def _(pe):
            if w is None:
                return
            if turned:
                for k in range(KT):
                    if k >= 2:
                        pe.wait_ge(taken, k - 1)
                    for i in range(TT):
                        mm = pe.transpose(tb[k % 2][:, i * P:(i + 1) * P], y_rows[:, i, k * P:(k + 1) * P], const["ident"][:])
                    mm.then_inc(turned_s, 1)
                pe.wait_ge(taken, KT)
            pe.wait_ge(w_loaded, 16 * KT)
            for i in range(TT):
                if i >= 2:
                    pe.wait_ge(y_used, i - 1)
                for half in range(2):
                    for k in range(KT):
                        mm = pe.matmul(yb[i % 2][:, half], yT[:, k, i * P:(i + 1) * P], w[:, k, half * 512:(half + 1) * 512],
                                       start=(k == 0), stop=(k == KT - 1))
                mm.then_inc(y_done, 1)

        @block.scalar
        def _(act):
            if turned:
                for k in range(KT):
                    act.wait_ge(turned_s, k + 1)
                    nc.scalar.activation(yT[:, k], tb[k % 2][:], ACT.Copy).then_inc(taken, 1)
            for i in range(TT):
                act.wait_ge(var_made, i + 1)
                nc.scalar.activation(dev[:, i % 2:i % 2 + 1], mv[:, i % 2, 1:2], ACT.Sqrt).then_inc(dev_made, 1)

        @block.vector
        def _(dve):
            v = nc.vector
            ch = Chain(dve, sem("dve"))
            dve.wait_ge(rows_loaded, 48)
            dve.wait_ge(x_loaded, 16)
            for i in range(TT):
                y = y_rows[:, i] if w is None else yb[i % 2][:].rearrange("p a q -> p (a q)")
                b = i % 2
                if w is not None:
                    dve.wait_ge(y_done, i + 1)
                v.tensor_tensor(t[:, b], y, gate[:], ALU.mult).then_inc(y_used, 1)
                dve.wait_ge(y_used, i + 1)
                ch(v.scalar_tensor_tensor(out=t[:, b], in0=xt[:, i], scalar=ALPHA, in1=t[:, b], op0=ALU.mult, op1=ALU.add))
                for half in range(2):
                    ch(v.bn_stats(stats[:, half], t[:, b, half * 512:(half + 1) * 512]))
                ch(v.bn_aggr(mv[:, b], stats[:]))
                v.tensor_scalar(mv[:, b, 1:2], mv[:, b, 1:2], LN_EPS, None, ALU.add).then_inc(var_made, 1)
                dve.wait_ge(dev_made, i + 1)
                ch(v.reciprocal(dev[:, b:b + 1], dev[:, b:b + 1]))
                ch(v.tensor_scalar(t[:, b], t[:, b], mv[:, b, 0:1], dev[:, b:b + 1], ALU.subtract, ALU.mult))
                ch(v.tensor_tensor(t[:, b], t[:, b], g_row[:], ALU.mult))
                v.tensor_tensor(xt[:, i], t[:, b], b_row[:], ALU.add).then_inc(normed, 1)


def phase_pool_products(nc, const, arena, y2T, x, p):
    with ExitStack() as ctx:
        sem = signals(nc, ctx, "pool_")
        S, D = x.shape
        KT, TT = D // P, S // P
        GROUPS = len(POOL_WINDOWS)
        TPG = KT // GROUPS
        PAD = 16
        x_sb = arena("x", [P, TT, D])
        hT = arena("hT", [P, KT, S])
        w = arena("w", [P, KT, D])
        wg = arena("wg", [P, GROUPS, TPG, TPG * P])
        zT = arena("zT", [P, KT, PAD + S])
        s_a, s_b = arena("s_a", [P, TPG, PAD + S]), arena("s_b", [P, TPG, PAD + S])
        pT = arena("pT", [P, KT, S])
        inv = arena("inv", [P, GROUPS, S])
        scale_rows, scale = arena("scale_rows", [KT, P]), arena("scale", [P, KT])
        banks = [ctx.enter_context(nc.psum_tensor(f"pool_ps{i}", [P, 512], F32)) for i in range(7)]
        ring, xb, cb = banks[0:4], banks[4:6], banks[6]
        x_loaded = [sem(f"x{t}_loaded") for t in range(TT)]
        x_turned, h_made, w_loaded, wg_loaded, scale_loaded = (
            sem("x_turned"), sem("h_made"), sem("w_loaded"), sem("wg_loaded"), sem("scale_loaded"))
        scale_turned, scale_made, counted = sem("scale_turned"), sem("scale"), sem("counted")
        product_done, z_made, p_made, y_made = sem("product"), sem("z_made"), sem("p_made"), sem("y_made")
        block = ctx.enter_context(nc.Block())

        @block.sync
        def _(sp):
            sp.dma_start(scale_rows[:], p["scale"].rearrange("(k p) -> k p", p=P)).then_inc(scale_loaded, 16)
            load_x(sp, rows(x), x_sb, x_loaded)
            for k in range(KT):
                sp.dma_start(w[:, k], p["w_in"][k * P:(k + 1) * P, :]).then_inc(w_loaded, 16)
            sp.dma_start(wg[:], p["w_grp"].rearrange("g (c p) e -> p g c e", p=P)).then_inc(wg_loaded, 16)

        @block.gpsimd
        def _(pool):
            for g, win in enumerate(POOL_WINDOWS):
                nc.gpsimd.iota(inv[:, g], pattern=[[1, S]], base=1, channel_multiplier=0,
                               allow_small_or_imprecise_dtypes=True).then_inc(counted, 1)

        @block.vector
        def _(dve):
            v = nc.vector
            ch = Chain(dve, sem("dve"))
            dve.wait_ge(scale_turned, 1)
            v.tensor_copy(scale[:], cb[:, 0:KT]).then_inc(scale_made, 1)
            ch(v.memset(zT[:, :, 0:PAD], 0.0))
            ch(v.memset(s_a[:, :, 0:PAD], 0.0))
            ch(v.memset(s_b[:, :, 0:PAD], 0.0))
            modulate(nc, dve, const, 1, 0, xb, hT, 0, x_turned, h_made)
            dve.wait_ge(counted, GROUPS)
            for g, win in enumerate(POOL_WINDOWS):
                ch(v.tensor_scalar(inv[:, g], inv[:, g], float(win), None, ALU.min))
            ch(v.reciprocal(inv[:], inv[:]))
            for g, win in enumerate(POOL_WINDOWS):
                two = slice(g * TPG, (g + 1) * TPG)
                dve.wait_ge(z_made, (g + 1) * TPG)
                src, dst, other, reach = zT[:, two], s_a, s_b, 1
                while reach < win:
                    ch(v.tensor_tensor(dst[:, :, PAD:], src[:, :, PAD:], src[:, :, PAD - reach:PAD + S - reach], ALU.add))
                    src, dst, other, reach = dst[:], other, dst, 2 * reach
                weights = inv[:, g].unsqueeze(1).to_broadcast([P, TPG, S])
                ch(v.tensor_tensor(pT[:, two], src[:, :, PAD:], weights, ALU.mult))
                v.tensor_tensor(pT[:, two], pT[:, two], zT[:, two, PAD:], ALU.subtract).then_inc(p_made, 1)

        @block.tensor
        def _(pe):
            pe.wait_ge(scale_loaded, 16)
            pe.transpose(cb[:, 0:KT], scale_rows[:], const["ident"][0:KT, 0:KT]).then_inc(scale_turned, 1)
            turn_x(pe, const, x_sb, xb, x_loaded, x_turned, h_made)
            pe.wait_ge(h_made, KT)
            pe.wait_ge(w_loaded, 16 * KT)
            for m in range(KT):
                if m >= 4:
                    pe.wait_ge(z_made, m - 3)
                for k in range(KT):
                    mm = pe.matmul(ring[m % 4][:], w[:, k, m * P:(m + 1) * P], hT[:, k], start=(k == 0), stop=(k == KT - 1))
                mm.then_inc(product_done, 1)
            pe.wait_ge(wg_loaded, 16)
            for m in range(KT):
                g = m // TPG
                pe.wait_ge(p_made, g + 1)
                if m < 4:
                    pe.wait_ge(z_made, m + 5)
                else:
                    pe.wait_ge(y_made, m - 3)
                for c in range(TPG):
                    mm = pe.matmul(ring[m % 4][:], wg[:, g, c, (m % TPG) * P:(m % TPG + 1) * P], pT[:, g * TPG + c],
                                   start=(c == 0), stop=(c == TPG - 1))
                mm.then_inc(product_done, 1)

        @block.scalar
        def _(act):
            for m in range(KT):
                act.wait_ge(product_done, m + 1)
                nc.scalar.activation(zT[:, m, PAD:], ring[m % 4][:], ACT.Copy).then_inc(z_made, 1)
            act.wait_ge(scale_made, 1)
            for m in range(KT):
                act.wait_ge(product_done, KT + m + 1)
                nc.scalar.activation(y2T[:, m], ring[m % 4][:], ACT.Copy, scale=scale[:, m:m + 1]).then_inc(y_made, 1)


def phase_route(nc, const, arena, pe_t, name, layer, x, w_q, keys):
    with ExitStack() as ctx:
        sem = signals(nc, ctx, name + "_")
        S, D = x.shape
        KT, TT = D // P, S // P
        HEADS = keys.shape[0]
        TURNS = HEADS // 2
        x_sb = arena("x", [P, TT, D])
        hT = arena("hT", [P, KT, S])
        wq, kr = arena("wq", [P, 2, KT, 2 * P]), arena("kr", [P, 2, 2, P])
        keyT, qT = arena("keyT", [P, 2, 2, P]), arena("qT", [P, 2, 2, S])
        sc, rest = arena("sc", [P, 2, TT, P]), arena("rest", [P, 2, TT, P])
        val, pos = arena("val", [P, 2, TT, TOPK]), arena("pos", [P, 2, TT, TOPK], U32)
        posf = arena("posf", [P, 2, TT, TOPK])
        cand, crest = arena("cand", [P, TT, TOPK, TOPK]), arena("crest", [P, TT, TOPK, TOPK])
        best, bpos = arena("best", [P, TT, TOPK]), arena("bpos", [P, TT, TOPK], U32)
        half_u, half_f = arena("half_u", [P, 2, TT * TOPK], U32), arena("half_f", [P, 2, TT * TOPK])
        hot = arena("hot", [P, 2, TT, TOPK, TOPK])
        picked = arena("picked", [P, 2, TT, TOPK])
        expo, gate = arena("expo", [P, TT, TOPK]), arena("gate", [P, TT, TOPK])
        total = arena("total", [P, TT])
        slots = arena("slots", [P, TT, 3, HEADS * TOPK])
        slotT, hhi, hlo = pe_t["slotT"], pe_t["hhi"], pe_t["hlo"]
        xb = [ctx.enter_context(nc.psum_tensor(f"{name}_xb{i}", [P, 512], F32)) for i in range(2)]
        kb = ctx.enter_context(nc.psum_tensor(f"{name}_kb", [P, 512], F32))
        qb = [ctx.enter_context(nc.psum_tensor(f"{name}_qb{i}", [P, 512], F32)) for i in range(2)]
        sb = [ctx.enter_context(nc.psum_tensor(f"{name}_sb{i}", [P, TT, P], F32)) for i in range(2)]
        x_loaded = [sem(f"x{t}_loaded") for t in range(TT)]
        x_turned, h_made, hhi_made, hlo_made = sem("x_turned"), sem("h_made"), sem("hhi"), sem("hlo")
        w_loaded = [sem("w0_loaded"), sem("w1_loaded")]
        key_turned, key_taken = sem("key_turned"), sem("key_taken")
        q_done, q_taken, s_done, s_taken = sem("q_done"), sem("q_taken"), sem("s_done"), sem("s_taken")
        less_made, exp_made, slots_made = sem("less"), sem("exp"), sem("slots")
        slots_turned, slotT_made = sem("slots_turned"), sem("slotT")
        s_dve, spare, spare_sp = sem("dve"), sem("spare"), sem("spare_sp")
        block = ctx.enter_context(nc.Block())
        wq_v = w_q.rearrange("(k p) e -> p k e", p=P)
        keys_v = keys.rearrange("h s k d -> k (h s) d")

        @block.sync
        def _(sp):
            load_x(sp, rows(x), x_sb, x_loaded)
            for b in range(2):
                sp.dma_start(wq[:, b], wq_v[:, :, b * 2 * P:(b + 1) * 2 * P]).then_inc(w_loaded[b], 16)
                sp.dma_start(kr[:, b], keys_v[:, 2 * b:2 * b + 2]).then_inc(w_loaded[b], 16)
            with sp.Fori(1, TURNS) as i:
                for b in range(2):
                    sp.wait_ge(q_done, 4 * i + (2 * b - 2))
                    hold(sp, spare_sp)
                    sp.dma_start(wq[:, b], wq_v[:, :, bass.ds((2 * i + b) * (2 * P), 2 * P)]).then_inc(w_loaded[b], 16)
                    sp.dma_start(kr[:, b], keys_v[:, bass.ds(4 * i + 2 * b, 2)]).then_inc(w_loaded[b], 16)

        @block.tensor
        def _(pe):
            turn_x(pe, const, x_sb, xb, x_loaded, x_turned, h_made)
            pe.wait_ge(h_made, KT)

            def head(i, b, first):
                n = 2 * i + b
                pe.wait_ge(w_loaded[b], 32 * i + 32)
                if not first:
                    pe.wait_ge(key_taken, n)
                for s in range(2):
                    mm = pe.transpose(kb[:, s * P:(s + 1) * P], kr[:, b, s], const["ident"][:])
                mm.then_inc(key_turned, 1)
                for s in range(2):
                    if not first:
                        pe.wait_ge(q_taken, 2 * n + (s - 1))
                    for k in range(KT):
                        mm = pe.matmul(qb[s][:], wq[:, b, k, s * P:(s + 1) * P], hT[:, k], start=(k == 0), stop=(k == KT - 1))
                    mm.then_inc(q_done, 1)
                pe.wait_ge(key_taken, n + 1)
                pe.wait_ge(q_taken, 2 * n + 2)
                for s in range(2):
                    if not first:
                        pe.wait_ge(s_taken, 2 * n + (s - 1))
                    for t in range(TT):
                        mm = pe.matmul(sb[s][:, t], qT[:, b, s, t * P:(t + 1) * P], keyT[:, b, s], start=True, stop=True)
                    mm.then_inc(s_done, 1)

            head(0, 0, True)
            head(0, 1, False)
            with pe.Fori(1, TURNS) as i:
                for b in range(2):
                    head(i, b, False)
            pe.wait_ge(slots_made, TURNS)
            for q in range(3):
                bank = (xb[0], xb[1], kb)[q]
                for t in range(TT):
                    mm = pe.transpose(bank[:, t * P:(t + 1) * P], slots[:, t, q], const["ident"][:])
                mm.then_inc(slots_turned, 1)

        @block.scalar
        def _(act):
            a = nc.scalar
            for k in range(KT):
                act.wait_ge(h_made, k + 1)
                a.activation(hhi[:, k], hT[:, k], ACT.Copy).then_inc(hhi_made, 1)
            with act.Fori(0, TURNS) as i:
                for b in range(2):
                    n = 2 * i + b
                    act.wait_ge(key_turned, n + 1)
                    a.activation(keyT[:, b].rearrange("p s k -> p (s k)"), kb[:, 0:2 * P], ACT.Copy).then_inc(key_taken, 1)
                    for s in range(2):
                        act.wait_ge(q_done, 2 * n + (s + 1))
                        a.activation(qT[:, b, s], qb[s][:], ACT.Copy).then_inc(q_taken, 1)
                    for s in range(2):
                        act.wait_ge(s_done, 2 * n + (s + 1))
                        if s == 0:
                            act.wait_ge(less_made, n + 1)
                        a.activation(sc[:, s], sb[s][:], ACT.Copy).then_inc(s_taken, 1)
                    act.wait_ge(less_made, n + 2)
                    a.activation(expo[:], expo[:], ACT.Exp).then_inc(exp_made, 1)
            for q in range(3):
                act.wait_ge(slots_turned, q + 1)
                a.activation(slotT[:, q], (xb[0], xb[1], kb)[q][:], ACT.Copy).then_inc(slotT_made, 1)

        @block.vector
        def _(dve):
            v = nc.vector
            ch = Chain(dve, s_dve, per=DVE_ROUTE_CHAIN)
            modulate(nc, dve, const, layer, 3, xb, hT, 0, x_turned, h_made)
            for k in range(KT):
                dve.wait_ge(hhi_made, k + 1)
                v.tensor_tensor(hlo[:, k], hT[:, k], hhi[:, k].bitcast(F32), ALU.subtract).then_inc(hlo_made, 1)
            v.memset(total[:], 0.0).then_inc(less_made, 1)

            def together(instructions):
                for ins in instructions[:-1]:
                    ins.then_inc(s_dve, 1)
                    ch.n += 1
                ch(instructions[-1])

            def top16(values, rest, out, index):
                lists = range(len(values))
                hold(dve, spare)
                together([v.max(out[n][:, 0:8], values[n]) for n in lists])
                hold(dve, spare)
                together([v.match_replace(rest[n], out[n][:, 0:8], values[n], LOWEST) for n in lists] +
                         [v.max_index(index[n][:, 0:8], out[n][:, 0:8], values[n]) for n in lists])
                hold(dve, spare)
                together([v.max(out[n][:, 8:16], rest[n]) for n in lists])
                hold(dve, spare)
                together([v.max_index(index[n][:, 8:16], out[n][:, 8:16], rest[n]) for n in lists])

            with dve.Fori(0, TURNS) as i:
                ch.enter(i)
                for b in range(2):
                    n = 2 * i + b
                    for s in range(2):
                        dve.wait_ge(s_taken, 2 * n + (s + 1))
                        top16([sc[:, s, t] for t in range(TT)], [rest[:, s, t] for t in range(TT)],
                              [val[:, s, t] for t in range(TT)], [pos[:, s, t] for t in range(TT)])
                    ch(v.tensor_copy(posf[:], pos[:]))
                    first = val[:, 0].unsqueeze(3).to_broadcast([P, TT, TOPK, TOPK])
                    second = val[:, 1].unsqueeze(2).to_broadcast([P, TT, TOPK, TOPK])
                    ch(v.tensor_tensor(cand[:], first, second, ALU.add))
                    flat = lambda x, t: x[:, t].rearrange("p a b -> p (a b)")
                    top16([flat(cand, t) for t in range(TT)], [flat(crest, t) for t in range(TT)],
                          [best[:, t] for t in range(TT)], [bpos[:, t] for t in range(TT)])
                    v.tensor_tensor(expo[:], best[:], best[:, :, 0:1].to_broadcast([P, TT, TOPK]),
                                    ALU.subtract).then_inc(less_made, 1)
                    bflat = bpos[:].rearrange("p t k -> p (t k)")
                    together([v.tensor_scalar(half_u[:, 0], bflat, 4, None, ALU.logical_shift_right),
                              v.tensor_scalar(half_u[:, 1], bflat, TOPK - 1, None, ALU.bitwise_and)])
                    ch(v.tensor_copy(half_f[:], half_u[:]))
                    ranks = const["iota"][:, 0:TOPK].unsqueeze(1).to_broadcast([P, TT * TOPK, TOPK])
                    for s in range(2):
                        hs = hot[:, s].rearrange("p t a b -> p (t a) b")
                        ch(v.tensor_tensor(hs, ranks, half_f[:, s].unsqueeze(2).to_broadcast([P, TT * TOPK, TOPK]), ALU.is_equal))
                        ch(v.tensor_tensor(hot[:, s], hot[:, s], posf[:, s].unsqueeze(2).to_broadcast([P, TT, TOPK, TOPK]), ALU.mult))
                        ch(v.tensor_reduce(picked[:, s].rearrange("p t k -> p (t k)"), hs, AX.X, ALU.add))
                    dve.wait_ge(exp_made, n + 1)
                    ch(v.tensor_reduce(total[:], expo[:], AX.X, ALU.add))
                    ch(v.reciprocal(total[:], total[:]))
                    ch(v.tensor_tensor(gate[:], expo[:], spread(total[:], TOPK), ALU.mult))
                    col = bass.ds(n * TOPK, TOPK)
                    together([v.tensor_scalar(slots[:, :, 0, col], gate[:], 1.0, None, ALU.mult),
                              v.tensor_scalar(slots[:, :, 1, col], picked[:, 0], 1.0, None, ALU.mult)])
                    ins = v.tensor_scalar(slots[:, :, 2, col], picked[:, 1], 1.0, None, ALU.mult)
                    if b == 0:
                        ch(ins)
                    else:
                        ins.then_inc(slots_made, 1)
            ch.leave(TURNS)


DVE_ROUTE_CHAIN = 153


def phase_expand(nc, const, arena, pe_t, name, w_dram):
    with ExitStack() as ctx:
        sem = signals(nc, ctx, name + "_")
        G = 8
        slotT = pe_t["slotT"]
        TT = slotT.shape[2] // P
        GROUPS = P // G
        NB = 2
        PER = 2 * GROUPS
        hot_j, hot_i = arena("hot_j", [P, 2, G, P]), arena("hot_i", [P, 2, G, P])
        wb = arena("wb", [P, 2, P, P])
        banks = [ctx.enter_context(nc.psum_tensor(f"{name}_b{n}", [P, G, P], F32)) for n in range(NB)]
        j_made, i_made = sem("hot_j"), sem("hot_i")
        spread_done, taken, stored = sem("spread"), sem("taken"), [sem("stored0"), sem("stored1")]
        spare = sem("spare")
        block = ctx.enter_context(nc.Block())
        TURNS = TT // 2
        iota = const["iota"][:].unsqueeze(1).to_broadcast([P, G, P])
        iota_row = const["iota"][:]

        @block.vector
        def _(dve):
            v = nc.vector

            def turn(i, first):
                for half in range(2):
                    for g in range(GROUPS):
                        n = half * GROUPS + g
                        if not first or n >= 2:
                            dve.wait_ge(spread_done, PER * i + (n - 1))
                        for q in range(G):
                            at = bass.ds((2 * i + half) * P + (g * G + q), 1)
                            ins = v.tensor_scalar(hot_i[:, n % 2, q], iota_row, slotT[:, 1, at], slotT[:, 0, at],
                                                  ALU.is_equal, ALU.mult)
                        ins.then_inc(i_made, 1)
                        js = slotT[:, 2, bass.ds((2 * i + half) * P + g * G, G)]
                        v.tensor_tensor(hot_j[:, n % 2], iota, spread(js, P), ALU.is_equal).then_inc(j_made, 1)

            turn(0, True)
            with dve.Fori(1, TURNS) as i:
                turn(i, False)

        @block.tensor
        def _(pe):
            def turn(i, first):
                for n in range(PER):
                    pe.wait_ge(i_made, PER * i + (n + 1))
                    pe.wait_ge(j_made, PER * i + (n + 1))
                    if not first or n >= 2:
                        pe.wait_ge(taken, PER * i + (n - 1))
                    for q in range(G):
                        mm = pe.matmul(banks[n % 2][:, q], hot_j[:, n % 2, q], hot_i[:, n % 2, q], start=True, stop=True)
                    mm.then_inc(spread_done, 1)

            turn(0, True)
            with pe.Fori(1, TURNS) as i:
                turn(i, False)

        @block.scalar
        def _(act):
            def turn(i, first):
                for n in range(PER):
                    half, g = n // GROUPS, n % GROUPS
                    if g == 0 and not first:
                        act.wait_ge(stored[half], 16 * i)
                    act.wait_ge(spread_done, PER * i + (n + 1))
                    nc.scalar.activation(wb[:, half, :, g * G:(g + 1) * G], banks[n % 2][:].rearrange("p t i -> p i t"),
                                         ACT.Copy).then_inc(taken, 1)

            turn(0, True)
            with act.Fori(1, TURNS) as i:
                turn(i, False)

        @block.sync
        def _(sp):
            with sp.Fori(0, TURNS) as i:
                for half in range(2):
                    sp.wait_ge(taken, PER * i + (half + 1) * GROUPS)
                    hold(sp, spare)
                    dst = w_dram[bass.ds(2 * i + half, 1)].rearrange("a j i t -> (a j) (i t)")
                    sp.dma_start(dst, wb[:, half].rearrange("p i t -> p (i t)")).then_inc(stored[half], 16)
            for half in range(2):
                sp.wait_ge(stored[half], 16 * TURNS)


def phase_experts(nc, const, arena, pe_t, name, u_tab, v_tab, w_dram):
    with ExitStack() as ctx:
        sem = signals(nc, ctx, name + "_")
        hhi, hlo, acc = pe_t["hhi"], pe_t["hlo"], pe_t["acc"]
        KT, S = hhi.shape[1], hhi.shape[2]
        D = KT * P
        TT = S // P
        ET = u_tab.shape[0] // P
        NBUF = 4
        TURNS = ET // NBUF
        OUTS = TT * 2
        u, vr, wt = arena("u", [P, NBUF, D]), arena("v", [P, NBUF, D]), arena("wt", [P, NBUF, S])
        uhi, ulo = arena("uhi", [P, 2, KT, P], F32R), arena("ulo", [P, 2, KT, P], F32R)
        vhi, vlo = arena("vhi", [P, 2, 2, D], F32R), arena("vlo", [P, 2, 2, D], F32R)
        phi, plo = arena("phi", [P, 2, 2, S], F32R), arena("plo", [P, 2, 2, S], F32R)
        gel, pf = arena("gel", [P, 2, S]), arena("pf", [P, 2, S])
        tb = ctx.enter_context(nc.psum_tensor(f"{name}_tb", [P, KT, P], F32))
        ub = [ctx.enter_context(nc.psum_tensor(f"{name}_ub{i}", [P, S], F32)) for i in range(2)]
        vb = [ctx.enter_context(nc.psum_tensor(f"{name}_vb{i}", [P, 512], F32)) for i in range(4)]
        u_loaded = [sem(f"u{q}_loaded") for q in range(NBUF)]
        v_loaded = [sem(f"v{q}_loaded") for q in range(NBUF)]
        w_loaded = [sem(f"w{q}_loaded") for q in range(NBUF)]
        u_turned, uhi_made, ulo_made, act_done = sem("u_turned"), sem("uhi"), sem("ulo"), sem("act_done")
        gel_made, pf_made, phi_made, plo_made = sem("gel"), sem("pf"), sem("phi"), sem("plo")
        vhi_made, vlo_made, out_done, added = sem("vhi"), sem("vlo"), sem("out_done"), sem("added")
        zeroed, spare = sem("zeroed"), sem("spare")
        block = ctx.enter_context(nc.Block())

        def loads(sp, q, e):
            experts = e * P if isinstance(e, int) else None
            rows_at = slice(experts, experts + P) if experts is not None else bass.ds(e * P, P)
            i_at = slice(e, e + 1) if isinstance(e, int) else bass.ds(e, 1)
            return (u_tab[rows_at, :], v_tab[rows_at, :], w_dram[:, :, i_at].rearrange("b j i t -> j b (i t)"))

        @block.sync
        def _(sp):
            wt_v = lambda q: wt[:, q].rearrange("p (b t) -> p b t", b=TT)
            for q in range(NBUF):
                us, vs, ws = loads(sp, q, q)
                sp.dma_start(u[:, q], us).then_inc(u_loaded[q], 16)
                sp.dma_start(wt_v(q), ws).then_inc(w_loaded[q], 16)
                sp.dma_start(vr[:, q], vs).then_inc(v_loaded[q], 16)
            with sp.Fori(1, TURNS) as i:
                for q in range(NBUF):
                    us, vs, ws = loads(sp, q, NBUF * i + q)
                    last = NBUF * i + (q - NBUF + 1)
                    sp.wait_ge(u_turned, last)
                    hold(sp, spare)
                    sp.dma_start(u[:, q], us).then_inc(u_loaded[q], 16)
                    sp.wait_ge(pf_made, last)
                    hold(sp, spare)
                    sp.dma_start(wt_v(q), ws).then_inc(w_loaded[q], 16)
                    sp.wait_ge(vlo_made, last)
                    hold(sp, spare)
                    sp.dma_start(vr[:, q], vs).then_inc(v_loaded[q], 16)

        @block.tensor
        def _(pe):
            def turn_u(q, turns, e, first=False):
                pe.wait_ge(u_loaded[q], 16 * turns)
                if not first:
                    pe.wait_ge(ulo_made, e)
                for k in range(KT):
                    mm = pe.transpose(tb[:, k], u[:, q, k * P:(k + 1) * P], const["ident"][:])
                mm.then_inc(u_turned, 1)

            def u_product(q, e, first=False):
                pe.wait_ge(ulo_made, e + 1)
                if not first:
                    pe.wait_ge(gel_made, e - 1)
                n = 0
                for k in range(KT):
                    for a, h in ((uhi, hhi), (uhi, hlo), (ulo, hhi)):
                        mm = pe.matmul(ub[q % 2][:], a[:, q % 2, k], h[:, k], start=(n == 0), stop=(n == 3 * KT - 1))
                        n += 1
                mm.then_inc(act_done, 1)

            def v_product(b, pair, first=False):
                pe.wait_ge(plo_made, 2 * pair + 2)
                pe.wait_ge(vlo_made, 2 * pair + 2)
                for o in range(OUTS):
                    if not first or o >= 4:
                        pe.wait_ge(added, OUTS * pair + (o - 3))
                    t, half = o // 2, o % 2
                    n = 0
                    for i in range(2):
                        for a, w in ((phi, vhi), (phi, vlo), (plo, vhi)):
                            mm = pe.matmul(vb[o % 4][:], a[:, b, i, t * P:(t + 1) * P], w[:, b, i, half * 512:(half + 1) * 512],
                                           start=(n == 0), stop=(n == 5))
                            n += 1
                    mm.then_inc(out_done, 1)

            def turn(i, first=False, last=False):
                for q in range(NBUF):
                    e = NBUF * i + q
                    u_product(q, e, first and q < 2)
                    if not (last and q >= 2):
                        turn_u((q + 2) % NBUF, i + 1 + (q >= 2), e + 2)
                    if q % 2 and not (first and q == 1):
                        v_product(((q // 2) + 1) % 2, 2 * i + (q // 2 - 1), first and q == 3)

            turn_u(0, 1, 0, True)
            turn_u(1, 1, 1)
            turn(0, first=True)
            with pe.Fori(1, TURNS - 1) as i:
                turn(i)
            turn(TURNS - 1, last=True)
            v_product(1, 2 * TURNS - 1)

        @block.scalar
        def _(act):
            a = nc.scalar

            def take_u(q, e):
                act.wait_ge(u_turned, e + 1)
                a.activation(uhi[:, q % 2], tb[:], ACT.Copy).then_inc(uhi_made, 1)

            def turn(i, first=False, last=False):
                for q in range(NBUF):
                    e = NBUF * i + q
                    b = q // 2
                    act.wait_ge(v_loaded[q], 16 * i + 16)
                    if not (first):
                        act.wait_ge(out_done, OUTS * (2 * i + (b - 1)))
                    a.activation(vhi[:, b, q % 2], vr[:, q], ACT.Copy).then_inc(vhi_made, 1)
                    if not (last and q >= 2):
                        take_u(q, e + 2)
                    act.wait_ge(act_done, e + 1)
                    if not (first and q < 2):
                        act.wait_ge(pf_made, e - 1)
                    a.activation(gel[:, q % 2], ub[q % 2][:], ACT.Gelu).then_inc(gel_made, 1)
                    act.wait_ge(pf_made, e + 1)
                    a.activation(phi[:, b, q % 2], pf[:, q % 2], ACT.Copy).then_inc(phi_made, 1)

            take_u(0, 0)
            take_u(1, 1)
            turn(0, first=True)
            with act.Fori(1, TURNS - 1) as i:
                turn(i)
            turn(TURNS - 1, last=True)

        @block.gpsimd
        def _(pool):
            def turn(i, first=False):
                for q in range(NBUF):
                    e = NBUF * i + q
                    pool.wait_ge(vhi_made, e + 1)
                    nc.gpsimd.tensor_tensor(vlo[:, q // 2, q % 2], vr[:, q], vhi[:, q // 2, q % 2].bitcast(F32),
                                            ALU.subtract).then_inc(vlo_made, 1)

            with pool.Fori(0, TURNS) as i:
                turn(i)

        @block.vector
        def _(dve):
            v = nc.vector

            def low_u(q, e):
                dve.wait_ge(uhi_made, e + 1)
                v.tensor_tensor(ulo[:, q % 2], tb[:], uhi[:, q % 2].bitcast(F32), ALU.subtract).then_inc(ulo_made, 1)

            def add(pair, first=False):
                for o in range(OUTS):
                    t, half = o // 2, o % 2
                    dve.wait_ge(out_done, OUTS * pair + (o + 1))
                    if not first:
                        dve.wait_ge(added, OUTS * pair + (o - OUTS + 1))
                    piece = acc[:, t, half * 512:(half + 1) * 512]
                    v.tensor_tensor(piece, piece, vb[o % 4][:], ALU.add).then_inc(added, 1)

            def turn(i, first=False, last=False):
                for q in range(NBUF):
                    e = NBUF * i + q
                    if not (last and q >= 2):
                        low_u(q, e + 2)
                    dve.wait_ge(gel_made, e + 1)
                    dve.wait_ge(w_loaded[q], 16 * i + 16)
                    if not (first and q < 2):
                        dve.wait_ge(plo_made, e - 1)
                    v.tensor_tensor(pf[:, q % 2], gel[:, q % 2], wt[:, q], ALU.mult).then_inc(pf_made, 1)
                    dve.wait_ge(phi_made, e + 1)
                    v.tensor_tensor(plo[:, q // 2, q % 2], pf[:, q % 2], phi[:, q // 2, q % 2].bitcast(F32),
                                    ALU.subtract).then_inc(plo_made, 1)
                    if q % 2 and not (first and q == 1):
                        add(2 * i + (q // 2 - 1), first and q == 3)

            v.memset(acc[:], 0.0).then_inc(zeroed, 1)
            dve.wait_ge(zeroed, 1)
            low_u(0, 0)
            low_u(1, 1)
            turn(0, first=True)
            with dve.Fori(1, TURNS - 1) as i:
                turn(i)
            turn(TURNS - 1, last=True)
            add(2 * TURNS - 1)



def hybrid_trunk(nc, x, c, ada_w, ada_b, ln_g, ln_b, rw_mu, rw_w_rkv, rw_w0, rw_w1, rw_w2, rw_a0, rw_a1, rw_a2,
                 rw_g1, rw_g2, rw_k_k, rw_k_a, rw_r_k, rw_lnx_g, rw_lnx_b, rw_w_o,
                 pl_w_in, pl_w_grp, pl_scale, pl_w_out, pe_w_q, pe_keys, pe_u, pe_v, out):
    x, out = x[0], out[0]
    S, D = x.shape
    KT, TT = D // P, S // P
    dram = lambda name, shape: nc.dram_tensor(name, shape, F32, kind="Internal").ap()
    stream = [dram(f"stream{i}", [S, D]) for i in range(3)]
    mod_rows = dram("mod_rows", [DEPTH * N_MOD * D])
    w_dram = dram("routing", [TT, P, P, P])
    base, end = (nc.sbuf_base + 31) // 32 * 32, nc.sbuf_usable_end
    fixed = Arena(nc, "const", base, end)
    const = dict(ident=fixed("ident", [P, P]), ones=fixed("ones", [P, P]), masks=fixed("masks", [P, 4 * P]),
                 blockones=fixed("blockones", [P, P]), level_masks=fixed("level_masks", [P, 6, P]),
                 pair_mask_T=fixed("pair_mask_T", [P, P]), iota=fixed("iota", [P, P]),
                 modT=fixed("modT", [P, DEPTH * N_MOD * KT]))
    area = lambda prefix, offset=fixed.offset: Arena(nc, prefix, offset, end)

    phase_constants(nc, const, area("make"))
    phase_modulation(nc, const, area("mod"), c, ada_w, ada_b, mod_rows)

    rwa = area("rw")
    rw = {n: rwa(n, [P, KT, S]) for n in ("rT", "kT", "aT", "sT")}
    rw.update({n: rwa(n, [P, TT, D]) for n in ("v", "g")})
    rw["cols"] = rwa("cols", [P, 88])
    pr = dict(mu=rw_mu[0].rearrange("n d -> (n d)"), w0=rw_w0[0], a0=rw_a0[0], k_k=rw_k_k[0], k_a=rw_k_a[0],
              r_k=rw_r_k[0].rearrange("h n -> (h n)"), w_rkv=rw_w_rkv[0], w1=rw_w1[0], w2=rw_w2[0], a1=rw_a1[0],
              a2=rw_a2[0], g1=rw_g1[0], g2=rw_g2[0], lnx_g=rw_lnx_g[0], lnx_b=rw_lnx_b[0])
    phase_rwkv_products(nc, const, area("rwp", rwa.offset), rw, x, pr)
    phase_rwkv_scan(nc, const, area("scan", rwa.offset), rw, pr, D, S)
    phase_mixer_out(nc, const, area("out0", rwa.offset), "out0", 0, None, rw["g"], rw_w_o[0], x, stream[0], mod_rows,
                    ln_g[0, 0], ln_b[0, 0])

    pea = area("peer")
    pe_t = dict(hhi=pea("hhi", [P, KT, S], F32R), hlo=pea("hlo", [P, KT, S], F32R), slotT=pea("slotT", [P, 3, S]),
                acc=pea("acc", [P, TT, D]))

    def peer(layer, src, dst):
        n = f"peer{layer}"
        phase_route(nc, const, area(n + "r", pea.offset), pe_t, n + "r", layer, src, pe_w_q[layer], pe_keys[layer])
        phase_expand(nc, const, area(n + "w", pea.offset), pe_t, n + "w", w_dram)
        phase_experts(nc, const, area(n + "e", pea.offset), pe_t, n + "e", pe_u[layer], pe_v[layer], w_dram)
        phase_mixer_out(nc, const, area(n + "o", pea.offset), n + "o", layer, None, pe_t["acc"], None, src, dst, mod_rows,
                        ln_g[layer, 1], ln_b[layer, 1], which=1)

    peer(0, stream[0], stream[1])
    pla = area("pl")
    y2T = pla("y2T", [P, KT, S])
    pp = dict(w_in=pl_w_in[0], w_grp=pl_w_grp[0], scale=pl_scale[0])
    phase_pool_products(nc, const, area("pool", pla.offset), y2T, stream[1], pp)
    phase_mixer_out(nc, const, area("out1", pla.offset), "out1", 1, y2T, None, pl_w_out[0], stream[1], stream[2], mod_rows,
                    ln_g[1, 0], ln_b[1, 0])
    peer(1, stream[2], out)


_INS = ["x", "c", "ada_w", "ada_b", "ln_g", "ln_b", "rw_mu", "rw_w_rkv", "rw_w0", "rw_w1", "rw_w2", "rw_a0", "rw_a1",
        "rw_a2", "rw_g1", "rw_g2", "rw_k_k", "rw_k_a", "rw_r_k", "rw_lnx_g", "rw_lnx_b", "rw_w_o", "pl_w_in", "pl_w_grp",
        "pl_scale", "pl_w_out", "pe_w_q", "pe_keys", "pe_u", "pe_v"]


def kernel(**inputs):
    import numpy as np
    import concourse.bacc as bacc
    from concourse.bass_utils import run_bass_kernel_spmd

    nc = bacc.Bacc("TRN2", target_bir_lowering=False, num_devices=1)
    arrays, args = {}, []
    for name in _INS:
        a = np.ascontiguousarray(inputs[name])
        arrays[f"in_{name}"] = a
        args.append(nc.dram_tensor(f"in_{name}", a.shape, mybir.dt.from_np(a.dtype), kind="ExternalInput").ap())
    args.append(nc.dram_tensor("out", arrays["in_x"].shape, F32, kind="ExternalOutput").ap())
    hybrid_trunk(nc, *args)
    r = run_bass_kernel_spmd(nc, [arrays], core_ids=[0])
    return r.results[0]["out"]
```

```python
from contextlib import ExitStack

import concourse.bass as bass
from concourse import mybir

F32 = mybir.dt.float32
F32R = mybir.dt.float32r
U32 = mybir.dt.uint32
ALU = mybir.AluOpType
ACT = mybir.ActivationFunctionType
AX = mybir.AxisListType

P = 128
HEAD = 64
TOPK = 16
POOL_WINDOWS = (2, 4, 8, 16)
DEPTH = 2
ALPHA = (2 * DEPTH) ** 0.25
LN_EPS = 1e-5
GN_EPS = 64e-5
N_MOD = 6
LOG_DECAY = -float(2.718281828459045 ** -0.5)
LOWEST = -3.0e38


class Chain:

    def __init__(self, eng, sem, per=0):
        self.eng, self.sem, self.per, self.base, self.n, self.turn = eng, sem, per, 0, 0, None

    def __call__(self, ins):
        ins.then_inc(self.sem, 1)
        self.n += 1
        if self.turn is None:
            self.eng.wait_ge(self.sem, self.base + self.n)
        else:
            self.eng.wait_ge(self.sem, self.turn * self.per + (self.base + self.n))

    def enter(self, turn):
        self.base, self.n, self.turn = self.base + self.n, 0, turn

    def leave(self, turns):
        assert self.n == self.per, f"{self.n} signals in a turn, {self.per} said"
        self.base, self.n, self.turn = self.base + turns * self.per, 0, None


def hold(eng, spare):
    eng.sem_inc(spare, 1)


def signals(nc, ctx, prefix):
    made = []

    def sem(name):
        made.append(nc.alloc_semaphore(prefix + name))
        return made[-1]

    def end():
        nc.clear_and_free_semaphores(made)
        nc.all_engine_barrier()

    ctx.callback(end)
    return sem


class Arena:

    def __init__(self, nc, prefix, offset, end):
        self.nc, self.prefix, self.offset, self.end = nc, prefix, offset, end

    def __call__(self, name, shape, dtype=F32):
        size = 4
        for n in shape[1:]:
            size *= n
        t = self.nc.alloc_sbuf_tensor_at(f"{self.prefix}_{name}", shape, dtype, offset=self.offset)
        self.offset += (size + 31) // 32 * 32
        assert self.offset <= self.end, f"{self.prefix}_{name} ends at {self.offset} of {self.end}"
        return t


def rows(ap):
    return ap.rearrange("(t p) d -> p t d", p=P)


def phase_constants(nc, const, arena):
    with ExitStack() as ctx:
        made = signals(nc, ctx, "const_")("made")
        block = ctx.enter_context(nc.Block())
        ident, ones, masks = const["ident"], const["ones"], const["masks"]
        blockones = const["blockones"]
        lvl, lvl1T, iota = const["level_masks"], const["pair_mask_T"], const["iota"]
        full = arena("full", [P, 2 * P])

        @block.gpsimd
        def _(pool):
            g = nc.gpsimd
            ch = Chain(pool, made)

            def select(out, in_, pattern, base, mult, op=ALU.is_ge, fill=0.0):
                return g.affine_select(out=out, in_=in_, pattern=pattern, compare_op=op, fill=fill, base=base,
                                       channel_multiplier=mult)

            ch(g.memset(full[:], 1.0))
            ch(g.memset(ones[:], 1.0))
            ch(g.iota(iota[:], pattern=[[1, P]], base=0, channel_multiplier=0,
                      allow_small_or_imprecise_dtypes=True))
            ch(select(ident[:], full[:, 0:P], [[-1, P]], 0, 1, ALU.is_equal))
            for j, strict in enumerate((1, 0, 1, 0)):
                ch(select(masks[:, j * P:(j + 1) * P], full[:, 0:P], [[1, P]], -strict, -1))
            b2 = blockones[:].rearrange("p (b q) -> p b q", b=2)
            ch(select(b2, full[:, 0:P].rearrange("p (b q) -> p b q", b=2), [[-HEAD, 2], [0, HEAD]], 0, 1))
            ch(select(b2, b2, [[HEAD, 2], [0, HEAD]], HEAD - 1, -1))
            for n in range(1, 7):
                half = 1 << n
                v = lvl[:, n - 1, :].rearrange("p (b q) -> p b q", q=2 * half)
                nb = P // (2 * half)
                src = full[:, 0:P].rearrange("p (b q) -> p b q", q=2 * half)
                ch(select(v, src, [[-2 * half, nb], [0, 2 * half]], -half, 1))
                ch(select(v, v, [[2 * half, nb], [0, 2 * half]], 2 * half - 1, -1))
                ch(select(v, v, [[0, nb], [-1, 2 * half]], half - 1, 0))
            v = lvl1T[:].rearrange("p (b q) -> p b q", q=2)
            ch(select(v, full[:, 0:P].rearrange("p (b q) -> p b q", q=2), [[-2, P // 2], [0, 2]], 0, 1, ALU.is_equal))
            ch(select(v, v, [[0, P // 2], [1, 2]], -1, 0))


FIRST_MODS = 2


def mod_source(ada_w, layer, n, k):
    D = ada_w.shape[1]
    return ada_w[layer, k * P:(k + 1) * P, bass.ds(n * D, D)]


def phase_first_modulation(nc, const, arena, c, ada_w, ada_b):
    with ExitStack() as ctx:
        sem = signals(nc, ctx, "mod_")
        modT, ident, cond, biasT, raw = (const[n] for n in ("modT", "ident", "cond", "biasT", "mod_raw"))
        D = ada_w.shape[1]
        KT = D // P
        NC = DEPTH * N_MOD * KT
        w, acc = arena("w", [P, FIRST_MODS, KT, D]), arena("acc", [P, FIRST_MODS, D])
        sig, in_rows = arena("sig", [P, KT]), arena("in_rows", [NC + KT, P])
        turned = ctx.enter_context(nc.psum_tensor("mod_turned", [P, 512], F32))
        sums = ctx.enter_context(nc.psum_tensor("mod_sums", [P, 512], F32))
        in_loaded, in_turned, sig_done, cond_done = sem("in_loaded"), sem("in_turned"), sem("sig"), sem("cond")
        w_loaded = [sem(f"w{i}_loaded") for i in range(FIRST_MODS * KT)]
        acc_done, sums_done = sem("acc"), sem("sums")
        block = ctx.enter_context(nc.Block())

        @block.sync
        def _(sp):
            sp.dma_start(in_rows[0:NC, :], ada_b.rearrange("l (m p) -> (l m) p", p=P)).then_inc(in_loaded, 16)
            sp.dma_start(in_rows[NC:NC + KT, :], c.rearrange("b (k p) -> (b k) p", p=P)).then_inc(in_loaded, 16)
            for m in range(FIRST_MODS):
                for k in range(KT):
                    sp.dma_start(w[:, m, k], mod_source(ada_w, 0, m, k)).then_inc(w_loaded[m * KT + k], 16)

        @block.scalar
        def _(act):
            act.wait_ge(in_turned, 1)
            nc.scalar.activation(sig[:], turned[:, NC:NC + KT], ACT.Sigmoid).then_inc(sig_done, 1)

        @block.vector
        def _(dve):
            v = nc.vector
            ch = Chain(dve, sem("dve"))
            dve.wait_ge(sig_done, 1)
            v.tensor_tensor(cond[:], turned[:, NC:NC + KT], sig[:], ALU.mult).then_inc(cond_done, 1)
            dve.wait_ge(cond_done, 1)
            ch(v.tensor_copy(biasT[:], turned[:, 0:NC]))
            for m in range(FIRST_MODS):
                for k in range(KT):
                    dve.wait_ge(w_loaded[m * KT + k], 16)
                    if k == 0:
                        ch(v.tensor_scalar(acc[:, m], w[:, m, 0], cond[:, 0:1], None, ALU.mult))
                        continue
                    ins = v.scalar_tensor_tensor(out=acc[:, m], in0=w[:, m, k], scalar=cond[:, k:k + 1], in1=acc[:, m],
                                                 op0=ALU.mult, op1=ALU.add)
                    if k < KT - 1:
                        ch(ins)
                    else:
                        ins.then_inc(acc_done, 1)
            dve.wait_ge(sums_done, 1)
            ch(v.tensor_copy(raw[:, 0:FIRST_MODS * KT], sums[:, 0:FIRST_MODS * KT]))
            ch(v.tensor_tensor(modT[:, 0:2 * KT], raw[:, 0:2 * KT], biasT[:, 0:2 * KT], ALU.add))
            v.tensor_scalar(modT[:, KT:2 * KT], modT[:, KT:2 * KT], 1.0, None, ALU.add)

        @block.tensor
        def _(pe):
            pe.wait_ge(in_loaded, 32)
            pe.transpose(turned[:, 0:NC + KT], in_rows[:], ident[0:NC + KT, 0:NC + KT]).then_inc(in_turned, 1)
            pe.wait_ge(acc_done, FIRST_MODS)
            for m in range(FIRST_MODS):
                for k in range(KT):
                    mm = pe.matmul(sums[:, m * KT + k:m * KT + k + 1], acc[:, m, k * P:(k + 1) * P], const["ones"][:, 0:1],
                                   start=True, stop=True)
            mm.then_inc(sums_done, 1)


def phase_last_modulation(nc, const, arena, mod_rows):
    with ExitStack() as ctx:
        sem = signals(nc, ctx, "modl_")
        modT, biasT, raw = const["modT"], const["biasT"], const["mod_raw"]
        NC = modT.shape[1]
        KT = NC // (DEPTH * N_MOD)
        first = FIRST_MODS * KT
        out_rows = arena("rows", [NC, P])
        bank = ctx.enter_context(nc.psum_tensor("modl_bank", [P, 512], F32))
        summed, turned, taken, stored = sem("summed"), sem("turned"), sem("taken"), sem("stored")
        block = ctx.enter_context(nc.Block())

        @block.vector
        def _(dve):
            v = nc.vector
            ch = Chain(dve, sem("dve"))
            v.tensor_tensor(raw[:], raw[:], biasT[:], ALU.add).then_inc(summed, 1)
            dve.wait_ge(summed, 1)
            ch(v.tensor_copy(modT[:, first:NC], raw[:, first:NC]))
            for layer in range(DEPTH):
                for n in (1, 4):
                    m = layer * N_MOD + n
                    if m >= FIRST_MODS:
                        cols = modT[:, m * KT:(m + 1) * KT]
                        ch(v.tensor_scalar(cols, cols, 1.0, None, ALU.add))
            dve.wait_ge(turned, 1)
            v.tensor_copy(out_rows[:], bank[0:NC, 0:P]).then_inc(taken, 1)

        @block.tensor
        def _(pe):
            pe.wait_ge(summed, 1)
            pe.transpose(bank[0:NC, 0:P], raw[:], const["ident"][:]).then_inc(turned, 1)

        @block.sync
        def _(sp):
            sp.wait_ge(taken, 1)
            sp.dma_start(mod_rows.rearrange("(m p) -> m p", p=P), out_rows[:]).then_inc(stored, 16)
            sp.wait_ge(stored, 16)



def load_x(sp, x_dram, x_sb, sem):
    for t in range(x_sb.shape[1]):
        sp.dma_start(x_sb[:, t], x_dram[:, t]).then_inc(sem[t], 16)


def turn_x(pe, const, x_sb, banks, x_loaded, x_turned, h_made):
    TT, KT = x_sb.shape[1], x_sb.shape[2] // P
    for k in range(KT):
        if k >= 2:
            pe.wait_ge(h_made, k - 1)
        for t in range(TT):
            if k == 0:
                pe.wait_ge(x_loaded[t], 16)
            mm = pe.transpose(banks[k % 2][:, t * P:(t + 1) * P], x_sb[:, t, k * P:(k + 1) * P], const["ident"][:])
        mm.then_inc(x_turned, 1)


def modulate(nc, dve, const, layer, which, banks, hT, at, x_turned, h_made):
    KT, S = hT.shape[1], 512
    for k in range(KT):
        dve.wait_ge(x_turned, k + 1)
        col = (layer * N_MOD + which) * KT + k
        shift, scale = const["modT"][:, col:col + 1], const["modT"][:, col + KT:col + KT + 1]
        nc.vector.tensor_scalar(hT[:, k, at:at + S], banks[k % 2][:, 0:S], scale, shift, ALU.mult,
                                ALU.add).then_inc(h_made, 1)


def phase_rwkv_products(nc, const, arena, rw, x, p):
    with ExitStack() as ctx:
        sem = signals(nc, ctx, "rwp_")
        D = x.shape[1]
        S = x.shape[0]
        KT, TT = D // P, S // P
        HALF = D // 2
        DL, AL, GL = p["w1"].shape[1], p["a1"].shape[1], p["g1"].shape[1]
        GR = GL - P
        hT = arena("hT", [P, KT, S + 1])
        xs = arena("xs", [P, 2, KT, S])
        w = arena("w", [P, 2, KT, HALF])
        w1, a1, g1 = arena("w1", [P, KT, DL]), arena("a1", [P, KT, AL]), arena("g1", [P, KT, GL])
        tw, ta, tg = arena("tw", [DL, S]), arena("ta", [AL, S]), arena("tg", [P, 2, S])
        x_sb = xs[:, 1].rearrange("p k s -> p (k s)").rearrange("p (t d) -> p t d", t=TT)
        colrows = w[:, 1].rearrange("p k s -> p (k s)")[0:88, 0:P]
        cols, mu1 = rw["cols"], arena("mu1", [P, 48])
        low = w[:, 0].rearrange("p k s -> p (k s)")
        w2, a2, g2a, g2b = (low[0:DL, 0:D], low[0:AL, D:2 * D], low[:, 2 * D:3 * D], low[0:GR, 3 * D:4 * D])
        banks = [ctx.enter_context(nc.psum_tensor(f"rwp_ps{i}", [P, 512], F32)) for i in range(7)]
        ring, xb, cb = banks[0:4], banks[4:6], banks[6]
        cols_loaded, cols_turned, cols_made, mu1_made = sem("cols_loaded"), sem("cols_turned"), sem("cols"), sem("mu1")
        x_loaded = [sem(f"x{t}_loaded") for t in range(TT)]
        x_turned, h_made, pad_made = sem("x_turned"), sem("h_made"), sem("pad_made")
        w_loaded, lora_loaded = [sem("w0_loaded"), sem("w1_loaded")], sem("lora_loaded")
        xs_made, product_done, evacuated = sem("xs_made"), sem("product_done"), sem("evacuated")
        R0, K0, V0 = 0, KT, 2 * KT
        TW = V0 + 2 * TT
        S0 = TW + 1
        TA = S0 + KT
        A0 = TA + 1
        TG = A0 + KT
        G0 = TG + 2
        END = G0 + 2 * TT
        last_use = [K0, V0, TW, S0, A0, G0]
        block = ctx.enter_context(nc.Block())

        @block.sync
        def _(sp):
            for q, (name, n) in enumerate((("mu", 6), ("w0", 1), ("a0", 1), ("k_k", 1), ("k_a", 1), ("r_k", 1))):
                r0 = 0 if q == 0 else 48 + 8 * (q - 1)
                sp.dma_start(colrows[r0:r0 + n * KT, :], p[name].rearrange("(m p) -> m p", p=P)).then_inc(cols_loaded, 16)
            load_x(sp, rows(x), x_sb, x_loaded)
            for n in range(6):
                if n == 1:
                    sp.wait_ge(cols_turned, 1)
                if n >= 2:
                    sp.wait_ge(product_done, (n - 1) * 4)
                src = p["w_rkv"][n // 2].rearrange("(k p) e -> p k e", p=P)[:, :, (n % 2) * HALF:(n % 2 + 1) * HALF]
                sp.dma_start(w[:, n % 2], src).then_inc(w_loaded[n % 2], 16)
                if n == 0:
                    for t, name in ((w1, "w1"), (a1, "a1"), (g1, "g1")):
                        sp.dma_start(t[:], p[name].rearrange("(k p) e -> p k e", p=P)).then_inc(lora_loaded, 16)
            sp.wait_ge(product_done, 5 * 4)
            for dst, src in ((w2, p["w2"]), (a2, p["a2"]), (g2a, p["g2"][0:P, :]), (g2b, p["g2"][P:GL, :])):
                sp.dma_start(dst, src).then_inc(w_loaded[0], 16)

        @block.vector
        def _(dve):
            v = nc.vector
            ch = Chain(dve, sem("dve"))
            dve.wait_ge(cols_turned, 1)
            v.tensor_copy(cols[:], cb[:, 0:88]).then_inc(cols_made, 1)
            dve.wait_ge(cols_made, 1)
            ch(v.tensor_scalar(mu1[:], cols[:, 0:48], -1.0, 1.0, ALU.mult, ALU.add))
            ch(v.memset(hT[:, :, 0:1], 0.0))
            modulate(nc, dve, const, 0, 0, xb, hT, 1, x_turned, h_made)
            dve.wait_ge(h_made, KT)
            for n in range(6):
                if n >= 2:
                    dve.wait_ge(product_done, last_use[n - 2])
                for k in range(KT):
                    ins = v.tensor_scalar(xs[:, n % 2, k], hT[:, k, 0:S], cols[:, n * KT + k:n * KT + k + 1], None, ALU.mult)
                    ins.then_inc(ch.sem, 1)
                    ch.n += 1
                dve.wait_ge(ch.sem, ch.base + ch.n)
                for k in range(KT):
                    v.scalar_tensor_tensor(out=xs[:, n % 2, k], in0=hT[:, k, 1:S + 1], scalar=mu1[:, n * KT + k:n * KT + k + 1],
                                           in1=xs[:, n % 2, k], op0=ALU.mult, op1=ALU.add).then_inc(xs_made, 1)

        @block.tensor
        def _(pe):
            pe.wait_ge(cols_loaded, 6 * 16)
            pe.transpose(cb[:, 0:88], colrows, const["ident"][0:88, 0:88]).then_inc(cols_turned, 1)
            turn_x(pe, const, x_sb, xb, x_loaded, x_turned, h_made)
            count = [0]

            def product(width, terms):
                n = count[0]
                if n >= len(ring):
                    pe.wait_ge(evacuated, n - len(ring) + 1)
                out = ring[n % len(ring)][0:width, :]
                for j, (lhsT, rhs) in enumerate(terms):
                    mm = pe.matmul(out, lhsT, rhs, start=(j == 0), stop=(j == len(terms) - 1))
                mm.then_inc(product_done, 1)
                count[0] += 1

            for n in range(2):
                pe.wait_ge(xs_made, (n + 1) * KT)
                for m in range(KT):
                    h = 2 * n + m // 4
                    pe.wait_ge(w_loaded[h % 2], 16 * (h // 2 + 1))
                    product(P, [(w[:, h % 2, k, (m % 4) * P:(m % 4 + 1) * P], xs[:, n % 2, k]) for k in range(KT)])
            pe.wait_ge(xs_made, 3 * KT)
            for half in range(2):
                pe.wait_ge(w_loaded[half], 16 * 3)
                for t in range(TT):
                    product(P, [(xs[:, 0, k, t * P:(t + 1) * P], w[:, half, k]) for k in range(KT)])
            pe.wait_ge(lora_loaded, 48)
            pe.wait_ge(xs_made, 4 * KT)
            product(DL, [(w1[:, k], xs[:, 1, k]) for k in range(KT)])
            pe.wait_ge(w_loaded[0], 16 * 7)
            pe.wait_ge(evacuated, TW + 1)
            for m in range(KT):
                product(P, [(w2[:, m * P:(m + 1) * P], tw[:])])
            pe.wait_ge(xs_made, 5 * KT)
            product(AL, [(a1[:, k], xs[:, 0, k]) for k in range(KT)])
            pe.wait_ge(evacuated, TA + 1)
            for m in range(KT):
                product(P, [(a2[:, m * P:(m + 1) * P], ta[:])])
            pe.wait_ge(xs_made, 6 * KT)
            product(P, [(g1[:, k, 0:P], xs[:, 1, k]) for k in range(KT)])
            product(GR, [(g1[:, k, P:GL], xs[:, 1, k]) for k in range(KT)])
            pe.wait_ge(evacuated, TG + 2)
            for half in range(2):
                for t in range(TT):
                    cs = slice(half * HALF, (half + 1) * HALF)
                    product(P, [(tg[:, 0, t * P:(t + 1) * P], g2a[:, cs]), (tg[0:GR, 1, t * P:(t + 1) * P], g2b[:, cs])])
            assert count[0] == END

        @block.scalar
        def _(act):
            def take(n, out, func, width=P, bias=0.0):
                act.wait_ge(product_done, n + 1)
                nc.scalar.activation(out, ring[n % len(ring)][0:width, :], func, bias=bias).then_inc(evacuated, 1)

            for m in range(KT):
                take(R0 + m, rw["rT"][:, m], ACT.Copy)
            for m in range(KT):
                take(K0 + m, rw["kT"][:, m], ACT.Copy)
            for half in range(2):
                for t in range(TT):
                    take(V0 + half * TT + t, rw["v"][:, t, half * HALF:(half + 1) * HALF], ACT.Copy)
            act.wait_ge(cols_made, 1)
            take(TW, tw[:], ACT.Tanh, DL)
            for m in range(KT):
                take(S0 + m, rw["sT"][:, m], ACT.Sigmoid, bias=cols[:, 48 + m:49 + m])
            take(TA, ta[:], ACT.Copy, AL)
            for m in range(KT):
                take(A0 + m, rw["aT"][:, m], ACT.Sigmoid, bias=cols[:, 56 + m:57 + m])
            take(TG, tg[:, 0], ACT.Sigmoid)
            take(TG + 1, tg[0:GR, 1], ACT.Sigmoid, GR)
            for half in range(2):
                for t in range(TT):
                    take(G0 + half * TT + t, rw["g"][:, t, half * HALF:(half + 1) * HALF], ACT.Copy)


def spread(cols, n):
    return cols.unsqueeze(2).to_broadcast([P, cols.shape[1], n])


def phase_rwkv_scan(nc, const, arena, rw, p, ada_w, D, S):
    with ExitStack() as ctx:
        sem = signals(nc, ctx, "scan_")
        KT, TT = D // P, S // P
        NH = D // HEAD
        RH = 8
        RT = RH * HEAD // P
        ROUNDS = NH // RH
        STREAMS, SH = 2, RH // 2
        MID = P // 2 - 1
        LEVELS = 6
        AR = arena("AR", [P, KT, 2, P])
        BT, KS = arena("BT", [P, KT, P]), arena("KS", [P, KT, P])
        e2 = KS
        t0, t1, t2, t3 = (arena(f"t{i}", [P, KT, P]) for i in range(4))
        state = arena("state", [P, KT, P])
        m4 = arena("m4", [P, RH, 4 * P])
        tt = arena("tt", [P, RH, 2, P])
        zs = arena("zs", [P, STREAMS, SH, P])
        qs, us = arena("qs", [P, RH * HEAD]), arena("us", [P, RH * HEAD])
        nat = arena("nat", [P, RT, 2, P])
        y = arena("y", [P, D])
        yc, ysq = t2[:].rearrange("p k s -> p (k s)"), t3[:].rearrange("p k s -> p (k s)")
        lnx_g, lnx_b = arena("lnx_g", [P, D]), arena("lnx_b", [P, D])
        cen, carry, fac = arena("cen", [P, KT]), arena("carry", [P, KT]), arena("fac", [P, KT])
        omka, bonus = arena("omka", [P, KT]), arena("bonus", [P, NH])
        st1, st2 = arena("st1", [P, NH]), arena("st2", [P, NH])
        ds_tmp = arena("ds_tmp", [P, RT, P])
        mod_w, mod_acc = arena("mod_w", [P, 2, D]), arena("mod_acc", [P, 2, D])
        zb = [ctx.enter_context(nc.psum_tensor(f"scan_z{i}", [P, SH, P], F32)) for i in range(STREAMS)]
        db = [ctx.enter_context(nc.psum_tensor(f"scan_d{i}", [P, SH, 2, P], F32)) for i in range(STREAMS)]
        sb2 = ctx.enter_context(nc.psum_tensor("scan_s", [P, 2, 512], F32))
        s0, s1 = sb2[:, 0], sb2[:, 1]
        cols = rw["cols"]
        c_kk, c_ka, c_rk = cols[:, 64:72], cols[:, 72:80], cols[:, 80:88]
        ident, masks, lvl, cond = const["ident"], const["masks"], const["level_masks"], const["cond"]
        rows_loaded = sem("rows_loaded")
        kk0_made, sq_made, norm_done, norm_clamped, root_made = (
            sem("kk0"), sem("sq"), sem("norm"), sem("clamped"), sem("root"))
        logs_made, exps_made, fac_made, state_scaled, stage_made = (
            sem("logs"), sem("exps"), sem("fac"), sem("state_scaled"), sem("stage"))
        rk_made, bonus_done, bonus_taken = sem("rk"), sem("bonus"), sem("bonus_taken")
        nat_turned, nat_taken = sem("nat_turned"), sem("nat_taken")
        gram_done, m4_made = sem("gram"), sem("m4")
        t1T_made, t1_turned, t1_taken = sem("t1T"), sem("t1_turned"), sem("t1_taken")
        z_done, zs_made, d_done, t_added = sem("z"), sem("zs"), sem("d"), sem("t_added")
        q_done, q_taken, u_done, u_taken = sem("q"), sem("q_taken"), sem("u"), sem("u_taken")
        y_done, y_taken, ds_done, ds_taken = sem("y"), sem("y_taken"), sem("ds"), sem("ds_taken")
        yc_made, ysq_made, var_made, dev_made = sem("yc"), sem("ysq"), sem("var"), sem("dev")
        mod_loaded = [sem("mod0_loaded"), sem("mod1_loaded")]
        mod_used, mod_summed, mod_done, mod_taken = sem("mod_used"), sem("mod_summed"), sem("mod_done"), sem("mod_taken")
        s_dve, s_pool, spare, spare_sp = sem("dve"), sem("pool"), sem("spare"), sem("spare_sp")
        MOD_RUNS = [(0, FIRST_MODS, (N_MOD - FIRST_MODS) // 2), (1, 0, N_MOD // 2)]
        MOD_PAIRS = sum(n for _, _, n in MOD_RUNS)
        block = ctx.enter_context(nc.Block())

        def gram_bank(j):
            s, q = j // SH, j % SH
            if q % 3 == 2:
                return zb[s][:].rearrange("p a q -> p (a q)")
            return db[s][:, 2 * (q % 3):2 * (q % 3) + 2].rearrange("p a b q -> p (a b q)")

        @block.sync
        def _(sp):
            sp.dma_start(lnx_g[:], p["lnx_g"].partition_broadcast(P)).then_inc(rows_loaded, 16)
            sp.dma_start(lnx_b[:], p["lnx_b"].partition_broadcast(P)).then_inc(rows_loaded, 16)

            def load(layer, n, k, used):
                if used is not None:
                    sp.wait_ge(mod_used, used)
                    hold(sp, spare_sp)
                sp.dma_start(mod_w[:, k % 2], mod_source(ada_w, layer, n, k)).then_inc(mod_loaded[k % 2], 16)

            before = 0
            for layer, n0, pairs in MOD_RUNS:
                start = 0
                if before == 0:
                    start = 1
                    for q in range(2):
                        for k in range(KT):
                            load(layer, n0 + q, k, None if KT * q + k < 2 else KT * q + k - 1)
                with sp.Fori(start, pairs) as i:
                    for q in range(2):
                        for k in range(KT):
                            load(layer, n0 + 2 * i + q, k, (2 * KT) * i + (2 * KT * before + KT * q + k - 1))
                before += pairs

        @block.gpsimd
        def _(pool):
            g = nc.gpsimd

            def pair(i, first):
                for q in range(2):
                    if not first:
                        pool.wait_ge(mod_done, 2 * i + (q - 1))
                    for k in range(KT):
                        n = KT * q + k
                        pool.wait_ge(mod_loaded[k % 2], 16 * KT * i + 16 * (n // 2 + 1))
                        hold(pool, spare)
                        if k == 0:
                            ins = g.tensor_scalar(mod_acc[:, q], mod_w[:, 0], cond[:, 0:1], None, ALU.mult)
                        else:
                            g.tensor_scalar(mod_w[:, k % 2], mod_w[:, k % 2], cond[:, k:k + 1], None, ALU.mult).then_inc(s_pool, 1)
                            pool.wait_ge(s_pool, (2 * KT - 2) * i + (n - q))
                            pool.wait_ge(mod_used, 2 * KT * i + n)
                            ins = g.tensor_tensor(mod_acc[:, q], mod_acc[:, q], mod_w[:, k % 2], ALU.add)
                        ins.then_inc(mod_used, 1)

            pair(0, True)
            with pool.Fori(1, MOD_PAIRS) as i:
                pair(i, False)

        @block.vector
        def _(dve):
            v = nc.vector
            ch = Chain(dve, s_dve, per=DVE_SCAN_CHAIN)
            ch(v.memset(state[:], 0.0))
            ch(v.memset(carry[:], 0.0))
            ch(v.tensor_scalar(omka[:], c_ka, -1.0, 1.0, ALU.mult, ALU.add))
            dve.wait_ge(rows_loaded, 32)

            def take_mods(pair):
                dve.wait_ge(mod_done, 2 * pair + 2)
                v.tensor_scalar(const["mod_raw"][:, bass.ds(2 * KT * pair + FIRST_MODS * KT, 2 * KT)], db[0][:, 0, 0, 0:2 * KT],
                                1.0, None, ALU.mult).then_inc(mod_taken, 1)

            with dve.Fori(0, TT) as c:
                ch.enter(c)
                here = bass.ds(c * P, P)
                rT, kT, aT, sT = (rw[n][:, :, here] for n in ("rT", "kT", "aT", "sT"))
                v.tensor_tensor(t0[:], kT, spread(c_kk, P), ALU.mult).then_inc(kk0_made, 1)
                for m in range(KT):
                    ins = v.tensor_tensor_scan(t2[:, m], const["ones"][:], rw["sT"][:, m, here], 0.0, ALU.mult, ALU.add)
                    if m < KT - 1:
                        ins.then_inc(s_dve, 1)
                        ch.n += 1
                ch(ins)
                ch(v.tensor_copy(cen[:], t2[:, :, MID]))
                ch(v.tensor_tensor(fac[:], carry[:], cen[:], ALU.add))
                ch(v.tensor_tensor(carry[:], t2[:, :, P - 1], cen[:], ALU.subtract))
                ch(v.tensor_tensor(t2[:], t2[:], spread(cen[:], P), ALU.subtract))
                v.tensor_tensor(t3[:], t2[:], sT, ALU.subtract).then_inc(logs_made, 1)
                dve.wait_ge(norm_done, c + 1)
                v.tensor_scalar(t1[:], sb2[:].rearrange("p b (m s) -> p (b m) s", s=P), 1e-24, None,
                                ALU.max).then_inc(norm_clamped, 1)
                dve.wait_ge(fac_made, c + 1)
                v.tensor_tensor(state[:], state[:], spread(fac[:], P), ALU.mult).then_inc(state_scaled, 1)
                dve.wait_ge(root_made, c + 1)
                ch(v.reciprocal(t1[:], t1[:]))
                dve.wait_ge(kk0_made, c + 1)
                ch(v.tensor_tensor(t0[:], t0[:], t1[:], ALU.mult))
                dve.wait_ge(exps_made, c + 1)
                ch(v.scalar_tensor_tensor(out=AR[:, :, 0], in0=t0[:], scalar=-1.0, in1=AR[:, :, 0], op0=ALU.mult, op1=ALU.mult))
                ch(v.tensor_tensor(t1[:], t0[:], aT, ALU.mult))
                ch(v.tensor_tensor(BT[:], t1[:], e2[:], ALU.mult))
                ch(v.tensor_tensor(t0[:], aT, spread(c_ka, P), ALU.mult))
                ch(v.tensor_tensor(t0[:], t0[:], spread(omka[:], P), ALU.add))
                ch(v.tensor_tensor(t0[:], t0[:], kT, ALU.mult))
                ch(v.tensor_tensor(KS[:], t0[:], e2[:], ALU.mult))
                v.tensor_tensor(AR[:, :, 1], AR[:, :, 1], rT, ALU.mult).then_inc(stage_made, 1)
                ch(v.tensor_tensor(t1[:], t0[:], rT, ALU.mult))
                v.tensor_tensor(t1[:], t1[:], spread(c_rk, P), ALU.mult).then_inc(rk_made, 1)
                for r in range(ROUNDS):
                    if r > 0:
                        dve.wait_ge(y_done, ROUNDS * c + r)
                    for s in range(STREAMS):
                        for j in range(SH * s, SH * s + SH):
                            dve.wait_ge(gram_done, RH * ROUNDS * c + (RH * r + j + 1))
                            v.tensor_tensor(m4[:, j], gram_bank(j), masks[:], ALU.mult).then_inc(m4_made, 1)
                        mine = slice(SH * s, SH * s + SH)
                        dve.wait_ge(m4_made, RH * ROUNDS * c + (RH * r + SH * s + SH))
                        mask = const["pair_mask_T"][:].unsqueeze(1).to_broadcast([P, SH, P])
                        eye = ident[:].unsqueeze(1).to_broadcast([P, SH, P])
                        ch(v.tensor_tensor(tt[:, mine, 1], m4[:, mine, 0:P], mask, ALU.mult))
                        v.tensor_tensor(tt[:, mine, 1], tt[:, mine, 1], eye, ALU.add).then_inc(t1T_made, 1)
                    for n in range(LEVELS):
                        k0 = STREAMS * LEVELS * ROUNDS * c + STREAMS * (LEVELS * r + n)
                        mask = lvl[:, n].unsqueeze(1).to_broadcast([P, SH, P])
                        for s in range(STREAMS):
                            dve.wait_ge(z_done, k0 + (s + 1))
                            v.tensor_tensor(zs[:, s], zb[s][:], mask, ALU.mult).then_inc(zs_made, 1)
                        for s in range(STREAMS):
                            mine = slice(SH * s, SH * s + SH)
                            dve.wait_ge(d_done, k0 + (s + 1))
                            if n < LEVELS - 1:
                                flat = lambda x: x.rearrange("p a b q -> p (a b q)")
                                v.tensor_tensor(flat(tt[:, mine]), flat(tt[:, mine]), flat(db[s][:]), ALU.add).then_inc(t_added, 1)
                            else:
                                v.tensor_tensor(tt[:, mine, 1], tt[:, mine, 1], db[s][:, :, 1], ALU.add).then_inc(t_added, 1)
                    dve.wait_ge(y_done, ROUNDS * c + (r + 1))
                    v.tensor_copy(y[:, RH * HEAD * r:RH * HEAD * (r + 1)], zb[0][:].rearrange("p a q -> p (a q)")).then_inc(y_taken, 1)
                    dve.wait_ge(ds_done, ROUNDS * c + (r + 1))
                    v.tensor_tensor(ds_tmp[:], zb[1][:], const["blockones"][:].unsqueeze(1).to_broadcast([P, RT, P]),
                                    ALU.mult).then_inc(ds_taken, 1)
                    dve.wait_ge(ds_taken, ROUNDS * c + (r + 1))
                    ch(v.tensor_tensor(state[:, RT * r:RT * r + RT], state[:, RT * r:RT * r + RT], ds_tmp[:], ALU.add))
                take_mods(c)
                dve.wait_ge(bonus_done, c + 1)
                v.tensor_copy(bonus[:], s0[:, 0:NH]).then_inc(bonus_taken, 1)
                dve.wait_ge(y_taken, ROUNDS * c + ROUNDS)
                heads = lambda t: t.rearrange("p (h n) -> p h n", n=HEAD)
                ch(v.tensor_reduce(st1[:], heads(y[:]), AX.X, ALU.add))
                ch(v.tensor_scalar(st1[:], st1[:], 1.0 / HEAD, None, ALU.mult))
                v.tensor_tensor(heads(yc), heads(y[:]), spread(st1[:], HEAD), ALU.subtract).then_inc(yc_made, 1)
                dve.wait_ge(yc_made, c + 1)
                vc = rw["v"][:, bass.ds(c, 1)].rearrange("p c d -> p (c d)")
                gc = rw["g"][:, bass.ds(c, 1)].rearrange("p c d -> p (c d)")
                dve.wait_ge(bonus_taken, c + 1)
                ch(v.tensor_tensor(heads(y[:]), heads(vc), spread(bonus[:], HEAD), ALU.mult))
                dve.wait_ge(ysq_made, c + 1)
                ch(v.tensor_reduce(st2[:], heads(ysq), AX.X, ALU.add))
                v.tensor_scalar(st2[:], st2[:], 1.0 / HEAD, GN_EPS, ALU.mult, ALU.add).then_inc(var_made, 1)
                dve.wait_ge(dev_made, c + 1)
                ch(v.reciprocal(st2[:], st2[:]))
                ch(v.tensor_tensor(heads(yc), heads(yc), spread(st2[:], HEAD), ALU.mult))
                ch(v.tensor_tensor(yc, yc, lnx_g[:], ALU.mult))
                ch(v.tensor_tensor(yc, yc, lnx_b[:], ALU.add))
                ch(v.tensor_tensor(y[:], y[:], yc, ALU.add))
                ch(v.tensor_tensor(gc, gc, y[:], ALU.mult))
            ch.leave(TT)
            for pair in range(TT, MOD_PAIRS):
                take_mods(pair)

        @block.scalar
        def _(act):
            a = nc.scalar
            with act.Fori(0, TT) as c:
                act.wait_ge(kk0_made, c + 1)
                a.activation(t1[:], t0[:], ACT.Square).then_inc(sq_made, 1)
                act.wait_ge(norm_clamped, c + 1)
                a.activation(t1[:], t1[:], ACT.Sqrt).then_inc(root_made, 1)
                act.wait_ge(logs_made, c + 1)
                a.activation(fac[:], fac[:], ACT.Exp, scale=LOG_DECAY).then_inc(fac_made, 1)
                a.activation(AR[:, :, 1], t2[:], ACT.Exp, scale=LOG_DECAY)
                a.activation(e2[:], t2[:], ACT.Exp, scale=-LOG_DECAY)
                a.activation(AR[:, :, 0], t3[:], ACT.Exp, scale=LOG_DECAY).then_inc(exps_made, 1)
                for r in range(ROUNDS):
                    for s in range(STREAMS):
                        act.wait_ge(t1_turned, STREAMS * ROUNDS * c + (STREAMS * r + s + 1))
                        a.activation(tt[:, SH * s:SH * s + SH, 0], zb[s][:], ACT.Copy).then_inc(t1_taken, 1)
                    act.wait_ge(nat_turned, ROUNDS * c + (r + 1))
                    a.activation(nat[:].rearrange("p a b q -> p (a b q)"), sb2[:].rearrange("p b q -> p (b q)"),
                                 ACT.Copy).then_inc(nat_taken, 1)
                    act.wait_ge(q_done, ROUNDS * c + (r + 1))
                    a.activation(qs[:], s0, ACT.Copy).then_inc(q_taken, 1)
                    act.wait_ge(u_done, ROUNDS * c + (r + 1))
                    a.activation(us[:], s1, ACT.Copy).then_inc(u_taken, 1)
                act.wait_ge(yc_made, c + 1)
                a.activation(ysq, yc, ACT.Square).then_inc(ysq_made, 1)
                act.wait_ge(var_made, c + 1)
                a.activation(st2[:], st2[:], ACT.Sqrt).then_inc(dev_made, 1)

        @block.tensor
        def _(pe):
            def sum_mods(pair):
                for q in range(2):
                    pe.wait_ge(mod_used, 2 * KT * pair + KT * (q + 1))
                    for k in range(KT):
                        mm = pe.matmul(db[0][:, 0, 0, KT * q + k:KT * q + k + 1], mod_acc[:, q, k * P:(k + 1) * P],
                                       const["ones"][:, 0:1], start=True, stop=True)
                    mm.then_inc(mod_done, 1)

            with pe.Fori(0, TT) as c:
                v_at = lambda lo, hi: rw["v"][:, bass.ds(c, 1), lo:hi].rearrange("p c d -> p (c d)")
                pe.wait_ge(sq_made, c + 1)
                for b in range(2):
                    mm = pe.matmul(sb2[:, b], const["blockones"][:], t1[:, 4 * b:4 * b + 4].rearrange("p k s -> p (k s)"),
                                   start=True, stop=True)
                mm.then_inc(norm_done, 1)
                pe.wait_ge(stage_made, c + 1)
                pe.wait_ge(norm_clamped, c + 1)
                pe.wait_ge(state_scaled, c + 1)
                for r in range(ROUNDS):
                    if r > 0:
                        pe.wait_ge(y_taken, ROUNDS * c + r)
                        pe.wait_ge(ds_taken, ROUNDS * c + r)
                    for j in range(RH):
                        m, part = RT * r + j // 2, slice(HEAD * (j % 2), HEAD * (j % 2) + HEAD)
                        if j % SH == 3:
                            pe.wait_ge(m4_made, RH * ROUNDS * c + (RH * r + j - 2))
                        ar = AR[part, m].rearrange("p b q -> p (b q)")
                        out = gram_bank(j)
                        pe.matmul(out[:, 0:2 * P], BT[part, m], ar, start=True, stop=True)
                        mm = pe.matmul(out[:, 2 * P:4 * P], KS[part, m], ar, start=True, stop=True)
                        mm.then_inc(gram_done, 1)
                    for q in range(RT):
                        for b, src in enumerate((BT, KS)):
                            n = 2 * q + b
                            mm = pe.transpose(sb2[:, n // 4, (n % 4) * P:(n % 4 + 1) * P], src[:, RT * r + q], ident[:])
                    mm.then_inc(nat_turned, 1)
                    for s in range(STREAMS):
                        pe.wait_ge(t1T_made, STREAMS * ROUNDS * c + (STREAMS * r + s + 1))
                        for i in range(SH):
                            mm = pe.transpose(zb[s][:, i], tt[:, SH * s + i, 1], ident[:])
                        mm.then_inc(t1_turned, 1)
                    for n in range(LEVELS):
                        k0 = STREAMS * LEVELS * ROUNDS * c + STREAMS * (LEVELS * r + n)
                        for s in range(STREAMS):
                            if n == 0:
                                pe.wait_ge(t1_taken, STREAMS * ROUNDS * c + (STREAMS * r + s + 1))
                            else:
                                pe.wait_ge(t_added, k0 + (s - 1))
                            for i in range(SH):
                                j = SH * s + i
                                mm = pe.matmul(zb[s][:, i], m4[:, j, 0:P], tt[:, j, 0], start=True, stop=True)
                            mm.then_inc(z_done, 1)
                        for s in range(STREAMS):
                            pe.wait_ge(zs_made, k0 + (s + 1))
                            for i in range(SH):
                                j = SH * s + i
                                if n < LEVELS - 1:
                                    pe.matmul(db[s][:, i, 0], tt[:, j, 1], zs[:, s, i], start=True, stop=True)
                                mm = pe.matmul(db[s][:, i, 1], zs[:, s, i], tt[:, j, 1], start=True, stop=True)
                            mm.then_inc(d_done, 1)
                    pe.wait_ge(nat_taken, ROUNDS * c + (r + 1))
                    for q in range(RT):
                        m = RT * r + q
                        pe.matmul(s0[:, q * P:(q + 1) * P], AR[:, m, 0], state[:, m], start=True, stop=False, skip_group_check=True)
                        for i in range(2):
                            j, lo = 2 * q + i, (2 * m + i) * HEAD
                            mm = pe.matmul(s0[:, j * HEAD:(j + 1) * HEAD], m4[:, j, 2 * P:3 * P], v_at(lo, lo + HEAD),
                                           start=False, stop=(i == 1), skip_group_check=True)
                    mm.then_inc(q_done, 1)
                    pe.wait_ge(t_added, STREAMS * LEVELS * ROUNDS * c + STREAMS * LEVELS * (r + 1))
                    pe.wait_ge(q_taken, ROUNDS * c + (r + 1))
                    for j in range(RH):
                        mm = pe.matmul(s1[:, j * HEAD:(j + 1) * HEAD], tt[:, j, 1], qs[:, j * HEAD:(j + 1) * HEAD], start=True, stop=True)
                    mm.then_inc(u_done, 1)
                    pe.wait_ge(u_taken, ROUNDS * c + (r + 1))
                    for q in range(RT):
                        m = RT * r + q
                        pe.matmul(zb[0][:, q], AR[:, m, 1], state[:, m], start=True, stop=False, skip_group_check=True)
                        for i in range(2):
                            j, lo = 2 * q + i, (2 * m + i) * HEAD
                            out = zb[0][:, q, i * HEAD:(i + 1) * HEAD]
                            pe.matmul(out, m4[:, j, P:2 * P], us[:, j * HEAD:(j + 1) * HEAD], start=False, stop=False, skip_group_check=True)
                            mm = pe.matmul(out, m4[:, j, 3 * P:4 * P], v_at(lo, lo + HEAD), start=False, stop=(i == 1),
                                           skip_group_check=True)
                    mm.then_inc(y_done, 1)
                    for q in range(RT):
                        m = RT * r + q
                        pe.matmul(zb[1][:, q], nat[:, q, 0], us[:, q * P:(q + 1) * P], start=True, stop=False)
                        mm = pe.matmul(zb[1][:, q], nat[:, q, 1], v_at(m * P, (m + 1) * P), start=False, stop=True)
                    mm.then_inc(ds_done, 1)
                sum_mods(c)
                pe.wait_ge(rk_made, c + 1)
                for m in range(KT):
                    mm = pe.matmul(s0[:, 2 * m:2 * m + 2], t1[:, m], const["blockones"][:, 0:P:HEAD], start=True, stop=True)
                mm.then_inc(bonus_done, 1)
                pe.wait_ge(bonus_taken, c + 1)
                pe.wait_ge(mod_taken, c + 1)
            for pair in range(TT, MOD_PAIRS):
                sum_mods(pair)


DVE_SCAN_CHAIN = 38



def phase_mixer_out(nc, const, arena, name, layer, yT, y_rows, w_out, x, out, mod_rows, ln_g, ln_b, y_ready=None, which=0):
    with ExitStack() as ctx:
        sem = signals(nc, ctx, name + "_")
        D, S = x.shape[1], x.shape[0]
        KT, TT = D // P, S // P
        gate, g_row, b_row = arena("gate", [P, D]), arena("g_row", [P, D]), arena("b_row", [P, D])
        xt = arena("xt", [P, TT, D])
        t = arena("t", [P, 2, D])
        stats, mv, dev = arena("stats", [P, 2, 6]), arena("mv", [P, 2, 2]), arena("dev", [P, 2])
        w = arena("w", [P, KT, D]) if w_out is not None else None
        turned = yT is None and w_out is not None
        if turned:
            yT = arena("yT", [P, KT, S])
        tb = [ctx.enter_context(nc.psum_tensor(f"{name}_tb{i}", [P, 512], F32)) for i in range(2)] if turned else None
        yb = [ctx.enter_context(nc.psum_tensor(f"{name}_yb{i}", [P, 2, 512], F32)) for i in range(2)] if w is not None else None
        rows_loaded, w_loaded, x_loaded = sem("rows_loaded"), sem("w_loaded"), sem("x_loaded")
        turned_s, taken, y_done, y_used = sem("turned"), sem("taken"), sem("y_done"), sem("y_used")
        normed, var_made, dev_made, stored = sem("normed"), sem("var"), sem("dev"), sem("stored")
        block = ctx.enter_context(nc.Block())
        x_v, out_v = rows(x), rows(out)

        @block.sync
        def _(sp):
            g0 = (layer * N_MOD + 3 * which + 2) * D
            if w is not None:
                for k in range(KT):
                    sp.dma_start(w[:, k], w_out[k * P:(k + 1) * P, :]).then_inc(w_loaded, 16)
            sp.dma_start(gate[:], mod_rows[g0:g0 + D].partition_broadcast(P)).then_inc(rows_loaded, 16)
            sp.dma_start(g_row[:], ln_g.partition_broadcast(P)).then_inc(rows_loaded, 16)
            sp.dma_start(b_row[:], ln_b.partition_broadcast(P)).then_inc(rows_loaded, 16)
            sp.dma_start(xt[:], x_v).then_inc(x_loaded, 16)
            for i in range(TT):
                sp.wait_ge(normed, i + 1)
                sp.dma_start(out_v[:, i], xt[:, i]).then_inc(stored, 16)
            sp.wait_ge(stored, 16 * TT)

        @block.tensor
        def _(pe):
            if w is None:
                return
            if turned:
                for k in range(KT):
                    if k >= 2:
                        pe.wait_ge(taken, k - 1)
                    for i in range(TT):
                        mm = pe.transpose(tb[k % 2][:, i * P:(i + 1) * P], y_rows[:, i, k * P:(k + 1) * P], const["ident"][:])
                    mm.then_inc(turned_s, 1)
                pe.wait_ge(taken, KT)
            pe.wait_ge(w_loaded, 16 * KT)
            for i in range(TT):
                if i >= 2:
                    pe.wait_ge(y_used, i - 1)
                for half in range(2):
                    for k in range(KT):
                        mm = pe.matmul(yb[i % 2][:, half], yT[:, k, i * P:(i + 1) * P], w[:, k, half * 512:(half + 1) * 512],
                                       start=(k == 0), stop=(k == KT - 1))
                mm.then_inc(y_done, 1)

        @block.scalar
        def _(act):
            if turned:
                for k in range(KT):
                    act.wait_ge(turned_s, k + 1)
                    nc.scalar.activation(yT[:, k], tb[k % 2][:], ACT.Copy).then_inc(taken, 1)
            for i in range(TT):
                act.wait_ge(var_made, i + 1)
                nc.scalar.activation(dev[:, i % 2:i % 2 + 1], mv[:, i % 2, 1:2], ACT.Sqrt).then_inc(dev_made, 1)

        @block.vector
        def _(dve):
            v = nc.vector
            ch = Chain(dve, sem("dve"))
            dve.wait_ge(rows_loaded, 48)
            dve.wait_ge(x_loaded, 16)
            for i in range(TT):
                y = y_rows[:, i] if w is None else yb[i % 2][:].rearrange("p a q -> p (a q)")
                b = i % 2
                if w is not None:
                    dve.wait_ge(y_done, i + 1)
                v.tensor_tensor(t[:, b], y, gate[:], ALU.mult).then_inc(y_used, 1)
                dve.wait_ge(y_used, i + 1)
                ch(v.scalar_tensor_tensor(out=t[:, b], in0=xt[:, i], scalar=ALPHA, in1=t[:, b], op0=ALU.mult, op1=ALU.add))
                for half in range(2):
                    ch(v.bn_stats(stats[:, half], t[:, b, half * 512:(half + 1) * 512]))
                ch(v.bn_aggr(mv[:, b], stats[:]))
                v.tensor_scalar(mv[:, b, 1:2], mv[:, b, 1:2], LN_EPS, None, ALU.add).then_inc(var_made, 1)
                dve.wait_ge(dev_made, i + 1)
                ch(v.reciprocal(dev[:, b:b + 1], dev[:, b:b + 1]))
                ch(v.tensor_scalar(t[:, b], t[:, b], mv[:, b, 0:1], dev[:, b:b + 1], ALU.subtract, ALU.mult))
                ch(v.tensor_tensor(t[:, b], t[:, b], g_row[:], ALU.mult))
                v.tensor_tensor(xt[:, i], t[:, b], b_row[:], ALU.add).then_inc(normed, 1)


def phase_pool_products(nc, const, arena, y2T, x, p):
    with ExitStack() as ctx:
        sem = signals(nc, ctx, "pool_")
        S, D = x.shape
        KT, TT = D // P, S // P
        GROUPS = len(POOL_WINDOWS)
        TPG = KT // GROUPS
        PAD = 16
        x_sb = arena("x", [P, TT, D])
        hT = arena("hT", [P, KT, S])
        w = arena("w", [P, KT, D])
        wg = arena("wg", [P, GROUPS, TPG, TPG * P])
        zT = arena("zT", [P, KT, PAD + S])
        s_a, s_b = arena("s_a", [P, TPG, PAD + S]), arena("s_b", [P, TPG, PAD + S])
        pT = arena("pT", [P, KT, S])
        inv = arena("inv", [P, GROUPS, S])
        scale_rows, scale = arena("scale_rows", [KT, P]), arena("scale", [P, KT])
        banks = [ctx.enter_context(nc.psum_tensor(f"pool_ps{i}", [P, 512], F32)) for i in range(7)]
        ring, xb, cb = banks[0:4], banks[4:6], banks[6]
        x_loaded = [sem(f"x{t}_loaded") for t in range(TT)]
        x_turned, h_made, w_loaded, wg_loaded, scale_loaded = (
            sem("x_turned"), sem("h_made"), sem("w_loaded"), sem("wg_loaded"), sem("scale_loaded"))
        scale_turned, scale_made, counted = sem("scale_turned"), sem("scale"), sem("counted")
        product_done, z_made, p_made, y_made = sem("product"), sem("z_made"), sem("p_made"), sem("y_made")
        block = ctx.enter_context(nc.Block())

        @block.sync
        def _(sp):
            sp.dma_start(scale_rows[:], p["scale"].rearrange("(k p) -> k p", p=P)).then_inc(scale_loaded, 16)
            load_x(sp, rows(x), x_sb, x_loaded)
            for k in range(KT):
                sp.dma_start(w[:, k], p["w_in"][k * P:(k + 1) * P, :]).then_inc(w_loaded, 16)
            sp.dma_start(wg[:], p["w_grp"].rearrange("g (c p) e -> p g c e", p=P)).then_inc(wg_loaded, 16)

        @block.gpsimd
        def _(pool):
            for g, win in enumerate(POOL_WINDOWS):
                nc.gpsimd.iota(inv[:, g], pattern=[[1, S]], base=1, channel_multiplier=0,
                               allow_small_or_imprecise_dtypes=True).then_inc(counted, 1)

        @block.vector
        def _(dve):
            v = nc.vector
            ch = Chain(dve, sem("dve"))
            dve.wait_ge(scale_turned, 1)
            v.tensor_copy(scale[:], cb[:, 0:KT]).then_inc(scale_made, 1)
            ch(v.memset(zT[:, :, 0:PAD], 0.0))
            ch(v.memset(s_a[:, :, 0:PAD], 0.0))
            ch(v.memset(s_b[:, :, 0:PAD], 0.0))
            modulate(nc, dve, const, 1, 0, xb, hT, 0, x_turned, h_made)
            dve.wait_ge(counted, GROUPS)
            for g, win in enumerate(POOL_WINDOWS):
                ch(v.tensor_scalar(inv[:, g], inv[:, g], float(win), None, ALU.min))
            ch(v.reciprocal(inv[:], inv[:]))
            for g, win in enumerate(POOL_WINDOWS):
                two = slice(g * TPG, (g + 1) * TPG)
                dve.wait_ge(z_made, (g + 1) * TPG)
                src, dst, other, reach = zT[:, two], s_a, s_b, 1
                while reach < win:
                    ch(v.tensor_tensor(dst[:, :, PAD:], src[:, :, PAD:], src[:, :, PAD - reach:PAD + S - reach], ALU.add))
                    src, dst, other, reach = dst[:], other, dst, 2 * reach
                weights = inv[:, g].unsqueeze(1).to_broadcast([P, TPG, S])
                ch(v.tensor_tensor(pT[:, two], src[:, :, PAD:], weights, ALU.mult))
                v.tensor_tensor(pT[:, two], pT[:, two], zT[:, two, PAD:], ALU.subtract).then_inc(p_made, 1)

        @block.tensor
        def _(pe):
            pe.wait_ge(scale_loaded, 16)
            pe.transpose(cb[:, 0:KT], scale_rows[:], const["ident"][0:KT, 0:KT]).then_inc(scale_turned, 1)
            turn_x(pe, const, x_sb, xb, x_loaded, x_turned, h_made)
            pe.wait_ge(h_made, KT)
            pe.wait_ge(w_loaded, 16 * KT)
            for m in range(KT):
                if m >= 4:
                    pe.wait_ge(z_made, m - 3)
                for k in range(KT):
                    mm = pe.matmul(ring[m % 4][:], w[:, k, m * P:(m + 1) * P], hT[:, k], start=(k == 0), stop=(k == KT - 1))
                mm.then_inc(product_done, 1)
            pe.wait_ge(wg_loaded, 16)
            for m in range(KT):
                g = m // TPG
                pe.wait_ge(p_made, g + 1)
                if m < 4:
                    pe.wait_ge(z_made, m + 5)
                else:
                    pe.wait_ge(y_made, m - 3)
                for c in range(TPG):
                    mm = pe.matmul(ring[m % 4][:], wg[:, g, c, (m % TPG) * P:(m % TPG + 1) * P], pT[:, g * TPG + c],
                                   start=(c == 0), stop=(c == TPG - 1))
                mm.then_inc(product_done, 1)

        @block.scalar
        def _(act):
            for m in range(KT):
                act.wait_ge(product_done, m + 1)
                nc.scalar.activation(zT[:, m, PAD:], ring[m % 4][:], ACT.Copy).then_inc(z_made, 1)
            act.wait_ge(scale_made, 1)
            for m in range(KT):
                act.wait_ge(product_done, KT + m + 1)
                nc.scalar.activation(y2T[:, m], ring[m % 4][:], ACT.Copy, scale=scale[:, m:m + 1]).then_inc(y_made, 1)


def phase_route(nc, const, arena, pe_t, name, layer, x, w_q, keys):
    with ExitStack() as ctx:
        sem = signals(nc, ctx, name + "_")
        S, D = x.shape
        KT, TT = D // P, S // P
        HEADS = keys.shape[0]
        TURNS = HEADS // 2
        x_sb = arena("x", [P, TT, D])
        hT = arena("hT", [P, KT, S])
        wq, kr = arena("wq", [P, 2, KT, 2 * P]), arena("kr", [P, 2, 2, P])
        keyT, qT = arena("keyT", [P, 2, 2, P]), arena("qT", [P, 2, 2, S])
        sc, rest = arena("sc", [P, 2, TT, P]), arena("rest", [P, 2, TT, P])
        val, pos = arena("val", [P, 2, TT, TOPK]), arena("pos", [P, 2, TT, TOPK], U32)
        posf = arena("posf", [P, 2, TT, TOPK])
        cand, crest = arena("cand", [P, TT, TOPK, TOPK]), arena("crest", [P, TT, TOPK, TOPK])
        best, bpos = arena("best", [P, TT, TOPK]), arena("bpos", [P, TT, TOPK], U32)
        half_u, half_f = arena("half_u", [P, 2, TT * TOPK], U32), arena("half_f", [P, 2, TT * TOPK])
        hot = arena("hot", [P, 2, TT, TOPK, TOPK])
        picked = arena("picked", [P, 2, TT, TOPK])
        expo, gate = arena("expo", [P, TT, TOPK]), arena("gate", [P, TT, TOPK])
        total = arena("total", [P, TT])
        slots = arena("slots", [P, TT, 3, HEADS * TOPK])
        slotT, hhi, hlo = pe_t["slotT"], pe_t["hhi"], pe_t["hlo"]
        xb = [ctx.enter_context(nc.psum_tensor(f"{name}_xb{i}", [P, 512], F32)) for i in range(2)]
        kb = ctx.enter_context(nc.psum_tensor(f"{name}_kb", [P, 512], F32))
        qb = [ctx.enter_context(nc.psum_tensor(f"{name}_qb{i}", [P, 512], F32)) for i in range(2)]
        sb = [ctx.enter_context(nc.psum_tensor(f"{name}_sb{i}", [P, TT, P], F32)) for i in range(2)]
        x_loaded = [sem(f"x{t}_loaded") for t in range(TT)]
        x_turned, h_made, hhi_made, hlo_made = sem("x_turned"), sem("h_made"), sem("hhi"), sem("hlo")
        w_loaded = [sem("w0_loaded"), sem("w1_loaded")]
        key_turned, key_taken = sem("key_turned"), sem("key_taken")
        q_done, q_taken, s_done, s_taken = sem("q_done"), sem("q_taken"), sem("s_done"), sem("s_taken")
        less_made, exp_made, slots_made = sem("less"), sem("exp"), sem("slots")
        slots_turned, slotT_made = sem("slots_turned"), sem("slotT")
        s_dve, spare, spare_sp = sem("dve"), sem("spare"), sem("spare_sp")
        block = ctx.enter_context(nc.Block())
        wq_v = w_q.rearrange("(k p) e -> p k e", p=P)
        keys_v = keys.rearrange("h s k d -> k (h s) d")

        @block.sync
        def _(sp):
            load_x(sp, rows(x), x_sb, x_loaded)
            for b in range(2):
                sp.dma_start(wq[:, b], wq_v[:, :, b * 2 * P:(b + 1) * 2 * P]).then_inc(w_loaded[b], 16)
                sp.dma_start(kr[:, b], keys_v[:, 2 * b:2 * b + 2]).then_inc(w_loaded[b], 16)
            with sp.Fori(1, TURNS) as i:
                for b in range(2):
                    sp.wait_ge(q_done, 4 * i + (2 * b - 2))
                    hold(sp, spare_sp)
                    sp.dma_start(wq[:, b], wq_v[:, :, bass.ds((2 * i + b) * (2 * P), 2 * P)]).then_inc(w_loaded[b], 16)
                    sp.dma_start(kr[:, b], keys_v[:, bass.ds(4 * i + 2 * b, 2)]).then_inc(w_loaded[b], 16)

        @block.tensor
        def _(pe):
            turn_x(pe, const, x_sb, xb, x_loaded, x_turned, h_made)
            pe.wait_ge(h_made, KT)

            def head(i, b, first):
                n = 2 * i + b
                pe.wait_ge(w_loaded[b], 32 * i + 32)
                if not first:
                    pe.wait_ge(key_taken, n)
                for s in range(2):
                    mm = pe.transpose(kb[:, s * P:(s + 1) * P], kr[:, b, s], const["ident"][:])
                mm.then_inc(key_turned, 1)
                for s in range(2):
                    if not first:
                        pe.wait_ge(q_taken, 2 * n + (s - 1))
                    for k in range(KT):
                        mm = pe.matmul(qb[s][:], wq[:, b, k, s * P:(s + 1) * P], hT[:, k], start=(k == 0), stop=(k == KT - 1))
                    mm.then_inc(q_done, 1)
                pe.wait_ge(key_taken, n + 1)
                pe.wait_ge(q_taken, 2 * n + 2)
                for s in range(2):
                    if not first:
                        pe.wait_ge(s_taken, 2 * n + (s - 1))
                    for t in range(TT):
                        mm = pe.matmul(sb[s][:, t], qT[:, b, s, t * P:(t + 1) * P], keyT[:, b, s], start=True, stop=True)
                    mm.then_inc(s_done, 1)

            head(0, 0, True)
            head(0, 1, False)
            with pe.Fori(1, TURNS) as i:
                for b in range(2):
                    head(i, b, False)
            pe.wait_ge(slots_made, TURNS)
            for q in range(3):
                bank = (xb[0], xb[1], kb)[q]
                for t in range(TT):
                    mm = pe.transpose(bank[:, t * P:(t + 1) * P], slots[:, t, q], const["ident"][:])
                mm.then_inc(slots_turned, 1)

        @block.scalar
        def _(act):
            a = nc.scalar
            for k in range(KT):
                act.wait_ge(h_made, k + 1)
                a.activation(hhi[:, k], hT[:, k], ACT.Copy).then_inc(hhi_made, 1)
            with act.Fori(0, TURNS) as i:
                for b in range(2):
                    n = 2 * i + b
                    act.wait_ge(key_turned, n + 1)
                    a.activation(keyT[:, b].rearrange("p s k -> p (s k)"), kb[:, 0:2 * P], ACT.Copy).then_inc(key_taken, 1)
                    for s in range(2):
                        act.wait_ge(q_done, 2 * n + (s + 1))
                        a.activation(qT[:, b, s], qb[s][:], ACT.Copy).then_inc(q_taken, 1)
                    for s in range(2):
                        act.wait_ge(s_done, 2 * n + (s + 1))
                        if s == 0:
                            act.wait_ge(less_made, n + 1)
                        a.activation(sc[:, s], sb[s][:], ACT.Copy).then_inc(s_taken, 1)
                    act.wait_ge(less_made, n + 2)
                    a.activation(expo[:], expo[:], ACT.Exp).then_inc(exp_made, 1)
            for q in range(3):
                act.wait_ge(slots_turned, q + 1)
                a.activation(slotT[:, q], (xb[0], xb[1], kb)[q][:], ACT.Copy).then_inc(slotT_made, 1)

        @block.vector
        def _(dve):
            v = nc.vector
            ch = Chain(dve, s_dve, per=DVE_ROUTE_CHAIN)
            modulate(nc, dve, const, layer, 3, xb, hT, 0, x_turned, h_made)
            for k in range(KT):
                dve.wait_ge(hhi_made, k + 1)
                v.tensor_tensor(hlo[:, k], hT[:, k], hhi[:, k].bitcast(F32), ALU.subtract).then_inc(hlo_made, 1)
            v.memset(total[:], 0.0).then_inc(less_made, 1)

            def together(instructions):
                for ins in instructions[:-1]:
                    ins.then_inc(s_dve, 1)
                    ch.n += 1
                ch(instructions[-1])

            def top16(values, rest, out, index):
                lists = range(len(values))
                hold(dve, spare)
                together([v.max(out[n][:, 0:8], values[n]) for n in lists])
                hold(dve, spare)
                together([v.match_replace(rest[n], out[n][:, 0:8], values[n], LOWEST) for n in lists] +
                         [v.max_index(index[n][:, 0:8], out[n][:, 0:8], values[n]) for n in lists])
                hold(dve, spare)
                together([v.max(out[n][:, 8:16], rest[n]) for n in lists])
                hold(dve, spare)
                together([v.max_index(index[n][:, 8:16], out[n][:, 8:16], rest[n]) for n in lists])

            with dve.Fori(0, TURNS) as i:
                ch.enter(i)
                for b in range(2):
                    n = 2 * i + b
                    for s in range(2):
                        dve.wait_ge(s_taken, 2 * n + (s + 1))
                        top16([sc[:, s, t] for t in range(TT)], [rest[:, s, t] for t in range(TT)],
                              [val[:, s, t] for t in range(TT)], [pos[:, s, t] for t in range(TT)])
                    ch(v.tensor_copy(posf[:], pos[:]))
                    first = val[:, 0].unsqueeze(3).to_broadcast([P, TT, TOPK, TOPK])
                    second = val[:, 1].unsqueeze(2).to_broadcast([P, TT, TOPK, TOPK])
                    ch(v.tensor_tensor(cand[:], first, second, ALU.add))
                    flat = lambda x, t: x[:, t].rearrange("p a b -> p (a b)")
                    top16([flat(cand, t) for t in range(TT)], [flat(crest, t) for t in range(TT)],
                          [best[:, t] for t in range(TT)], [bpos[:, t] for t in range(TT)])
                    v.tensor_tensor(expo[:], best[:], best[:, :, 0:1].to_broadcast([P, TT, TOPK]),
                                    ALU.subtract).then_inc(less_made, 1)
                    bflat = bpos[:].rearrange("p t k -> p (t k)")
                    together([v.tensor_scalar(half_u[:, 0], bflat, 4, None, ALU.logical_shift_right),
                              v.tensor_scalar(half_u[:, 1], bflat, TOPK - 1, None, ALU.bitwise_and)])
                    ch(v.tensor_copy(half_f[:], half_u[:]))
                    ranks = const["iota"][:, 0:TOPK].unsqueeze(1).to_broadcast([P, TT * TOPK, TOPK])
                    for s in range(2):
                        hs = hot[:, s].rearrange("p t a b -> p (t a) b")
                        ch(v.tensor_tensor(hs, ranks, half_f[:, s].unsqueeze(2).to_broadcast([P, TT * TOPK, TOPK]), ALU.is_equal))
                        ch(v.tensor_tensor(hot[:, s], hot[:, s], posf[:, s].unsqueeze(2).to_broadcast([P, TT, TOPK, TOPK]), ALU.mult))
                        ch(v.tensor_reduce(picked[:, s].rearrange("p t k -> p (t k)"), hs, AX.X, ALU.add))
                    dve.wait_ge(exp_made, n + 1)
                    ch(v.tensor_reduce(total[:], expo[:], AX.X, ALU.add))
                    ch(v.reciprocal(total[:], total[:]))
                    ch(v.tensor_tensor(gate[:], expo[:], spread(total[:], TOPK), ALU.mult))
                    col = bass.ds(n * TOPK, TOPK)
                    together([v.tensor_scalar(slots[:, :, 0, col], gate[:], 1.0, None, ALU.mult),
                              v.tensor_scalar(slots[:, :, 1, col], picked[:, 0], 1.0, None, ALU.mult)])
                    ins = v.tensor_scalar(slots[:, :, 2, col], picked[:, 1], 1.0, None, ALU.mult)
                    if b == 0:
                        ch(ins)
                    else:
                        ins.then_inc(slots_made, 1)
            ch.leave(TURNS)


DVE_ROUTE_CHAIN = 153


def phase_expand(nc, const, arena, pe_t, name, w_dram):
    with ExitStack() as ctx:
        sem = signals(nc, ctx, name + "_")
        G = 8
        slotT = pe_t["slotT"]
        TT = slotT.shape[2] // P
        GROUPS = P // G
        NB = 2
        PER = 2 * GROUPS
        hot_j, hot_i = arena("hot_j", [P, 2, G, P]), arena("hot_i", [P, 2, G, P])
        wb = arena("wb", [P, 2, P, P])
        banks = [ctx.enter_context(nc.psum_tensor(f"{name}_b{n}", [P, G, P], F32)) for n in range(NB)]
        gcur = arena("gcur", [P, 2, P])
        j_made, raw_made, i_made, gates_made = sem("hot_j"), sem("raw_i"), sem("hot_i"), sem("gates")
        spread_done, taken, stored = sem("spread"), sem("taken"), [sem("stored0"), sem("stored1")]
        spare = sem("spare")
        block = ctx.enter_context(nc.Block())
        TURNS = TT // 2
        iota = const["iota"][:].unsqueeze(1).to_broadcast([P, G, P])

        @block.vector
        def _(dve):
            v = nc.vector

            def turn(i, first):
                for half in range(2):
                    gates = slotT[:, 0, bass.ds((2 * i + half) * P, P)]
                    if not first:
                        dve.wait_ge(i_made, PER * i + (half - 1) * GROUPS)
                    v.tensor_scalar(gcur[:, half], gates, 1.0, None, ALU.mult).then_inc(gates_made, 1)
                    for g in range(GROUPS):
                        n = half * GROUPS + g
                        if not first or n >= 2:
                            dve.wait_ge(spread_done, PER * i + (n - 1))
                        at = slotT[:, 1, bass.ds((2 * i + half) * P + g * G, G)]
                        v.tensor_tensor(hot_i[:, n % 2], iota, spread(at, P), ALU.is_equal).then_inc(raw_made, 1)
                        js = slotT[:, 2, bass.ds((2 * i + half) * P + g * G, G)]
                        v.tensor_tensor(hot_j[:, n % 2], iota, spread(js, P), ALU.is_equal).then_inc(j_made, 1)

            turn(0, True)
            with dve.Fori(1, TURNS) as i:
                turn(i, False)

        @block.gpsimd
        def _(pool):
            with pool.Fori(0, TURNS) as i:
                for n in range(PER):
                    half, g = n // GROUPS, n % GROUPS
                    if g == 0:
                        pool.wait_ge(gates_made, 2 * i + (half + 1))
                    pool.wait_ge(raw_made, PER * i + (n + 1))
                    nc.gpsimd.tensor_tensor(hot_i[:, n % 2], hot_i[:, n % 2], spread(gcur[:, half, g * G:(g + 1) * G], P),
                                            ALU.mult).then_inc(i_made, 1)

        @block.tensor
        def _(pe):
            def turn(i, first):
                for n in range(PER):
                    pe.wait_ge(i_made, PER * i + (n + 1))
                    pe.wait_ge(j_made, PER * i + (n + 1))
                    if not first or n >= 2:
                        pe.wait_ge(taken, PER * i + (n - 1))
                    for q in range(G):
                        mm = pe.matmul(banks[n % 2][:, q], hot_j[:, n % 2, q], hot_i[:, n % 2, q], start=True, stop=True)
                    mm.then_inc(spread_done, 1)

            turn(0, True)
            with pe.Fori(1, TURNS) as i:
                turn(i, False)

        @block.scalar
        def _(act):
            def turn(i, first):
                for n in range(PER):
                    half, g = n // GROUPS, n % GROUPS
                    if g == 0 and not first:
                        act.wait_ge(stored[half], 16 * i)
                    act.wait_ge(spread_done, PER * i + (n + 1))
                    nc.scalar.activation(wb[:, half, :, g * G:(g + 1) * G], banks[n % 2][:].rearrange("p t i -> p i t"),
                                         ACT.Copy).then_inc(taken, 1)

            turn(0, True)
            with act.Fori(1, TURNS) as i:
                turn(i, False)

        @block.sync
        def _(sp):
            with sp.Fori(0, TURNS) as i:
                for half in range(2):
                    sp.wait_ge(taken, PER * i + (half + 1) * GROUPS)
                    hold(sp, spare)
                    dst = w_dram[bass.ds(2 * i + half, 1)].rearrange("a j i t -> (a j) (i t)")
                    sp.dma_start(dst, wb[:, half].rearrange("p i t -> p (i t)")).then_inc(stored[half], 16)
            for half in range(2):
                sp.wait_ge(stored[half], 16 * TURNS)


def phase_experts(nc, const, arena, pe_t, name, u_tab, v_tab, w_dram):
    with ExitStack() as ctx:
        sem = signals(nc, ctx, name + "_")
        hhi, hlo, acc = pe_t["hhi"], pe_t["hlo"], pe_t["acc"]
        KT, S = hhi.shape[1], hhi.shape[2]
        D = KT * P
        TT = S // P
        ET = u_tab.shape[0] // P
        NBUF = 4
        TURNS = ET // NBUF
        OUTS = TT * 2
        u, vr, wt = arena("u", [P, NBUF, D]), arena("v", [P, NBUF, D]), arena("wt", [P, NBUF, S])
        uhi, ulo = arena("uhi", [P, 2, KT, P], F32R), arena("ulo", [P, 2, KT, P], F32R)
        vhi, vlo = arena("vhi", [P, 2, 2, D], F32R), arena("vlo", [P, 2, 2, D], F32R)
        phi, plo = arena("phi", [P, 2, 2, S], F32R), arena("plo", [P, 2, 2, S], F32R)
        gel, pf = arena("gel", [P, 2, S]), arena("pf", [P, 2, S])
        tb = ctx.enter_context(nc.psum_tensor(f"{name}_tb", [P, KT, P], F32))
        ub = [ctx.enter_context(nc.psum_tensor(f"{name}_ub{i}", [P, S], F32)) for i in range(2)]
        vb = [ctx.enter_context(nc.psum_tensor(f"{name}_vb{i}", [P, 512], F32)) for i in range(4)]
        u_loaded = [sem(f"u{q}_loaded") for q in range(NBUF)]
        v_loaded = [sem(f"v{q}_loaded") for q in range(NBUF)]
        w_loaded = [sem(f"w{q}_loaded") for q in range(NBUF)]
        u_turned, uhi_made, ulo_made, act_done = sem("u_turned"), sem("uhi"), sem("ulo"), sem("act_done")
        gel_made, pf_made, phi_made, plo_made = sem("gel"), sem("pf"), sem("phi"), sem("plo")
        vhi_made, vlo_made, out_done, added = sem("vhi"), sem("vlo"), sem("out_done"), sem("added")
        zeroed, spare = sem("zeroed"), sem("spare")
        block = ctx.enter_context(nc.Block())

        def loads(sp, q, e):
            experts = e * P if isinstance(e, int) else None
            rows_at = slice(experts, experts + P) if experts is not None else bass.ds(e * P, P)
            i_at = slice(e, e + 1) if isinstance(e, int) else bass.ds(e, 1)
            return (u_tab[rows_at, :], v_tab[rows_at, :], w_dram[:, :, i_at].rearrange("b j i t -> j b (i t)"))

        @block.sync
        def _(sp):
            wt_v = lambda q: wt[:, q].rearrange("p (b t) -> p b t", b=TT)
            for q in range(NBUF):
                us, vs, ws = loads(sp, q, q)
                sp.dma_start(u[:, q], us).then_inc(u_loaded[q], 16)
                sp.dma_start(wt_v(q), ws).then_inc(w_loaded[q], 16)
                sp.dma_start(vr[:, q], vs).then_inc(v_loaded[q], 16)
            with sp.Fori(1, TURNS) as i:
                for q in range(NBUF):
                    us, vs, ws = loads(sp, q, NBUF * i + q)
                    last = NBUF * i + (q - NBUF + 1)
                    sp.wait_ge(u_turned, last)
                    hold(sp, spare)
                    sp.dma_start(u[:, q], us).then_inc(u_loaded[q], 16)
                    sp.wait_ge(pf_made, last)
                    hold(sp, spare)
                    sp.dma_start(wt_v(q), ws).then_inc(w_loaded[q], 16)
                    sp.wait_ge(vlo_made, last)
                    hold(sp, spare)
                    sp.dma_start(vr[:, q], vs).then_inc(v_loaded[q], 16)

        @block.tensor
        def _(pe):
            def turn_u(q, turns, e, first=False):
                pe.wait_ge(u_loaded[q], 16 * turns)
                if not first:
                    pe.wait_ge(ulo_made, e)
                for k in range(KT):
                    mm = pe.transpose(tb[:, k], u[:, q, k * P:(k + 1) * P], const["ident"][:])
                mm.then_inc(u_turned, 1)

            def u_product(q, e, first=False):
                pe.wait_ge(ulo_made, e + 1)
                if not first:
                    pe.wait_ge(gel_made, e - 1)
                n = 0
                for k in range(KT):
                    for a, h in ((uhi, hhi), (uhi, hlo), (ulo, hhi)):
                        mm = pe.matmul(ub[q % 2][:], a[:, q % 2, k], h[:, k], start=(n == 0), stop=(n == 3 * KT - 1))
                        n += 1
                mm.then_inc(act_done, 1)

            def v_product(b, pair, first=False):
                pe.wait_ge(plo_made, 2 * pair + 2)
                pe.wait_ge(vlo_made, 2 * pair + 2)
                for o in range(OUTS):
                    if not first or o >= 4:
                        pe.wait_ge(added, OUTS * pair + (o - 3))
                    t, half = o // 2, o % 2
                    n = 0
                    for i in range(2):
                        for a, w in ((phi, vhi), (phi, vlo), (plo, vhi)):
                            mm = pe.matmul(vb[o % 4][:], a[:, b, i, t * P:(t + 1) * P], w[:, b, i, half * 512:(half + 1) * 512],
                                           start=(n == 0), stop=(n == 5))
                            n += 1
                    mm.then_inc(out_done, 1)

            def turn(i, first=False, last=False):
                for q in range(NBUF):
                    e = NBUF * i + q
                    u_product(q, e, first and q < 2)
                    if not (last and q >= 2):
                        turn_u((q + 2) % NBUF, i + 1 + (q >= 2), e + 2)
                    if q % 2 and not (first and q == 1):
                        v_product(((q // 2) + 1) % 2, 2 * i + (q // 2 - 1), first and q == 3)

            turn_u(0, 1, 0, True)
            turn_u(1, 1, 1)
            turn(0, first=True)
            with pe.Fori(1, TURNS - 1) as i:
                turn(i)
            turn(TURNS - 1, last=True)
            v_product(1, 2 * TURNS - 1)

        @block.scalar
        def _(act):
            a = nc.scalar

            def take_u(q, e):
                act.wait_ge(u_turned, e + 1)
                a.activation(uhi[:, q % 2], tb[:], ACT.Copy).then_inc(uhi_made, 1)

            def turn(i, first=False, last=False):
                for q in range(NBUF):
                    e = NBUF * i + q
                    b = q // 2
                    act.wait_ge(v_loaded[q], 16 * i + 16)
                    if not (first):
                        act.wait_ge(out_done, OUTS * (2 * i + (b - 1)))
                    a.activation(vhi[:, b, q % 2], vr[:, q], ACT.Copy).then_inc(vhi_made, 1)
                    if not (last and q >= 2):
                        take_u(q, e + 2)
                    act.wait_ge(act_done, e + 1)
                    if not (first and q < 2):
                        act.wait_ge(pf_made, e - 1)
                    a.activation(gel[:, q % 2], ub[q % 2][:], ACT.Gelu).then_inc(gel_made, 1)
                    act.wait_ge(pf_made, e + 1)
                    a.activation(phi[:, b, q % 2], pf[:, q % 2], ACT.Copy).then_inc(phi_made, 1)

            take_u(0, 0)
            take_u(1, 1)
            turn(0, first=True)
            with act.Fori(1, TURNS - 1) as i:
                turn(i)
            turn(TURNS - 1, last=True)

        @block.gpsimd
        def _(pool):
            def turn(i, first=False):
                for q in range(NBUF):
                    e = NBUF * i + q
                    pool.wait_ge(vhi_made, e + 1)
                    nc.gpsimd.tensor_tensor(vlo[:, q // 2, q % 2], vr[:, q], vhi[:, q // 2, q % 2].bitcast(F32),
                                            ALU.subtract).then_inc(vlo_made, 1)

            with pool.Fori(0, TURNS) as i:
                turn(i)

        @block.vector
        def _(dve):
            v = nc.vector

            def low_u(q, e):
                dve.wait_ge(uhi_made, e + 1)
                v.tensor_tensor(ulo[:, q % 2], tb[:], uhi[:, q % 2].bitcast(F32), ALU.subtract).then_inc(ulo_made, 1)

            def add(pair, first=False):
                for o in range(OUTS):
                    t, half = o // 2, o % 2
                    dve.wait_ge(out_done, OUTS * pair + (o + 1))
                    if not first:
                        dve.wait_ge(added, OUTS * pair + (o - OUTS + 1))
                    piece = acc[:, t, half * 512:(half + 1) * 512]
                    v.tensor_tensor(piece, piece, vb[o % 4][:], ALU.add).then_inc(added, 1)

            def turn(i, first=False, last=False):
                for q in range(NBUF):
                    e = NBUF * i + q
                    if not (last and q >= 2):
                        low_u(q, e + 2)
                    dve.wait_ge(gel_made, e + 1)
                    dve.wait_ge(w_loaded[q], 16 * i + 16)
                    if not (first and q < 2):
                        dve.wait_ge(plo_made, e - 1)
                    v.tensor_tensor(pf[:, q % 2], gel[:, q % 2], wt[:, q], ALU.mult).then_inc(pf_made, 1)
                    dve.wait_ge(phi_made, e + 1)
                    v.tensor_tensor(plo[:, q // 2, q % 2], pf[:, q % 2], phi[:, q // 2, q % 2].bitcast(F32),
                                    ALU.subtract).then_inc(plo_made, 1)
                    if q % 2 and not (first and q == 1):
                        add(2 * i + (q // 2 - 1), first and q == 3)

            v.memset(acc[:], 0.0).then_inc(zeroed, 1)
            dve.wait_ge(zeroed, 1)
            low_u(0, 0)
            low_u(1, 1)
            turn(0, first=True)
            with dve.Fori(1, TURNS - 1) as i:
                turn(i)
            turn(TURNS - 1, last=True)
            add(2 * TURNS - 1)



def hybrid_trunk(nc, x, c, ada_w, ada_b, ln_g, ln_b, rw_mu, rw_w_rkv, rw_w0, rw_w1, rw_w2, rw_a0, rw_a1, rw_a2,
                 rw_g1, rw_g2, rw_k_k, rw_k_a, rw_r_k, rw_lnx_g, rw_lnx_b, rw_w_o,
                 pl_w_in, pl_w_grp, pl_scale, pl_w_out, pe_w_q, pe_keys, pe_u, pe_v, out):
    x, out = x[0], out[0]
    S, D = x.shape
    KT, TT = D // P, S // P
    dram = lambda name, shape: nc.dram_tensor(name, shape, F32, kind="Internal").ap()
    stream = [dram(f"stream{i}", [S, D]) for i in range(3)]
    mod_rows = dram("mod_rows", [DEPTH * N_MOD * D])
    w_dram = dram("routing", [TT, P, P, P])
    base, end = (nc.sbuf_base + 31) // 32 * 32, nc.sbuf_usable_end
    fixed = Arena(nc, "const", base, end)
    const = dict(ident=fixed("ident", [P, P]), ones=fixed("ones", [P, P]), masks=fixed("masks", [P, 4 * P]),
                 blockones=fixed("blockones", [P, P]), level_masks=fixed("level_masks", [P, 6, P]),
                 pair_mask_T=fixed("pair_mask_T", [P, P]), iota=fixed("iota", [P, P]),
                 cond=fixed("cond", [P, KT]),
                 **{n: fixed(n, [P, DEPTH * N_MOD * KT]) for n in ("modT", "mod_raw", "biasT")})
    area = lambda prefix, offset=fixed.offset: Arena(nc, prefix, offset, end)

    phase_constants(nc, const, area("make"))
    phase_first_modulation(nc, const, area("mod"), c, ada_w, ada_b)

    rwa = area("rw")
    rw = {n: rwa(n, [P, KT, S]) for n in ("rT", "kT", "aT", "sT")}
    rw.update({n: rwa(n, [P, TT, D]) for n in ("v", "g")})
    rw["cols"] = rwa("cols", [P, 88])
    pr = dict(mu=rw_mu[0].rearrange("n d -> (n d)"), w0=rw_w0[0], a0=rw_a0[0], k_k=rw_k_k[0], k_a=rw_k_a[0],
              r_k=rw_r_k[0].rearrange("h n -> (h n)"), w_rkv=rw_w_rkv[0], w1=rw_w1[0], w2=rw_w2[0], a1=rw_a1[0],
              a2=rw_a2[0], g1=rw_g1[0], g2=rw_g2[0], lnx_g=rw_lnx_g[0], lnx_b=rw_lnx_b[0])
    phase_rwkv_products(nc, const, area("rwp", rwa.offset), rw, x, pr)
    phase_rwkv_scan(nc, const, area("scan", rwa.offset), rw, pr, ada_w, D, S)
    phase_last_modulation(nc, const, area("modl", rwa.offset), mod_rows)
    phase_mixer_out(nc, const, area("out0", rwa.offset), "out0", 0, None, rw["g"], rw_w_o[0], x, stream[0], mod_rows,
                    ln_g[0, 0], ln_b[0, 0])

    pea = area("peer")
    pe_t = dict(hhi=pea("hhi", [P, KT, S], F32R), hlo=pea("hlo", [P, KT, S], F32R), slotT=pea("slotT", [P, 3, S]),
                acc=pea("acc", [P, TT, D]))

    def peer(layer, src, dst):
        n = f"peer{layer}"
        phase_route(nc, const, area(n + "r", pea.offset), pe_t, n + "r", layer, src, pe_w_q[layer], pe_keys[layer])
        phase_expand(nc, const, area(n + "w", pea.offset), pe_t, n + "w", w_dram)
        phase_experts(nc, const, area(n + "e", pea.offset), pe_t, n + "e", pe_u[layer], pe_v[layer], w_dram)
        phase_mixer_out(nc, const, area(n + "o", pea.offset), n + "o", layer, None, pe_t["acc"], None, src, dst, mod_rows,
                        ln_g[layer, 1], ln_b[layer, 1], which=1)

    peer(0, stream[0], stream[1])
    pla = area("pl")
    y2T = pla("y2T", [P, KT, S])
    pp = dict(w_in=pl_w_in[0], w_grp=pl_w_grp[0], scale=pl_scale[0])
    phase_pool_products(nc, const, area("pool", pla.offset), y2T, stream[1], pp)
    phase_mixer_out(nc, const, area("out1", pla.offset), "out1", 1, y2T, None, pl_w_out[0], stream[1], stream[2], mod_rows,
                    ln_g[1, 0], ln_b[1, 0])
    peer(1, stream[2], out)


_INS = ["x", "c", "ada_w", "ada_b", "ln_g", "ln_b", "rw_mu", "rw_w_rkv", "rw_w0", "rw_w1", "rw_w2", "rw_a0", "rw_a1",
        "rw_a2", "rw_g1", "rw_g2", "rw_k_k", "rw_k_a", "rw_r_k", "rw_lnx_g", "rw_lnx_b", "rw_w_o", "pl_w_in", "pl_w_grp",
        "pl_scale", "pl_w_out", "pe_w_q", "pe_keys", "pe_u", "pe_v"]


def kernel(**inputs):
    import numpy as np
    import concourse.bacc as bacc
    from concourse.bass_utils import run_bass_kernel_spmd

    nc = bacc.Bacc("TRN2", target_bir_lowering=False, num_devices=1)
    arrays, args = {}, []
    for name in _INS:
        a = np.ascontiguousarray(inputs[name])
        arrays[f"in_{name}"] = a
        args.append(nc.dram_tensor(f"in_{name}", a.shape, mybir.dt.from_np(a.dtype), kind="ExternalInput").ap())
    args.append(nc.dram_tensor("out", arrays["in_x"].shape, F32, kind="ExternalOutput").ap())
    hybrid_trunk(nc, *args)
    r = run_bass_kernel_spmd(nc, [arrays], core_ids=[0])
    return r.results[0]["out"]
```

```python
from contextlib import ExitStack

import concourse.bass as bass
from concourse import mybir

F32 = mybir.dt.float32
F32R = mybir.dt.float32r
U32 = mybir.dt.uint32
ALU = mybir.AluOpType
ACT = mybir.ActivationFunctionType
AX = mybir.AxisListType

P = 128
HEAD = 64
TOPK = 16
POOL_WINDOWS = (2, 4, 8, 16)
DEPTH = 2
ALPHA = (2 * DEPTH) ** 0.25
LN_EPS = 1e-5
GN_EPS = 64e-5
N_MOD = 6
LOG_DECAY = -float(2.718281828459045 ** -0.5)
LOWEST = -3.0e38


class Chain:

    def __init__(self, eng, sem, per=0):
        self.eng, self.sem, self.per, self.base, self.n, self.turn = eng, sem, per, 0, 0, None

    def __call__(self, ins):
        ins.then_inc(self.sem, 1)
        self.n += 1
        if self.turn is None:
            self.eng.wait_ge(self.sem, self.base + self.n)
        else:
            self.eng.wait_ge(self.sem, self.turn * self.per + (self.base + self.n))

    def enter(self, turn):
        self.base, self.n, self.turn = self.base + self.n, 0, turn

    def leave(self, turns):
        assert self.n == self.per, f"{self.n} signals in a turn, {self.per} said"
        self.base, self.n, self.turn = self.base + turns * self.per, 0, None


def hold(eng, spare):
    eng.sem_inc(spare, 1)


def signals(nc, ctx, prefix):
    made = []

    def sem(name):
        made.append(nc.alloc_semaphore(prefix + name))
        return made[-1]

    def end():
        nc.clear_and_free_semaphores(made)
        nc.all_engine_barrier()

    ctx.callback(end)
    return sem


class Arena:

    def __init__(self, nc, prefix, offset, end):
        self.nc, self.prefix, self.offset, self.end = nc, prefix, offset, end

    def __call__(self, name, shape, dtype=F32):
        size = 4
        for n in shape[1:]:
            size *= n
        t = self.nc.alloc_sbuf_tensor_at(f"{self.prefix}_{name}", shape, dtype, offset=self.offset)
        self.offset += (size + 31) // 32 * 32
        assert self.offset <= self.end, f"{self.prefix}_{name} ends at {self.offset} of {self.end}"
        return t


def rows(ap):
    return ap.rearrange("(t p) d -> p t d", p=P)


def phase_constants(nc, const, arena):
    with ExitStack() as ctx:
        made = signals(nc, ctx, "const_")("made")
        block = ctx.enter_context(nc.Block())
        ident, ones, masks = const["ident"], const["ones"], const["masks"]
        blockones = const["blockones"]
        lvl, lvl1T, iota = const["level_masks"], const["pair_mask_T"], const["iota"]
        full = arena("full", [P, 2 * P])

        @block.gpsimd
        def _(pool):
            g = nc.gpsimd
            ch = Chain(pool, made)

            def select(out, in_, pattern, base, mult, op=ALU.is_ge, fill=0.0):
                return g.affine_select(out=out, in_=in_, pattern=pattern, compare_op=op, fill=fill, base=base,
                                       channel_multiplier=mult)

            ch(g.memset(full[:], 1.0))
            ch(g.memset(ones[:], 1.0))
            ch(g.iota(iota[:], pattern=[[1, P]], base=0, channel_multiplier=0,
                      allow_small_or_imprecise_dtypes=True))
            ch(select(ident[:], full[:, 0:P], [[-1, P]], 0, 1, ALU.is_equal))
            for j, strict in enumerate((1, 0, 1, 0)):
                ch(select(masks[:, j * P:(j + 1) * P], full[:, 0:P], [[1, P]], -strict, -1))
            b2 = blockones[:].rearrange("p (b q) -> p b q", b=2)
            ch(select(b2, full[:, 0:P].rearrange("p (b q) -> p b q", b=2), [[-HEAD, 2], [0, HEAD]], 0, 1))
            ch(select(b2, b2, [[HEAD, 2], [0, HEAD]], HEAD - 1, -1))
            for n in range(1, 7):
                half = 1 << n
                v = lvl[:, n - 1, :].rearrange("p (b q) -> p b q", q=2 * half)
                nb = P // (2 * half)
                src = full[:, 0:P].rearrange("p (b q) -> p b q", q=2 * half)
                ch(select(v, src, [[-2 * half, nb], [0, 2 * half]], -half, 1))
                ch(select(v, v, [[2 * half, nb], [0, 2 * half]], 2 * half - 1, -1))
                ch(select(v, v, [[0, nb], [-1, 2 * half]], half - 1, 0))
            v = lvl1T[:].rearrange("p (b q) -> p b q", q=2)
            ch(select(v, full[:, 0:P].rearrange("p (b q) -> p b q", q=2), [[-2, P // 2], [0, 2]], 0, 1, ALU.is_equal))
            ch(select(v, v, [[0, P // 2], [1, 2]], -1, 0))


FIRST_MODS = 2


def mod_source(ada_w, layer, n, k):
    D = ada_w.shape[1]
    return ada_w[layer, k * P:(k + 1) * P, bass.ds(n * D, D)]


def phase_first_modulation(nc, const, arena, c, ada_w, ada_b):
    with ExitStack() as ctx:
        sem = signals(nc, ctx, "mod_")
        modT, ident, cond, biasT, raw = (const[n] for n in ("modT", "ident", "cond", "biasT", "mod_raw"))
        D = ada_w.shape[1]
        KT = D // P
        NC = DEPTH * N_MOD * KT
        w, acc = arena("w", [P, FIRST_MODS, KT, D]), arena("acc", [P, FIRST_MODS, D])
        sig, in_rows = arena("sig", [P, KT]), arena("in_rows", [NC + KT, P])
        turned = ctx.enter_context(nc.psum_tensor("mod_turned", [P, 512], F32))
        sums = ctx.enter_context(nc.psum_tensor("mod_sums", [P, 512], F32))
        in_loaded, in_turned, sig_done, cond_done = sem("in_loaded"), sem("in_turned"), sem("sig"), sem("cond")
        w_loaded = [sem(f"w{i}_loaded") for i in range(FIRST_MODS * KT)]
        acc_done, sums_done = sem("acc"), sem("sums")
        block = ctx.enter_context(nc.Block())

        @block.sync
        def _(sp):
            sp.dma_start(in_rows[0:NC, :], ada_b.rearrange("l (m p) -> (l m) p", p=P)).then_inc(in_loaded, 16)
            sp.dma_start(in_rows[NC:NC + KT, :], c.rearrange("b (k p) -> (b k) p", p=P)).then_inc(in_loaded, 16)
            for m in range(FIRST_MODS):
                for k in range(KT):
                    sp.dma_start(w[:, m, k], mod_source(ada_w, 0, m, k)).then_inc(w_loaded[m * KT + k], 16)

        @block.scalar
        def _(act):
            act.wait_ge(in_turned, 1)
            nc.scalar.activation(sig[:], turned[:, NC:NC + KT], ACT.Sigmoid).then_inc(sig_done, 1)

        @block.vector
        def _(dve):
            v = nc.vector
            ch = Chain(dve, sem("dve"))
            dve.wait_ge(sig_done, 1)
            v.tensor_tensor(cond[:], turned[:, NC:NC + KT], sig[:], ALU.mult).then_inc(cond_done, 1)
            dve.wait_ge(cond_done, 1)
            ch(v.tensor_copy(biasT[:], turned[:, 0:NC]))
            for m in range(FIRST_MODS):
                for k in range(KT):
                    dve.wait_ge(w_loaded[m * KT + k], 16)
                    if k == 0:
                        ch(v.tensor_scalar(acc[:, m], w[:, m, 0], cond[:, 0:1], None, ALU.mult))
                        continue
                    ins = v.scalar_tensor_tensor(out=acc[:, m], in0=w[:, m, k], scalar=cond[:, k:k + 1], in1=acc[:, m],
                                                 op0=ALU.mult, op1=ALU.add)
                    if k < KT - 1:
                        ch(ins)
                    else:
                        ins.then_inc(acc_done, 1)
            dve.wait_ge(sums_done, 1)
            ch(v.tensor_copy(raw[:, 0:FIRST_MODS * KT], sums[:, 0:FIRST_MODS * KT]))
            ch(v.tensor_tensor(modT[:, 0:2 * KT], raw[:, 0:2 * KT], biasT[:, 0:2 * KT], ALU.add))
            v.tensor_scalar(modT[:, KT:2 * KT], modT[:, KT:2 * KT], 1.0, None, ALU.add)

        @block.tensor
        def _(pe):
            pe.wait_ge(in_loaded, 32)
            pe.transpose(turned[:, 0:NC + KT], in_rows[:], ident[0:NC + KT, 0:NC + KT]).then_inc(in_turned, 1)
            pe.wait_ge(acc_done, FIRST_MODS)
            for m in range(FIRST_MODS):
                for k in range(KT):
                    mm = pe.matmul(sums[:, m * KT + k:m * KT + k + 1], acc[:, m, k * P:(k + 1) * P], const["ones"][:, 0:1],
                                   start=True, stop=True)
            mm.then_inc(sums_done, 1)


def phase_last_modulation(nc, const, arena, mod_rows):
    with ExitStack() as ctx:
        sem = signals(nc, ctx, "modl_")
        modT, biasT, raw = const["modT"], const["biasT"], const["mod_raw"]
        NC = modT.shape[1]
        KT = NC // (DEPTH * N_MOD)
        first = FIRST_MODS * KT
        out_rows = arena("rows", [NC, P])
        bank = ctx.enter_context(nc.psum_tensor("modl_bank", [P, 512], F32))
        summed, turned, taken, stored = sem("summed"), sem("turned"), sem("taken"), sem("stored")
        block = ctx.enter_context(nc.Block())

        @block.vector
        def _(dve):
            v = nc.vector
            ch = Chain(dve, sem("dve"))
            v.tensor_tensor(raw[:], raw[:], biasT[:], ALU.add).then_inc(summed, 1)
            dve.wait_ge(summed, 1)
            ch(v.tensor_copy(modT[:, first:NC], raw[:, first:NC]))
            for layer in range(DEPTH):
                for n in (1, 4):
                    m = layer * N_MOD + n
                    if m >= FIRST_MODS:
                        cols = modT[:, m * KT:(m + 1) * KT]
                        ch(v.tensor_scalar(cols, cols, 1.0, None, ALU.add))
            dve.wait_ge(turned, 1)
            v.tensor_copy(out_rows[:], bank[0:NC, 0:P]).then_inc(taken, 1)

        @block.tensor
        def _(pe):
            pe.wait_ge(summed, 1)
            pe.transpose(bank[0:NC, 0:P], raw[:], const["ident"][:]).then_inc(turned, 1)

        @block.sync
        def _(sp):
            sp.wait_ge(taken, 1)
            sp.dma_start(mod_rows.rearrange("(m p) -> m p", p=P), out_rows[:]).then_inc(stored, 16)
            sp.wait_ge(stored, 16)



def load_x(sp, x_dram, x_sb, sem):
    for t in range(x_sb.shape[1]):
        sp.dma_start(x_sb[:, t], x_dram[:, t]).then_inc(sem[t], 16)


def turn_x(pe, const, x_sb, banks, x_loaded, x_turned, h_made):
    TT, KT = x_sb.shape[1], x_sb.shape[2] // P
    for k in range(KT):
        if k >= 2:
            pe.wait_ge(h_made, k - 1)
        for t in range(TT):
            if k == 0 and x_loaded is not None:
                pe.wait_ge(x_loaded[t], 16)
            mm = pe.transpose(banks[k % 2][:, t * P:(t + 1) * P], x_sb[:, t, k * P:(k + 1) * P], const["ident"][:])
        mm.then_inc(x_turned, 1)


def modulate(nc, dve, const, layer, which, banks, hT, at, x_turned, h_made):
    KT, S = hT.shape[1], 512
    for k in range(KT):
        dve.wait_ge(x_turned, k + 1)
        col = (layer * N_MOD + which) * KT + k
        shift, scale = const["modT"][:, col:col + 1], const["modT"][:, col + KT:col + KT + 1]
        nc.vector.tensor_scalar(hT[:, k, at:at + S], banks[k % 2][:, 0:S], scale, shift, ALU.mult,
                                ALU.add).then_inc(h_made, 1)


def phase_rwkv_products(nc, const, arena, rw, x, p):
    with ExitStack() as ctx:
        sem = signals(nc, ctx, "rwp_")
        D = x.shape[1]
        S = x.shape[0]
        KT, TT = D // P, S // P
        HALF = D // 2
        DL, AL, GL = p["w1"].shape[1], p["a1"].shape[1], p["g1"].shape[1]
        GR = GL - P
        hT = arena("hT", [P, KT, S + 1])
        xs = arena("xs", [P, 2, KT, S])
        w = arena("w", [P, 2, KT, HALF])
        w1, a1, g1 = arena("w1", [P, KT, DL]), arena("a1", [P, KT, AL]), arena("g1", [P, KT, GL])
        tw, ta, tg = arena("tw", [DL, S]), arena("ta", [AL, S]), arena("tg", [P, 2, S])
        x_sb = xs[:, 1].rearrange("p k s -> p (k s)").rearrange("p (t d) -> p t d", t=TT)
        colrows = w[:, 1].rearrange("p k s -> p (k s)")[0:88, 0:P]
        cols, mu1 = rw["cols"], arena("mu1", [P, 48])
        low = w[:, 0].rearrange("p k s -> p (k s)")
        w2, a2, g2a, g2b = (low[0:DL, 0:D], low[0:AL, D:2 * D], low[:, 2 * D:3 * D], low[0:GR, 3 * D:4 * D])
        banks = [ctx.enter_context(nc.psum_tensor(f"rwp_ps{i}", [P, 512], F32)) for i in range(7)]
        ring, xb, cb = banks[0:4], banks[4:6], banks[6]
        cols_loaded, cols_turned, cols_made, mu1_made = sem("cols_loaded"), sem("cols_turned"), sem("cols"), sem("mu1")
        x_loaded = [sem(f"x{t}_loaded") for t in range(TT)]
        x_turned, h_made, pad_made = sem("x_turned"), sem("h_made"), sem("pad_made")
        w_loaded, lora_loaded = [sem("w0_loaded"), sem("w1_loaded")], sem("lora_loaded")
        xs_made, product_done, evacuated = sem("xs_made"), sem("product_done"), sem("evacuated")
        R0, K0, V0 = 0, KT, 2 * KT
        TW = V0 + 2 * TT
        S0 = TW + 1
        TA = S0 + KT
        A0 = TA + 1
        TG = A0 + KT
        G0 = TG + 2
        END = G0 + 2 * TT
        last_use = [K0, V0, TW, S0, A0, G0]
        block = ctx.enter_context(nc.Block())

        @block.sync
        def _(sp):
            for q, (name, n) in enumerate((("mu", 6), ("w0", 1), ("a0", 1), ("k_k", 1), ("k_a", 1), ("r_k", 1))):
                r0 = 0 if q == 0 else 48 + 8 * (q - 1)
                sp.dma_start(colrows[r0:r0 + n * KT, :], p[name].rearrange("(m p) -> m p", p=P)).then_inc(cols_loaded, 16)
            load_x(sp, rows(x), x_sb, x_loaded)
            for n in range(6):
                if n == 1:
                    sp.wait_ge(cols_turned, 1)
                if n >= 2:
                    sp.wait_ge(product_done, (n - 1) * 4)
                src = p["w_rkv"][n // 2].rearrange("(k p) e -> p k e", p=P)[:, :, (n % 2) * HALF:(n % 2 + 1) * HALF]
                sp.dma_start(w[:, n % 2], src).then_inc(w_loaded[n % 2], 16)
                if n == 0:
                    for t, name in ((w1, "w1"), (a1, "a1"), (g1, "g1")):
                        sp.dma_start(t[:], p[name].rearrange("(k p) e -> p k e", p=P)).then_inc(lora_loaded, 16)
            sp.wait_ge(product_done, 5 * 4)
            for dst, src in ((w2, p["w2"]), (a2, p["a2"]), (g2a, p["g2"][0:P, :]), (g2b, p["g2"][P:GL, :])):
                sp.dma_start(dst, src).then_inc(w_loaded[0], 16)

        @block.vector
        def _(dve):
            v = nc.vector
            ch = Chain(dve, sem("dve"))
            dve.wait_ge(cols_turned, 1)
            v.tensor_copy(cols[:], cb[:, 0:88]).then_inc(cols_made, 1)
            dve.wait_ge(cols_made, 1)
            ch(v.tensor_scalar(mu1[:], cols[:, 0:48], -1.0, 1.0, ALU.mult, ALU.add))
            ch(v.memset(hT[:, :, 0:1], 0.0))
            modulate(nc, dve, const, 0, 0, xb, hT, 1, x_turned, h_made)
            dve.wait_ge(h_made, KT)
            for n in range(6):
                if n >= 2:
                    dve.wait_ge(product_done, last_use[n - 2])
                for k in range(KT):
                    ins = v.tensor_scalar(xs[:, n % 2, k], hT[:, k, 0:S], cols[:, n * KT + k:n * KT + k + 1], None, ALU.mult)
                    ins.then_inc(ch.sem, 1)
                    ch.n += 1
                dve.wait_ge(ch.sem, ch.base + ch.n)
                for k in range(KT):
                    v.scalar_tensor_tensor(out=xs[:, n % 2, k], in0=hT[:, k, 1:S + 1], scalar=mu1[:, n * KT + k:n * KT + k + 1],
                                           in1=xs[:, n % 2, k], op0=ALU.mult, op1=ALU.add).then_inc(xs_made, 1)

        @block.tensor
        def _(pe):
            pe.wait_ge(cols_loaded, 6 * 16)
            pe.transpose(cb[:, 0:88], colrows, const["ident"][0:88, 0:88]).then_inc(cols_turned, 1)
            turn_x(pe, const, x_sb, xb, x_loaded, x_turned, h_made)
            count = [0]

            def product(width, terms):
                n = count[0]
                if n >= len(ring):
                    pe.wait_ge(evacuated, n - len(ring) + 1)
                out = ring[n % len(ring)][0:width, :]
                for j, (lhsT, rhs) in enumerate(terms):
                    mm = pe.matmul(out, lhsT, rhs, start=(j == 0), stop=(j == len(terms) - 1))
                mm.then_inc(product_done, 1)
                count[0] += 1

            for n in range(2):
                pe.wait_ge(xs_made, (n + 1) * KT)
                for m in range(KT):
                    h = 2 * n + m // 4
                    pe.wait_ge(w_loaded[h % 2], 16 * (h // 2 + 1))
                    product(P, [(w[:, h % 2, k, (m % 4) * P:(m % 4 + 1) * P], xs[:, n % 2, k]) for k in range(KT)])
            pe.wait_ge(xs_made, 3 * KT)
            for half in range(2):
                pe.wait_ge(w_loaded[half], 16 * 3)
                for t in range(TT):
                    product(P, [(xs[:, 0, k, t * P:(t + 1) * P], w[:, half, k]) for k in range(KT)])
            pe.wait_ge(lora_loaded, 48)
            pe.wait_ge(xs_made, 4 * KT)
            product(DL, [(w1[:, k], xs[:, 1, k]) for k in range(KT)])
            pe.wait_ge(w_loaded[0], 16 * 7)
            pe.wait_ge(evacuated, TW + 1)
            for m in range(KT):
                product(P, [(w2[:, m * P:(m + 1) * P], tw[:])])
            pe.wait_ge(xs_made, 5 * KT)
            product(AL, [(a1[:, k], xs[:, 0, k]) for k in range(KT)])
            pe.wait_ge(evacuated, TA + 1)
            for m in range(KT):
                product(P, [(a2[:, m * P:(m + 1) * P], ta[:])])
            pe.wait_ge(xs_made, 6 * KT)
            product(P, [(g1[:, k, 0:P], xs[:, 1, k]) for k in range(KT)])
            product(GR, [(g1[:, k, P:GL], xs[:, 1, k]) for k in range(KT)])
            pe.wait_ge(evacuated, TG + 2)
            for half in range(2):
                for t in range(TT):
                    cs = slice(half * HALF, (half + 1) * HALF)
                    product(P, [(tg[:, 0, t * P:(t + 1) * P], g2a[:, cs]), (tg[0:GR, 1, t * P:(t + 1) * P], g2b[:, cs])])
            assert count[0] == END

        @block.scalar
        def _(act):
            def take(n, out, func, width=P, bias=0.0):
                act.wait_ge(product_done, n + 1)
                nc.scalar.activation(out, ring[n % len(ring)][0:width, :], func, bias=bias).then_inc(evacuated, 1)

            for m in range(KT):
                take(R0 + m, rw["rT"][:, m], ACT.Copy)
            for m in range(KT):
                take(K0 + m, rw["kT"][:, m], ACT.Copy)
            for half in range(2):
                for t in range(TT):
                    take(V0 + half * TT + t, rw["v"][:, t, half * HALF:(half + 1) * HALF], ACT.Copy)
            act.wait_ge(cols_made, 1)
            take(TW, tw[:], ACT.Tanh, DL)
            for m in range(KT):
                take(S0 + m, rw["sT"][:, m], ACT.Sigmoid, bias=cols[:, 48 + m:49 + m])
            take(TA, ta[:], ACT.Copy, AL)
            for m in range(KT):
                take(A0 + m, rw["aT"][:, m], ACT.Sigmoid, bias=cols[:, 56 + m:57 + m])
            take(TG, tg[:, 0], ACT.Sigmoid)
            take(TG + 1, tg[0:GR, 1], ACT.Sigmoid, GR)
            for half in range(2):
                for t in range(TT):
                    take(G0 + half * TT + t, rw["g"][:, t, half * HALF:(half + 1) * HALF], ACT.Copy)


def spread(cols, n):
    return cols.unsqueeze(2).to_broadcast([P, cols.shape[1], n])


def phase_rwkv_scan(nc, const, arena, rw, p, ada_w, D, S):
    with ExitStack() as ctx:
        sem = signals(nc, ctx, "scan_")
        KT, TT = D // P, S // P
        NH = D // HEAD
        RH = 8
        RT = RH * HEAD // P
        assert NH == 2 * RH
        STREAMS, SH = 2, RH // 2
        MID = P // 2 - 1
        LEVELS = 6
        AR = arena("AR", [P, KT, 2, P])
        BT, KS = arena("BT", [P, KT, P]), arena("KS", [P, KT, P])
        t0, t1, t2, t3, rkp = (arena(f"t{i}", [P, RT, P]) for i in range(5))
        state = arena("state", [P, KT, P])
        m4 = arena("m4", [P, RH, 4 * P])
        tt = arena("tt", [P, RH, 2, P])
        zs = arena("zs", [P, STREAMS, SH, P])
        qs, us = arena("qs", [P, RH * HEAD]), arena("us", [P, RH * HEAD])
        nat = arena("nat", [P, RT, 2, P])
        factor = arena("factor", [P, RT, P])
        rk_sum = arena("rk_sum", [P, KT, 2])
        RD = RH * HEAD
        y, yc, ysq = arena("y", [P, RD]), arena("yc", [P, RD]), arena("ysq", [P, RD])
        lnx_g, lnx_b = arena("lnx_g", [P, D]), arena("lnx_b", [P, D])
        cen, carry, fac = arena("cen", [P, KT]), arena("carry", [P, KT]), arena("fac", [P, KT])
        omka, bonus = arena("omka", [P, KT]), arena("bonus", [P, RH])
        st1, st2 = arena("st1", [P, RH]), arena("st2", [P, RH])
        ds_tmp = arena("ds_tmp", [P, RT, P])
        mod_w, mod_acc = arena("mod_w", [P, 2, D]), arena("mod_acc", [P, 2, D])
        zb = [ctx.enter_context(nc.psum_tensor(f"scan_z{i}", [P, SH, P], F32)) for i in range(STREAMS)]
        db = [ctx.enter_context(nc.psum_tensor(f"scan_d{i}", [P, SH, 2, P], F32)) for i in range(STREAMS)]
        sb2 = ctx.enter_context(nc.psum_tensor("scan_s", [P, 2, 512], F32))
        s0, s1 = sb2[:, 0], sb2[:, 1]
        mod_cols = s0[:, NH:NH + KT]
        cols = rw["cols"]
        c_kk, c_ka, c_rk = cols[:, 64:72], cols[:, 72:80], cols[:, 80:88]
        ident, masks, lvl, cond = const["ident"], const["masks"], const["level_masks"], const["cond"]
        rows_loaded = sem("rows_loaded")
        kk0_made, sq_made, norm_done, norm_clamped, root_made = (
            sem("kk0"), sem("sq"), sem("norm"), sem("clamped"), sem("root"))
        logs_made, exps_made, fac_made, state_scaled, stage_made = (
            sem("logs"), sem("exps"), sem("fac"), sem("state_scaled"), sem("stage"))
        factor_made, omka_made, rk_sum_made = sem("factor"), sem("omka"), sem("rk_sum")
        rk_made, bonus_done, bonus_taken = sem("rk"), sem("bonus"), sem("bonus_taken")
        nat_turned, nat_taken = sem("nat_turned"), sem("nat_taken")
        gram_done, m4_made = sem("gram"), sem("m4")
        t1T_made, t1_turned, t1_taken = sem("t1T"), sem("t1_turned"), sem("t1_taken")
        z_done, zs_made, d_done, t_added = sem("z"), sem("zs"), sem("d"), sem("t_added")
        q_done, q_taken, u_done, u_taken = sem("q"), sem("q_taken"), sem("u"), sem("u_taken")
        y_done, y_taken, ds_done, ds_taken = sem("y"), sem("y_taken"), sem("ds"), sem("ds_taken")
        yc_made, ysq_made, var_made, dev_made = sem("yc"), sem("ysq"), sem("var"), sem("dev")
        mod_loaded = [sem("mod0_loaded"), sem("mod1_loaded")]
        mod_used, mod_summed, mod_done, mod_taken = sem("mod_used"), sem("mod_summed"), sem("mod_done"), sem("mod_taken")
        s_dve, s_pool, spare, spare_sp = sem("dve"), sem("pool"), sem("spare"), sem("spare_sp")
        spare_act = sem("spare_act")
        MOD_RUNS = [(0, FIRST_MODS, (N_MOD - FIRST_MODS) // 2), (1, 0, N_MOD // 2)]
        MOD_PAIRS = sum(n for _, _, n in MOD_RUNS)
        block = ctx.enter_context(nc.Block())

        def gram_bank(j):
            s, q = j // SH, j % SH
            if q % 3 == 2:
                return zb[s][:].rearrange("p a q -> p (a q)")
            return db[s][:, 2 * (q % 3):2 * (q % 3) + 2].rearrange("p a b q -> p (a b q)")

        @block.sync
        def _(sp):
            sp.dma_start(lnx_g[:], p["lnx_g"].partition_broadcast(P)).then_inc(rows_loaded, 16)
            sp.dma_start(lnx_b[:], p["lnx_b"].partition_broadcast(P)).then_inc(rows_loaded, 16)

            def load(layer, n, k, used):
                if used is not None:
                    sp.wait_ge(mod_used, used)
                    hold(sp, spare_sp)
                sp.dma_start(mod_w[:, k % 2], mod_source(ada_w, layer, n, k)).then_inc(mod_loaded[k % 2], 16)

            before = 0
            for layer, n0, pairs in MOD_RUNS:
                start = 0
                if before == 0:
                    start = 1
                    for q in range(2):
                        for k in range(KT):
                            load(layer, n0 + q, k, None if KT * q + k < 2 else KT * q + k - 1)
                with sp.Fori(start, pairs) as i:
                    for q in range(2):
                        for k in range(KT):
                            load(layer, n0 + 2 * i + q, k, (2 * KT) * i + (2 * KT * before + KT * q + k - 1))
                before += pairs

        @block.gpsimd
        def _(pool):
            g = nc.gpsimd

            def pair(i, first):
                for q in range(2):
                    if not first:
                        pool.wait_ge(mod_done, 2 * i + (q - 1))
                    for k in range(KT):
                        n = KT * q + k
                        pool.wait_ge(mod_loaded[k % 2], 16 * KT * i + 16 * (n // 2 + 1))
                        hold(pool, spare)
                        if k == 0:
                            ins = g.tensor_scalar(mod_acc[:, q], mod_w[:, 0], cond[:, 0:1], None, ALU.mult)
                        else:
                            g.tensor_scalar(mod_w[:, k % 2], mod_w[:, k % 2], cond[:, k:k + 1], None, ALU.mult).then_inc(s_pool, 1)
                            pool.wait_ge(s_pool, (2 * KT - 2) * i + (n - q))
                            pool.wait_ge(mod_used, 2 * KT * i + n)
                            ins = g.tensor_tensor(mod_acc[:, q], mod_acc[:, q], mod_w[:, k % 2], ALU.add)
                        ins.then_inc(mod_used, 1)

            pair(0, True)
            with pool.Fori(1, MOD_PAIRS) as i:
                pair(i, False)

        @block.vector
        def _(dve):
            v = nc.vector
            ch = Chain(dve, s_dve, per=DVE_SCAN_CHAIN)
            ch(v.memset(state[:], 0.0))
            ch(v.memset(carry[:], 0.0))
            v.tensor_scalar(omka[:], c_ka, -1.0, 1.0, ALU.mult, ALU.add).then_inc(omka_made, 1)
            ends = const["blockones"][:, 0:P:HEAD].unsqueeze(1).to_broadcast([P, KT, 2])
            v.tensor_tensor(rk_sum[:], ends, spread(c_rk, 2), ALU.mult).then_inc(rk_sum_made, 1)
            dve.wait_ge(rows_loaded, 32)

            def take_mod(n):
                dve.wait_ge(mod_done, n + 1)
                v.tensor_scalar(const["mod_raw"][:, bass.ds(KT * n + FIRST_MODS * KT, KT)], mod_cols,
                                1.0, None, ALU.mult).then_inc(mod_taken, 1)

            def half(name, c, r):
                return rw[name][:, RT * r:RT * r + RT, bass.ds(c * P, P)]

            def heads(t):
                return t.rearrange("p (h n) -> p h n", n=HEAD)

            def sum_decays(K, c, r):
                for m in range(RT):
                    ins = v.tensor_tensor_scan(t2[:, m], const["ones"][:], rw["sT"][:, RT * r + m, bass.ds(c * P, P)], 0.0,
                                               ALU.mult, ALU.add)
                    if m < RT - 1:
                        ins.then_inc(s_dve, 1)
                        ch.n += 1
                ch(ins)

            def centre_decays(K, c, r):
                mine = slice(RT * r, RT * r + RT)
                ch(v.tensor_copy(cen[:, mine], t2[:, :, MID]))
                ch(v.tensor_tensor(fac[:, mine], carry[:, mine], cen[:, mine], ALU.add))
                ch(v.tensor_tensor(carry[:, mine], t2[:, :, P - 1], cen[:, mine], ALU.subtract))
                ch(v.tensor_tensor(t2[:], t2[:], spread(cen[:, mine], P), ALU.subtract))
                v.tensor_tensor(t3[:], t2[:], half("sT", c, r), ALU.subtract).then_inc(logs_made, 1)

            def scale_state(K, r):
                mine = slice(RT * r, RT * r + RT)
                dve.wait_ge(fac_made, K + 1)
                v.tensor_tensor(state[:, mine], state[:, mine], spread(fac[:, mine], P), ALU.mult).then_inc(state_scaled, 1)

            def clamp_norms(K):
                dve.wait_ge(norm_done, K + 1)
                v.tensor_scalar(t1[:], s1.rearrange("p (m s) -> p m s", s=P), 1e-24, None, ALU.max).then_inc(norm_clamped, 1)

            def invert_norms(K, part):
                mine = slice(RT // 2 * part, RT // 2 * part + RT // 2)
                if part == 0:
                    dve.wait_ge(root_made, K + 1)
                ch(v.reciprocal(t1[:, mine], t1[:, mine]))

            def make_a(K, r):
                mine = slice(RT * r, RT * r + RT)
                dve.wait_ge(kk0_made, K + 1)
                ch(v.tensor_tensor(t0[:], t0[:], t1[:], ALU.mult))
                dve.wait_ge(exps_made, K + 1)
                ch(v.scalar_tensor_tensor(out=AR[:, mine, 0], in0=t0[:], scalar=-1.0, in1=AR[:, mine, 0], op0=ALU.mult, op1=ALU.mult))

            def make_b(c, r):
                mine = slice(RT * r, RT * r + RT)
                ch(v.tensor_tensor(t1[:], t0[:], half("aT", c, r), ALU.mult))
                ch(v.tensor_tensor(BT[:, mine], t1[:], KS[:, mine], ALU.mult))

            def make_key(K, c, r):
                dve.wait_ge(factor_made, K + 1)
                ch(v.tensor_tensor(t0[:], factor[:], half("kT", c, r), ALU.mult))

            def make_kr(c, r):
                mine = slice(RT * r, RT * r + RT)
                ch(v.tensor_tensor(KS[:, mine], t0[:], KS[:, mine], ALU.mult))
                v.tensor_tensor(AR[:, mine, 1], AR[:, mine, 1], half("rT", c, r), ALU.mult).then_inc(stage_made, 1)

            def make_rk(c, r):
                v.tensor_tensor(rkp[:], t0[:], half("rT", c, r), ALU.mult).then_inc(rk_made, 1)

            def centre_y(K):
                dve.wait_ge(y_taken, K + 1)
                ch(v.tensor_reduce(st1[:], heads(y[:]), AX.X, ALU.add))
                ch(v.tensor_scalar(st1[:], st1[:], 1.0 / HEAD, None, ALU.mult))
                v.tensor_tensor(heads(yc[:]), heads(y[:]), spread(st1[:], HEAD), ALU.subtract).then_inc(yc_made, 1)

            def weigh_v(K, c, r):
                vc = rw["v"][:, bass.ds(c, 1), RD * r:RD * r + RD].rearrange("p c d -> p (c d)")
                dve.wait_ge(yc_made, K + 1)
                dve.wait_ge(bonus_taken, K + 1)
                ch(v.tensor_tensor(heads(y[:]), heads(vc), spread(bonus[:], HEAD), ALU.mult))

            def take_variance(K):
                dve.wait_ge(ysq_made, K + 1)
                ch(v.tensor_reduce(st2[:], heads(ysq[:]), AX.X, ALU.add))
                v.tensor_scalar(st2[:], st2[:], 1.0 / HEAD, GN_EPS, ALU.mult, ALU.add).then_inc(var_made, 1)

            def divide_y(K):
                dve.wait_ge(dev_made, K + 1)
                ch(v.reciprocal(st2[:], st2[:]))
                ch(v.tensor_tensor(heads(yc[:]), heads(yc[:]), spread(st2[:], HEAD), ALU.mult))

            def scale_y(r):
                ch(v.tensor_tensor(yc[:], yc[:], lnx_g[:, RD * r:RD * r + RD], ALU.mult))
                ch(v.tensor_tensor(yc[:], yc[:], lnx_b[:, RD * r:RD * r + RD], ALU.add))

            def gate_y(c, r):
                gc = rw["g"][:, bass.ds(c, 1), RD * r:RD * r + RD].rearrange("p c d -> p (c d)")
                ch(v.tensor_tensor(y[:], y[:], yc[:], ALU.add))
                ch(v.tensor_tensor(gc, gc, y[:], ALU.mult))

            def take_bonus(K):
                dve.wait_ge(bonus_done, K + 1)
                v.tensor_copy(bonus[:], s0[:, 0:RH]).then_inc(bonus_taken, 1)

            def round(K, r, c, coming=True, past=True):
                nr = 1 - r
                nc_, pc = c + r, c - 1 + r
                for s in range(STREAMS):
                    for j in range(SH * s, SH * s + SH):
                        dve.wait_ge(gram_done, RH * K + (j + 1))
                        v.tensor_tensor(m4[:, j], gram_bank(j), masks[:], ALU.mult).then_inc(m4_made, 1)
                        if coming:
                            if j == 2:
                                sum_decays(K + 1, nc_, nr)
                            elif j == 5:
                                centre_decays(K + 1, nc_, nr)
                        if past:
                            if j == 0:
                                centre_y(K - 1)
                            elif j == 1:
                                weigh_v(K - 1, pc, nr)
                    mine = slice(SH * s, SH * s + SH)
                    dve.wait_ge(m4_made, RH * K + (SH * s + SH))
                    mask = const["pair_mask_T"][:].unsqueeze(1).to_broadcast([P, SH, P])
                    eye = ident[:].unsqueeze(1).to_broadcast([P, SH, P])
                    ch(v.tensor_tensor(tt[:, mine, 1], m4[:, mine, 0:P], mask, ALU.mult))
                    v.tensor_tensor(tt[:, mine, 1], tt[:, mine, 1], eye, ALU.add).then_inc(t1T_made, 1)
                for n in range(LEVELS):
                    k0 = STREAMS * LEVELS * K + STREAMS * n
                    mask = lvl[:, n].unsqueeze(1).to_broadcast([P, SH, P])
                    for s in range(STREAMS):
                        dve.wait_ge(z_done, k0 + (s + 1))
                        v.tensor_tensor(zs[:, s], zb[s][:], mask, ALU.mult).then_inc(zs_made, 1)
                    if n == 1:
                        take_bonus(K)
                        if past:
                            take_mod(K)
                    if coming:
                        if n == 1:
                            clamp_norms(K + 1)
                        elif n == 2:
                            invert_norms(K + 1, 0)
                        elif n == 3:
                            make_a(K + 1, nr)
                        elif n == 4:
                            make_key(K + 1, nc_, nr)
                            make_kr(nc_, nr)
                    if n == 5 and past:
                        scale_y(nr)
                    for s in range(STREAMS):
                        mine = slice(SH * s, SH * s + SH)
                        dve.wait_ge(d_done, k0 + (s + 1))
                        if n < LEVELS - 1:
                            flat = lambda x: x.rearrange("p a b q -> p (a b q)")
                            v.tensor_tensor(flat(tt[:, mine]), flat(tt[:, mine]), flat(db[s][:]), ALU.add).then_inc(t_added, 1)
                        else:
                            v.tensor_tensor(tt[:, mine, 1], tt[:, mine, 1], db[s][:, :, 1], ALU.add).then_inc(t_added, 1)
                        if coming:
                            if (n, s) == (0, 0):
                                scale_state(K + 1, nr)
                            elif (n, s) == (2, 0):
                                invert_norms(K + 1, 1)
                            elif (n, s) == (3, 0):
                                make_b(nc_, nr)
                            elif (n, s) == (4, 0):
                                make_rk(nc_, nr)
                        if past:
                            if (n, s) == (0, 1):
                                take_variance(K - 1)
                            elif (n, s) == (1, 1):
                                divide_y(K - 1)
                            elif (n, s) == (5, 0):
                                gate_y(pc, nr)
                dve.wait_ge(y_done, K + 1)
                v.tensor_copy(y[:], zb[0][:].rearrange("p a q -> p (a q)")).then_inc(y_taken, 1)
                dve.wait_ge(ds_done, K + 1)
                v.tensor_tensor(ds_tmp[:], zb[1][:], const["blockones"][:].unsqueeze(1).to_broadcast([P, RT, P]),
                                ALU.mult).then_inc(ds_taken, 1)
                dve.wait_ge(ds_taken, K + 1)
                ch(v.tensor_tensor(state[:, RT * r:RT * r + RT], state[:, RT * r:RT * r + RT], ds_tmp[:], ALU.add))
                if not past:
                    take_mod(K)

            sum_decays(0, 0, 0)
            centre_decays(0, 0, 0)
            scale_state(0, 0)
            clamp_norms(0)
            invert_norms(0, 0)
            invert_norms(0, 1)
            make_a(0, 0)
            make_b(0, 0)
            make_key(0, 0, 0)
            make_kr(0, 0)
            make_rk(0, 0)
            round(0, 0, 0, past=False)
            with dve.Fori(0, TT - 1) as i:
                ch.enter(i)
                round(2 * i + 1, 1, i)
                round(2 * i + 2, 0, i + 1)
            ch.leave(TT - 1)
            round(2 * TT - 1, 1, TT - 1, coming=False)
            K = 2 * TT - 1
            centre_y(K)
            weigh_v(K, TT - 1, 1)
            take_variance(K)
            divide_y(K)
            scale_y(1)
            gate_y(TT - 1, 1)
            for n in range(2 * TT, 2 * MOD_PAIRS):
                take_mod(n)

        @block.scalar
        def _(act):
            a = nc.scalar

            def square_keys(K, c, r, first=False):
                if not first:
                    act.wait_ge(rk_made, K)
                    hold(act, spare_act)
                for m in range(RT):
                    ins = a.activation(t0[:, m], rw["kT"][:, RT * r + m, bass.ds(c * P, P)], ACT.Copy, scale=c_kk[:, RT * r + m:RT * r + m + 1])
                ins.then_inc(kk0_made, 1)
                for m in range(RT):
                    n = RT * r + m
                    ins = a.activation(factor[:, m], rw["aT"][:, n, bass.ds(c * P, P)], ACT.Identity, scale=c_ka[:, n:n + 1],
                                       bias=omka[:, n:n + 1])
                ins.then_inc(factor_made, 1)
                act.wait_ge(kk0_made, K + 1)
                a.activation(t1[:], t0[:], ACT.Square).then_inc(sq_made, 1)

            def decays(K, r):
                mine = slice(RT * r, RT * r + RT)
                act.wait_ge(logs_made, K + 1)
                a.activation(fac[:, mine], fac[:, mine], ACT.Exp, scale=LOG_DECAY).then_inc(fac_made, 1)
                a.activation(AR[:, mine, 1], t2[:], ACT.Exp, scale=LOG_DECAY)
                a.activation(KS[:, mine], t2[:], ACT.Exp, scale=-LOG_DECAY)
                a.activation(AR[:, mine, 0], t3[:], ACT.Exp, scale=LOG_DECAY).then_inc(exps_made, 1)

            def root_of_norms(K):
                act.wait_ge(norm_clamped, K + 1)
                a.activation(t1[:], t1[:], ACT.Sqrt).then_inc(root_made, 1)

            def square_y(K):
                act.wait_ge(yc_made, K + 1)
                a.activation(ysq[:], yc[:], ACT.Square).then_inc(ysq_made, 1)

            def root_of_variance(K):
                act.wait_ge(var_made, K + 1)
                a.activation(st2[:], st2[:], ACT.Sqrt).then_inc(dev_made, 1)

            def round(K, r, c, coming=True, past=True):
                if past:
                    square_y(K - 1)
                if coming:
                    square_keys(K + 1, c + r, 1 - r)
                if coming:
                    decays(K + 1, 1 - r)
                for s in range(STREAMS):
                    act.wait_ge(t1_turned, STREAMS * K + (s + 1))
                    a.activation(tt[:, SH * s:SH * s + SH, 0], zb[s][:], ACT.Copy).then_inc(t1_taken, 1)
                act.wait_ge(nat_turned, K + 1)
                a.activation(nat[:].rearrange("p a b q -> p (a b q)"), sb2[:].rearrange("p b q -> p (b q)"),
                             ACT.Copy).then_inc(nat_taken, 1)
                if past:
                    root_of_variance(K - 1)
                if coming:
                    root_of_norms(K + 1)
                act.wait_ge(q_done, K + 1)
                a.activation(qs[:], s0, ACT.Copy).then_inc(q_taken, 1)
                act.wait_ge(u_done, K + 1)
                a.activation(us[:], s1, ACT.Copy).then_inc(u_taken, 1)

            act.wait_ge(omka_made, 1)
            square_keys(0, 0, 0, first=True)
            decays(0, 0)
            root_of_norms(0)
            round(0, 0, 0, past=False)
            with act.Fori(0, TT - 1) as i:
                round(2 * i + 1, 1, i)
                round(2 * i + 2, 0, i + 1)
            round(2 * TT - 1, 1, TT - 1, coming=False)
            square_y(2 * TT - 1)
            root_of_variance(2 * TT - 1)

        @block.tensor
        def _(pe):
            def sum_mod(n, q):
                pe.wait_ge(mod_used, KT * n + KT)
                for k in range(KT):
                    mm = pe.matmul(mod_cols[:, k:k + 1], mod_acc[:, q, k * P:(k + 1) * P], const["ones"][:, 0:1],
                                   start=True, stop=True)
                mm.then_inc(mod_done, 1)

            def sum_norms(K):
                pe.wait_ge(sq_made, K + 1)
                pe.matmul(s1, const["blockones"][:], t1[:].rearrange("p k s -> p (k s)"), start=True,
                          stop=True).then_inc(norm_done, 1)

            def sum_bonus(K, r):
                pe.wait_ge(rk_made, K + 1)
                for m in range(RT):
                    mm = pe.matmul(s0[:, 2 * m:2 * m + 2], rkp[:, m], rk_sum[:, RT * r + m], start=True, stop=True)
                mm.then_inc(bonus_done, 1)

            def round(K, r, c, coming=True, first=False):
                v_at = lambda lo, hi: rw["v"][:, bass.ds(c, 1), lo:hi].rearrange("p c d -> p (c d)")
                pe.wait_ge(stage_made, K + 1)
                if not first:
                    pe.wait_ge(y_taken, K)
                    pe.wait_ge(ds_taken, K)
                for j in range(RH):
                    m, part = RT * r + j // 2, slice(HEAD * (j % 2), HEAD * (j % 2) + HEAD)
                    if j % SH == 3:
                        pe.wait_ge(m4_made, RH * K + (j - 2))
                    ar = AR[part, m].rearrange("p b q -> p (b q)")
                    out = gram_bank(j)
                    pe.matmul(out[:, 0:2 * P], BT[part, m], ar, start=True, stop=True)
                    mm = pe.matmul(out[:, 2 * P:4 * P], KS[part, m], ar, start=True, stop=True)
                    mm.then_inc(gram_done, 1)
                for q in range(RT):
                    for b, src in enumerate((BT, KS)):
                        n = 2 * q + b
                        mm = pe.transpose(sb2[:, n // 4, (n % 4) * P:(n % 4 + 1) * P], src[:, RT * r + q], ident[:])
                mm.then_inc(nat_turned, 1)
                for s in range(STREAMS):
                    pe.wait_ge(t1T_made, STREAMS * K + (s + 1))
                    for i in range(SH):
                        mm = pe.transpose(zb[s][:, i], tt[:, SH * s + i, 1], ident[:])
                    mm.then_inc(t1_turned, 1)
                for n in range(LEVELS):
                    k0 = STREAMS * LEVELS * K + STREAMS * n
                    for s in range(STREAMS):
                        if n == 0:
                            pe.wait_ge(t1_taken, STREAMS * K + (s + 1))
                        else:
                            pe.wait_ge(t_added, k0 + (s - 1))
                        for i in range(SH):
                            j = SH * s + i
                            mm = pe.matmul(zb[s][:, i], m4[:, j, 0:P], tt[:, j, 0], start=True, stop=True)
                        mm.then_inc(z_done, 1)
                    for s in range(STREAMS):
                        pe.wait_ge(zs_made, k0 + (s + 1))
                        for i in range(SH):
                            j = SH * s + i
                            if n < LEVELS - 1:
                                pe.matmul(db[s][:, i, 0], tt[:, j, 1], zs[:, s, i], start=True, stop=True)
                            mm = pe.matmul(db[s][:, i, 1], zs[:, s, i], tt[:, j, 1], start=True, stop=True)
                        mm.then_inc(d_done, 1)
                    if n == 0:
                        pe.wait_ge(nat_taken, K + 1)
                        sum_bonus(K, r)
                        if not first:
                            sum_mod(K, r)
                        if coming:
                            sum_norms(K + 1)
                pe.wait_ge(bonus_taken, K + 1)
                if not first:
                    pe.wait_ge(mod_taken, K + 1)
                if coming:
                    pe.wait_ge(norm_clamped, K + 2)
                pe.wait_ge(state_scaled, K + 1)
                for q in range(RT):
                    m = RT * r + q
                    pe.matmul(s0[:, q * P:(q + 1) * P], AR[:, m, 0], state[:, m], start=True, stop=False, skip_group_check=True)
                    for i in range(2):
                        j, lo = 2 * q + i, (2 * m + i) * HEAD
                        mm = pe.matmul(s0[:, j * HEAD:(j + 1) * HEAD], m4[:, j, 2 * P:3 * P], v_at(lo, lo + HEAD),
                                       start=False, stop=(i == 1), skip_group_check=True)
                mm.then_inc(q_done, 1)
                pe.wait_ge(t_added, STREAMS * LEVELS * K + STREAMS * LEVELS)
                pe.wait_ge(q_taken, K + 1)
                for j in range(RH):
                    mm = pe.matmul(s1[:, j * HEAD:(j + 1) * HEAD], tt[:, j, 1], qs[:, j * HEAD:(j + 1) * HEAD], start=True, stop=True)
                mm.then_inc(u_done, 1)
                pe.wait_ge(u_taken, K + 1)
                for q in range(RT):
                    m = RT * r + q
                    pe.matmul(zb[0][:, q], AR[:, m, 1], state[:, m], start=True, stop=False, skip_group_check=True)
                    for i in range(2):
                        j, lo = 2 * q + i, (2 * m + i) * HEAD
                        out = zb[0][:, q, i * HEAD:(i + 1) * HEAD]
                        pe.matmul(out, m4[:, j, P:2 * P], us[:, j * HEAD:(j + 1) * HEAD], start=False, stop=False, skip_group_check=True)
                        mm = pe.matmul(out, m4[:, j, 3 * P:4 * P], v_at(lo, lo + HEAD), start=False, stop=(i == 1),
                                       skip_group_check=True)
                mm.then_inc(y_done, 1)
                for q in range(RT):
                    m = RT * r + q
                    pe.matmul(zb[1][:, q], nat[:, q, 0], us[:, q * P:(q + 1) * P], start=True, stop=False)
                    mm = pe.matmul(zb[1][:, q], nat[:, q, 1], v_at(m * P, (m + 1) * P), start=False, stop=True)
                mm.then_inc(ds_done, 1)
                if first:
                    sum_mod(K, r)
                    pe.wait_ge(mod_taken, K + 1)

            sum_norms(0)
            pe.wait_ge(rk_sum_made, 1)
            round(0, 0, 0, first=True)
            with pe.Fori(0, TT - 1) as i:
                round(2 * i + 1, 1, i)
                round(2 * i + 2, 0, i + 1)
            round(2 * TT - 1, 1, TT - 1, coming=False)
            for n in range(2 * TT, 2 * MOD_PAIRS):
                if n > 2 * TT:
                    pe.wait_ge(mod_taken, n)
                sum_mod(n, n % 2)


DVE_SCAN_CHAIN = 58



def load_norm_rows(sp, kept, layer, which, mod_rows, ln_g, ln_b, loaded):
    D = ln_g.shape[0]
    g0 = (layer * N_MOD + 3 * which + 2) * D
    for name, row in (("gate", mod_rows[g0:g0 + D]), ("g_row", ln_g), ("b_row", ln_b)):
        sp.dma_start(kept[name][:], row.partition_broadcast(P)).then_inc(loaded, 16)


def phase_mixer_out(nc, const, arena, kept, name, yT=None, y_rows=None, w_out=None, w=None, x=None, load_norm=None, out=None):
    with ExitStack() as ctx:
        sem = signals(nc, ctx, name + "_")
        xt, gate, g_row, b_row = kept["x"], kept["gate"], kept["g_row"], kept["b_row"]
        TT, D = xt.shape[1], xt.shape[2]
        KT, S = D // P, TT * P
        t = arena("t", [P, 2, D])
        stats, mv, dev = arena("stats", [P, 2, 6]), arena("mv", [P, 2, 2]), arena("dev", [P, 2])
        if w_out is not None:
            w = arena("w", [P, KT, D])
        turned = yT is None and w is not None
        if turned:
            yT = arena("yT", [P, KT, S])
        tb = [ctx.enter_context(nc.psum_tensor(f"{name}_tb{i}", [P, 512], F32)) for i in range(2)] if turned else None
        yb = [ctx.enter_context(nc.psum_tensor(f"{name}_yb{i}", [P, 2, 512], F32)) for i in range(2)] if w is not None else None
        rows_loaded, x_loaded = sem("rows_loaded"), sem("x_loaded")
        w_loaded = [sem(f"w{k}_loaded") for k in range(KT)] if w_out is not None else None
        turned_s, taken, y_done, y_used = sem("turned"), sem("taken"), sem("y_done"), sem("y_used")
        normed, var_made, dev_made, stored = sem("normed"), sem("var"), sem("dev"), sem("stored")
        block = ctx.enter_context(nc.Block())
        @block.sync
        def _(sp):
            if w_out is not None:
                for k in range(KT):
                    sp.dma_start(w[:, k], w_out[k * P:(k + 1) * P, :]).then_inc(w_loaded[k], 16)
            if load_norm is not None:
                load_norm(sp, rows_loaded)
            if x is not None:
                sp.dma_start(xt[:], rows(x)).then_inc(x_loaded, 16)
            if out is not None:
                for i in range(TT):
                    sp.wait_ge(normed, i + 1)
                    sp.dma_start(rows(out)[:, i], xt[:, i]).then_inc(stored, 16)
                sp.wait_ge(stored, 16 * TT)

        @block.tensor
        def _(pe):
            if w is None:
                return
            if turned:
                for k in range(KT):
                    if k >= 2:
                        pe.wait_ge(taken, k - 1)
                    for i in range(TT):
                        mm = pe.transpose(tb[k % 2][:, i * P:(i + 1) * P], y_rows[:, i, k * P:(k + 1) * P], const["ident"][:])
                    mm.then_inc(turned_s, 1)
                pe.wait_ge(taken, KT)
            for i in range(TT):
                if i >= 2:
                    pe.wait_ge(y_used, i - 1)
                for half in range(2):
                    for k in range(KT):
                        if i == 0 and half == 0 and w_loaded is not None:
                            pe.wait_ge(w_loaded[k], 16)
                        mm = pe.matmul(yb[i % 2][:, half], yT[:, k, i * P:(i + 1) * P], w[:, k, half * 512:(half + 1) * 512],
                                       start=(k == 0), stop=(k == KT - 1))
                mm.then_inc(y_done, 1)

        @block.scalar
        def _(act):
            if turned:
                for k in range(KT):
                    act.wait_ge(turned_s, k + 1)
                    nc.scalar.activation(yT[:, k], tb[k % 2][:], ACT.Copy).then_inc(taken, 1)
            for i in range(TT):
                act.wait_ge(var_made, i + 1)
                nc.scalar.activation(dev[:, i % 2:i % 2 + 1], mv[:, i % 2, 1:2], ACT.Sqrt).then_inc(dev_made, 1)

        @block.vector
        def _(dve):
            v = nc.vector
            ch = Chain(dve, sem("dve"))
            if load_norm is not None:
                dve.wait_ge(rows_loaded, 48)
            if x is not None:
                dve.wait_ge(x_loaded, 16)
            for i in range(TT):
                y = y_rows[:, i] if w is None else yb[i % 2][:].rearrange("p a q -> p (a q)")
                b = i % 2
                if w is not None:
                    dve.wait_ge(y_done, i + 1)
                v.tensor_tensor(t[:, b], y, gate[:], ALU.mult).then_inc(y_used, 1)
                dve.wait_ge(y_used, i + 1)
                ch(v.scalar_tensor_tensor(out=t[:, b], in0=xt[:, i], scalar=ALPHA, in1=t[:, b], op0=ALU.mult, op1=ALU.add))
                for half in range(2):
                    ch(v.bn_stats(stats[:, half], t[:, b, half * 512:(half + 1) * 512]))
                ch(v.bn_aggr(mv[:, b], stats[:]))
                v.tensor_scalar(mv[:, b, 1:2], mv[:, b, 1:2], LN_EPS, None, ALU.add).then_inc(var_made, 1)
                dve.wait_ge(dev_made, i + 1)
                ch(v.reciprocal(dev[:, b:b + 1], dev[:, b:b + 1]))
                ch(v.tensor_scalar(t[:, b], t[:, b], mv[:, b, 0:1], dev[:, b:b + 1], ALU.subtract, ALU.mult))
                ch(v.tensor_tensor(t[:, b], t[:, b], g_row[:], ALU.mult))
                v.tensor_tensor(xt[:, i], t[:, b], b_row[:], ALU.add).then_inc(normed, 1)


def phase_pool_products(nc, const, arena, kept, y2T, w_out, load_norm, p):
    with ExitStack() as ctx:
        sem = signals(nc, ctx, "pool_")
        x_sb = kept["x"]
        TT, D = x_sb.shape[1], x_sb.shape[2]
        KT, S = D // P, TT * P
        GROUPS = len(POOL_WINDOWS)
        TPG = KT // GROUPS
        PAD = 16
        hT = arena("hT", [P, KT, S])
        w = arena("w", [P, KT, D])
        wg = arena("wg", [P, GROUPS, TPG, TPG * P])
        zT = arena("zT", [P, KT, PAD + S])
        s_a, s_b = arena("s_a", [P, TPG, PAD + S]), arena("s_b", [P, TPG, PAD + S])
        pT = arena("pT", [P, KT, S])
        inv = arena("inv", [P, GROUPS, S])
        scale_rows, scale = arena("scale_rows", [KT, P]), arena("scale", [P, KT])
        banks = [ctx.enter_context(nc.psum_tensor(f"pool_ps{i}", [P, 512], F32)) for i in range(7)]
        ring, xb, cb = banks[0:4], banks[4:6], banks[6]
        next_loaded = sem("next_loaded")
        x_turned, h_made, w_loaded, wg_loaded, scale_loaded = (
            sem("x_turned"), sem("h_made"), sem("w_loaded"), sem("wg_loaded"), sem("scale_loaded"))
        scale_turned, scale_made, counted = sem("scale_turned"), sem("scale"), sem("counted")
        product_done, z_made, p_made, y_made = sem("product"), sem("z_made"), sem("p_made"), sem("y_made")
        block = ctx.enter_context(nc.Block())

        @block.sync
        def _(sp):
            sp.dma_start(scale_rows[:], p["scale"].rearrange("(k p) -> k p", p=P)).then_inc(scale_loaded, 16)
            for k in range(KT):
                sp.dma_start(w[:, k], p["w_in"][k * P:(k + 1) * P, :]).then_inc(w_loaded, 16)
            sp.dma_start(wg[:], p["w_grp"].rearrange("g (c p) e -> p g c e", p=P)).then_inc(wg_loaded, 16)
            for k in range(KT):
                sp.dma_start(w_out[:, k], p["w_out"][k * P:(k + 1) * P, :]).then_inc(next_loaded, 16)
            load_norm(sp, next_loaded)
            sp.wait_ge(next_loaded, 16 * (KT + 3))

        @block.gpsimd
        def _(pool):
            for g, win in enumerate(POOL_WINDOWS):
                nc.gpsimd.iota(inv[:, g], pattern=[[1, S]], base=1, channel_multiplier=0,
                               allow_small_or_imprecise_dtypes=True).then_inc(counted, 1)

        @block.vector
        def _(dve):
            v = nc.vector
            ch = Chain(dve, sem("dve"))
            dve.wait_ge(scale_turned, 1)
            v.tensor_copy(scale[:], cb[:, 0:KT]).then_inc(scale_made, 1)
            ch(v.memset(zT[:, :, 0:PAD], 0.0))
            ch(v.memset(s_a[:, :, 0:PAD], 0.0))
            ch(v.memset(s_b[:, :, 0:PAD], 0.0))
            modulate(nc, dve, const, 1, 0, xb, hT, 0, x_turned, h_made)
            dve.wait_ge(counted, GROUPS)
            for g, win in enumerate(POOL_WINDOWS):
                ch(v.tensor_scalar(inv[:, g], inv[:, g], float(win), None, ALU.min))
            ch(v.reciprocal(inv[:], inv[:]))
            for g, win in enumerate(POOL_WINDOWS):
                two = slice(g * TPG, (g + 1) * TPG)
                dve.wait_ge(z_made, (g + 1) * TPG)
                src, dst, other, reach = zT[:, two], s_a, s_b, 1
                while reach < win:
                    ch(v.tensor_tensor(dst[:, :, PAD:], src[:, :, PAD:], src[:, :, PAD - reach:PAD + S - reach], ALU.add))
                    src, dst, other, reach = dst[:], other, dst, 2 * reach
                weights = inv[:, g].unsqueeze(1).to_broadcast([P, TPG, S])
                ch(v.tensor_tensor(pT[:, two], src[:, :, PAD:], weights, ALU.mult))
                v.tensor_tensor(pT[:, two], pT[:, two], zT[:, two, PAD:], ALU.subtract).then_inc(p_made, 1)

        @block.tensor
        def _(pe):
            pe.wait_ge(scale_loaded, 16)
            pe.transpose(cb[:, 0:KT], scale_rows[:], const["ident"][0:KT, 0:KT]).then_inc(scale_turned, 1)
            turn_x(pe, const, x_sb, xb, None, x_turned, h_made)
            pe.wait_ge(h_made, KT)
            pe.wait_ge(w_loaded, 16 * KT)
            for m in range(KT):
                if m >= 4:
                    pe.wait_ge(z_made, m - 3)
                for k in range(KT):
                    mm = pe.matmul(ring[m % 4][:], w[:, k, m * P:(m + 1) * P], hT[:, k], start=(k == 0), stop=(k == KT - 1))
                mm.then_inc(product_done, 1)
            pe.wait_ge(wg_loaded, 16)
            for m in range(KT):
                g = m // TPG
                pe.wait_ge(p_made, g + 1)
                if m < 4:
                    pe.wait_ge(z_made, m + 5)
                else:
                    pe.wait_ge(y_made, m - 3)
                for c in range(TPG):
                    mm = pe.matmul(ring[m % 4][:], wg[:, g, c, (m % TPG) * P:(m % TPG + 1) * P], pT[:, g * TPG + c],
                                   start=(c == 0), stop=(c == TPG - 1))
                mm.then_inc(product_done, 1)

        @block.scalar
        def _(act):
            for m in range(KT):
                act.wait_ge(product_done, m + 1)
                nc.scalar.activation(zT[:, m, PAD:], ring[m % 4][:], ACT.Copy).then_inc(z_made, 1)
            act.wait_ge(scale_made, 1)
            for m in range(KT):
                act.wait_ge(product_done, KT + m + 1)
                nc.scalar.activation(y2T[:, m], ring[m % 4][:], ACT.Copy, scale=scale[:, m:m + 1]).then_inc(y_made, 1)


def phase_route(nc, const, arena, kept, pe_t, name, layer, w_q, keys, u_tab, gelu_dram):
    with ExitStack() as ctx:
        sem = signals(nc, ctx, name + "_")
        x_sb = kept["x"]
        TT, D = x_sb.shape[1], x_sb.shape[2]
        KT, S = D // P, TT * P
        HEADS = keys.shape[0]
        TURNS = HEADS // 2
        hT = arena("hT", [P, KT, S])
        wq, kr = arena("wq", [P, 2, KT, 2 * P]), arena("kr", [P, 2, 2, P])
        keyT, qT = arena("keyT", [P, 2, 2, P]), arena("qT", [P, 2, 2, S])
        sc, rest = arena("sc", [P, 2, TT, P]), arena("rest", [P, 2, TT, P])
        val, pos = arena("val", [P, 2, TT, TOPK]), arena("pos", [P, 2, TT, TOPK], U32)
        posf = arena("posf", [P, 2, TT, TOPK])
        cand, crest = arena("cand", [P, TT, TOPK, TOPK]), arena("crest", [P, TT, TOPK, TOPK])
        best, bpos = arena("best", [P, TT, TOPK]), arena("bpos", [P, TT, TOPK], U32)
        half_u, half_f = arena("half_u", [P, 2, TT * TOPK], U32), arena("half_f", [P, 2, TT * TOPK])
        hot = arena("hot", [P, 2, TT, TOPK, TOPK])
        picked = arena("picked", [P, 2, TT, TOPK])
        expo, gate = arena("expo", [P, TT, TOPK]), arena("gate", [P, TT, TOPK])
        total = arena("total", [P, TT])
        slots = arena("slots", [P, TT, 3, HEADS * TOPK])
        slotT, hhi, hlo = pe_t["slotT"], pe_t["hhi"], pe_t["hlo"]
        xb = [ctx.enter_context(nc.psum_tensor(f"{name}_xb{i}", [P, 512], F32)) for i in range(2)]
        kb = ctx.enter_context(nc.psum_tensor(f"{name}_kb", [P, 512], F32))
        qb = [ctx.enter_context(nc.psum_tensor(f"{name}_qb{i}", [P, 512], F32)) for i in range(2)]
        sb = [ctx.enter_context(nc.psum_tensor(f"{name}_sb{i}", [P, TT, P], F32)) for i in range(2)]
        u, ut = pe_t["acc"][:, 0:2], pe_t["acc"][:, 3]
        uhi, ulo, gel = arena("uhi", [P, KT, P], F32R), arena("ulo", [P, KT, P], F32R), arena("gel", [P, HEADS, S])
        ub = ctx.enter_context(nc.psum_tensor(f"{name}_ub", [P, 512], F32))
        KH = KT // 2
        u_loaded = [sem("u0_loaded"), sem("u1_loaded")]
        u_turned, uhi_made, ut_made, ulo_made = sem("u_turned"), sem("uhi"), sem("ut"), sem("ulo")
        act_done, gel_made, gel_stored, spare_act = sem("act_done"), sem("gel"), sem("gel_stored"), sem("spare_act")
        x_turned, h_made, hhi_made, hlo_made = sem("x_turned"), sem("h_made"), sem("hhi"), sem("hlo")
        w_loaded = [sem("w0_loaded"), sem("w1_loaded")]
        key_turned, key_taken = sem("key_turned"), sem("key_taken")
        q_done, q_taken, s_done, s_taken = sem("q_done"), sem("q_taken"), sem("s_done"), sem("s_taken")
        less_made, exp_made, slots_made = sem("less"), sem("exp"), sem("slots")
        slots_turned, slotT_made = sem("slots_turned"), sem("slotT")
        s_dve, spare, spare_sp = sem("dve"), sem("spare"), sem("spare_sp")
        block = ctx.enter_context(nc.Block())
        wq_v = w_q.rearrange("(k p) e -> p k e", p=P)
        keys_v = keys.rearrange("h s k d -> k (h s) d")

        @block.sync
        def _(sp):
            for b in range(2):
                sp.dma_start(wq[:, b], wq_v[:, :, b * 2 * P:(b + 1) * 2 * P]).then_inc(w_loaded[b], 16)
                sp.dma_start(kr[:, b], keys_v[:, 2 * b:2 * b + 2]).then_inc(w_loaded[b], 16)
                sp.dma_start(u[:, b], u_tab[b * P:(b + 1) * P, :]).then_inc(u_loaded[b], 16)
            with sp.Fori(1, TURNS) as i:
                for b in range(2):
                    sp.wait_ge(q_done, 4 * i + (2 * b - 2))
                    hold(sp, spare_sp)
                    sp.dma_start(wq[:, b], wq_v[:, :, bass.ds((2 * i + b) * (2 * P), 2 * P)]).then_inc(w_loaded[b], 16)
                    sp.dma_start(kr[:, b], keys_v[:, bass.ds(4 * i + 2 * b, 2)]).then_inc(w_loaded[b], 16)
                    sp.wait_ge(u_turned, 2 * i + (b - 1))
                    hold(sp, spare_sp)
                    sp.dma_start(u[:, b], u_tab[bass.ds((2 * i + b) * P, P), :]).then_inc(u_loaded[b], 16)
            sp.wait_ge(gel_made, HEADS)
            sp.dma_start(gelu_dram.rearrange("n j t -> j n t"), gel[:]).then_inc(gel_stored, 16)
            sp.wait_ge(gel_stored, 16)

        @block.tensor
        def _(pe):
            turn_x(pe, const, x_sb, xb, None, x_turned, h_made)
            pe.wait_ge(h_made, KT)

            def head(i, b, first):
                n = 2 * i + b
                pe.wait_ge(w_loaded[b], 32 * i + 32)
                if not first:
                    pe.wait_ge(key_taken, n)
                for s in range(2):
                    mm = pe.transpose(kb[:, s * P:(s + 1) * P], kr[:, b, s], const["ident"][:])
                mm.then_inc(key_turned, 1)
                pe.wait_ge(u_loaded[b], 16 * i + 16)
                if not first:
                    pe.wait_ge(ulo_made, n)
                for k in range(KT):
                    mm = pe.transpose(xb[k // KH][:, (k % KH) * P:(k % KH + 1) * P], u[:, b, k * P:(k + 1) * P], const["ident"][:])
                mm.then_inc(u_turned, 1)
                for s in range(2):
                    if not first:
                        pe.wait_ge(q_taken, 2 * n + (s - 1))
                    for k in range(KT):
                        mm = pe.matmul(qb[s][:], wq[:, b, k, s * P:(s + 1) * P], hT[:, k], start=(k == 0), stop=(k == KT - 1))
                    mm.then_inc(q_done, 1)
                pe.wait_ge(key_taken, n + 1)
                pe.wait_ge(q_taken, 2 * n + 2)
                for s in range(2):
                    if not first:
                        pe.wait_ge(s_taken, 2 * n + (s - 1))
                    for t in range(TT):
                        mm = pe.matmul(sb[s][:, t], qT[:, b, s, t * P:(t + 1) * P], keyT[:, b, s], start=True, stop=True)
                    mm.then_inc(s_done, 1)
                pe.wait_ge(ulo_made, n + 1)
                if first:
                    pe.wait_ge(hhi_made, KT)
                    pe.wait_ge(hlo_made, KT)
                if not first:
                    pe.wait_ge(gel_made, n)
                for k in range(KT):
                    for m, (a, h) in enumerate(((uhi, hhi), (uhi, hlo), (ulo, hhi))):
                        mm = pe.matmul(ub[:], a[:, k], h[:, k], start=(k == 0 and m == 0), stop=(k == KT - 1 and m == 2))
                mm.then_inc(act_done, 1)

            head(0, 0, True)
            head(0, 1, False)
            with pe.Fori(1, TURNS) as i:
                for b in range(2):
                    head(i, b, False)
            pe.wait_ge(slots_made, TURNS)
            for q in range(3):
                bank = (xb[0], xb[1], kb)[q]
                for t in range(TT):
                    mm = pe.transpose(bank[:, t * P:(t + 1) * P], slots[:, t, q], const["ident"][:])
                mm.then_inc(slots_turned, 1)

        @block.scalar
        def _(act):
            a = nc.scalar
            for k in range(KT):
                act.wait_ge(h_made, k + 1)
                a.activation(hhi[:, k], hT[:, k], ACT.Copy).then_inc(hhi_made, 1)
            with act.Fori(0, TURNS) as i:
                for b in range(2):
                    n = 2 * i + b
                    act.wait_ge(key_turned, n + 1)
                    a.activation(keyT[:, b].rearrange("p s k -> p (s k)"), kb[:, 0:2 * P], ACT.Copy).then_inc(key_taken, 1)
                    act.wait_ge(u_turned, n + 1)
                    for h in range(2):
                        ins = a.activation(uhi[:, KH * h:KH * h + KH].rearrange("p k e -> p (k e)"), xb[h][:], ACT.Copy)
                    ins.then_inc(uhi_made, 1)
                    for h in range(2):
                        ins = a.activation(ut[:, h * KH * P:(h + 1) * KH * P], xb[h][:], ACT.Copy)
                    ins.then_inc(ut_made, 1)
                    for s in range(2):
                        act.wait_ge(q_done, 2 * n + (s + 1))
                        a.activation(qT[:, b, s], qb[s][:], ACT.Copy).then_inc(q_taken, 1)
                    for s in range(2):
                        act.wait_ge(s_done, 2 * n + (s + 1))
                        if s == 0:
                            act.wait_ge(less_made, n + 1)
                        a.activation(sc[:, s], sb[s][:], ACT.Copy).then_inc(s_taken, 1)
                    act.wait_ge(act_done, n + 1)
                    hold(act, spare_act)
                    a.activation(gel[:, bass.ds(n, 1)].rearrange("p n s -> p (n s)"), ub[:], ACT.Gelu).then_inc(gel_made, 1)
                    act.wait_ge(less_made, n + 2)
                    a.activation(expo[:], expo[:], ACT.Exp).then_inc(exp_made, 1)
            for q in range(3):
                act.wait_ge(slots_turned, q + 1)
                a.activation(slotT[:, q], (xb[0], xb[1], kb)[q][:], ACT.Copy).then_inc(slotT_made, 1)

        @block.gpsimd
        def _(pool):
            for k in range(KT):
                pool.wait_ge(hhi_made, k + 1)
                nc.gpsimd.tensor_tensor(hlo[:, k], hT[:, k], hhi[:, k].bitcast(F32), ALU.subtract).then_inc(hlo_made, 1)
            with pool.Fori(0, TURNS) as i:
                for b in range(2):
                    pool.wait_ge(uhi_made, 2 * i + (b + 1))
                    pool.wait_ge(ut_made, 2 * i + (b + 1))
                    nc.gpsimd.tensor_tensor(ulo[:].rearrange("p k e -> p (k e)"), ut,
                                            uhi[:].bitcast(F32).rearrange("p k e -> p (k e)"), ALU.subtract).then_inc(ulo_made, 1)

        @block.vector
        def _(dve):
            v = nc.vector
            ch = Chain(dve, s_dve, per=DVE_ROUTE_CHAIN)
            modulate(nc, dve, const, layer, 3, xb, hT, 0, x_turned, h_made)
            v.memset(total[:], 0.0).then_inc(less_made, 1)

            def together(instructions):
                for ins in instructions[:-1]:
                    ins.then_inc(s_dve, 1)
                    ch.n += 1
                ch(instructions[-1])

            def top16(values, rest, out, index):
                lists = range(len(values))
                hold(dve, spare)
                together([v.max(out[n][:, 0:8], values[n]) for n in lists])
                hold(dve, spare)
                together([v.match_replace(rest[n], out[n][:, 0:8], values[n], LOWEST) for n in lists] +
                         [v.max_index(index[n][:, 0:8], out[n][:, 0:8], values[n]) for n in lists])
                hold(dve, spare)
                together([v.max(out[n][:, 8:16], rest[n]) for n in lists])
                hold(dve, spare)
                together([v.max_index(index[n][:, 8:16], out[n][:, 8:16], rest[n]) for n in lists])

            with dve.Fori(0, TURNS) as i:
                ch.enter(i)
                for b in range(2):
                    n = 2 * i + b
                    for s in range(2):
                        dve.wait_ge(s_taken, 2 * n + (s + 1))
                        top16([sc[:, s, t] for t in range(TT)], [rest[:, s, t] for t in range(TT)],
                              [val[:, s, t] for t in range(TT)], [pos[:, s, t] for t in range(TT)])
                    ch(v.tensor_copy(posf[:], pos[:]))
                    first = val[:, 0].unsqueeze(3).to_broadcast([P, TT, TOPK, TOPK])
                    second = val[:, 1].unsqueeze(2).to_broadcast([P, TT, TOPK, TOPK])
                    ch(v.tensor_tensor(cand[:], first, second, ALU.add))
                    flat = lambda x, t: x[:, t].rearrange("p a b -> p (a b)")
                    top16([flat(cand, t) for t in range(TT)], [flat(crest, t) for t in range(TT)],
                          [best[:, t] for t in range(TT)], [bpos[:, t] for t in range(TT)])
                    v.tensor_tensor(expo[:], best[:], best[:, :, 0:1].to_broadcast([P, TT, TOPK]),
                                    ALU.subtract).then_inc(less_made, 1)
                    bflat = bpos[:].rearrange("p t k -> p (t k)")
                    together([v.tensor_scalar(half_u[:, 0], bflat, 4, None, ALU.logical_shift_right),
                              v.tensor_scalar(half_u[:, 1], bflat, TOPK - 1, None, ALU.bitwise_and)])
                    ch(v.tensor_copy(half_f[:], half_u[:]))
                    ranks = const["iota"][:, 0:TOPK].unsqueeze(1).to_broadcast([P, TT * TOPK, TOPK])
                    for s in range(2):
                        hs = hot[:, s].rearrange("p t a b -> p (t a) b")
                        ch(v.tensor_tensor(hs, ranks, half_f[:, s].unsqueeze(2).to_broadcast([P, TT * TOPK, TOPK]), ALU.is_equal))
                        ch(v.tensor_tensor(hot[:, s], hot[:, s], posf[:, s].unsqueeze(2).to_broadcast([P, TT, TOPK, TOPK]), ALU.mult))
                        ch(v.tensor_reduce(picked[:, s].rearrange("p t k -> p (t k)"), hs, AX.X, ALU.add))
                    dve.wait_ge(exp_made, n + 1)
                    ch(v.tensor_reduce(total[:], expo[:], AX.X, ALU.add))
                    ch(v.reciprocal(total[:], total[:]))
                    ch(v.tensor_tensor(gate[:], expo[:], spread(total[:], TOPK), ALU.mult))
                    col = bass.ds(n * TOPK, TOPK)
                    together([v.tensor_scalar(slots[:, :, 0, col], gate[:], 1.0, None, ALU.mult),
                              v.tensor_scalar(slots[:, :, 1, col], picked[:, 0], 1.0, None, ALU.mult)])
                    ins = v.tensor_scalar(slots[:, :, 2, col], picked[:, 1], 1.0, None, ALU.mult)
                    if b == 0:
                        ch(ins)
                    else:
                        ins.then_inc(slots_made, 1)
            ch.leave(TURNS)


DVE_ROUTE_CHAIN = 153


def phase_expand(nc, const, arena, pe_t, name, w_dram, u_tab, gelu_dram):
    with ExitStack() as ctx:
        sem = signals(nc, ctx, name + "_")
        G = 8
        slotT = pe_t["slotT"]
        TB = w_dram.shape[3]
        TT = slotT.shape[2] // TB
        GROUPS = TB // G
        NB = 4
        PER = 2 * GROUPS
        hot_j, hot_i = arena("hot_j", [P, NB, G, P]), arena("hot_i", [P, NB, G, P])
        wb = arena("wb", [P, 2, P, TB])
        NP = 2
        banks = [ctx.enter_context(nc.psum_tensor(f"{name}_b{n}", [P, G, P], F32)) for n in range(NP)]
        tb = ctx.enter_context(nc.psum_tensor(f"{name}_tb", [P, P * 8], F32))
        ub = ctx.enter_context(nc.psum_tensor(f"{name}_ub", [P, 512], F32))
        hhi, hlo = pe_t["hhi"], pe_t["hlo"]
        KT, S = hhi.shape[1], hhi.shape[2]
        u, gel = pe_t["acc"][:, 0:2], pe_t["acc"][:, 2].rearrange("p (b s) -> p b s", b=2)
        ut = pe_t["acc"][:, 3]
        uhi, ulo = arena("uhi", [P, KT, P], F32R), arena("ulo", [P, KT, P], F32R)
        FROM = 3
        products = [(k, a, h) for k in range(KT) for a, h in ((uhi, hhi), (uhi, hlo), (ulo, hhi))]
        SHARE = -(-len(products) // (GROUPS - FROM))
        u_loaded, gel_stored = [sem("u0_loaded"), sem("u1_loaded")], [sem("gel0_stored"), sem("gel1_stored")]
        u_turned, uhi_made, ulo_made, act_done, gel_made = sem("u_turned"), sem("uhi"), sem("ulo"), sem("act_done"), sem("gel")
        ut_made = sem("ut")
        gcur = arena("gcur", [P, 2, TB])
        j_made, raw_made, i_made, gates_made = sem("hot_j"), sem("raw_i"), sem("hot_i"), sem("gates")
        spread_done, taken, stored = sem("spread"), sem("taken"), [sem("stored0"), sem("stored1")]
        spare = sem("spare")
        block = ctx.enter_context(nc.Block())
        TURNS = TT // 2
        iota = const["iota"][:].unsqueeze(1).to_broadcast([P, G, P])

        @block.vector
        def _(dve):
            v = nc.vector

            def turn(i, first):
                for half in range(2):
                    gates = slotT[:, 0, bass.ds((2 * i + half) * TB, TB)]
                    if not first:
                        dve.wait_ge(i_made, PER * i + (half - 1) * GROUPS)
                    v.tensor_scalar(gcur[:, half], gates, 1.0, None, ALU.mult).then_inc(gates_made, 1)
                    for g in range(GROUPS):
                        n = half * GROUPS + g
                        if not first or n >= NB:
                            dve.wait_ge(spread_done, PER * i + (n + 1 - NB))
                        at = slotT[:, 1, bass.ds((2 * i + half) * TB + g * G, G)]
                        v.tensor_tensor(hot_i[:, n % NB], iota, spread(at, P), ALU.is_equal).then_inc(raw_made, 1)
                        js = slotT[:, 2, bass.ds((2 * i + half) * TB + g * G, G)]
                        v.tensor_tensor(hot_j[:, n % NB], iota, spread(js, P), ALU.is_equal).then_inc(j_made, 1)

            turn(0, True)
            with dve.Fori(1, TURNS) as i:
                turn(i, False)

        @block.gpsimd
        def _(pool):
            with pool.Fori(0, TURNS) as i:
                for n in range(PER):
                    half, g = n // GROUPS, n % GROUPS
                    if g == 0:
                        pool.wait_ge(gates_made, 2 * i + (half + 1))
                    pool.wait_ge(raw_made, PER * i + (n + 1))
                    nc.gpsimd.tensor_tensor(hot_i[:, n % NB], hot_i[:, n % NB], spread(gcur[:, half, g * G:(g + 1) * G], P),
                                            ALU.mult).then_inc(i_made, 1)
                    if g == 4:
                        pool.wait_ge(ut_made, 2 * i + (half + 1))
                        pool.wait_ge(uhi_made, 2 * i + (half + 1))
                        nc.gpsimd.tensor_tensor(ulo[:].rearrange("p k e -> p (k e)"), ut,
                                                uhi[:].bitcast(F32).rearrange("p k e -> p (k e)"), ALU.subtract).then_inc(ulo_made, 1)

        @block.tensor
        def _(pe):
            def turn(i, first):
                for n in range(PER):
                    pe.wait_ge(i_made, PER * i + (n + 1))
                    pe.wait_ge(j_made, PER * i + (n + 1))
                    if not first or n >= NP:
                        pe.wait_ge(taken, PER * i + (n + 1 - NP))
                    for q in range(G):
                        mm = pe.matmul(banks[n % NP][:, q], hot_j[:, n % NB, q], hot_i[:, n % NB, q], start=True, stop=True)
                    mm.then_inc(spread_done, 1)
                    half, g = n // GROUPS, n % GROUPS
                    if g == 0:
                        pe.wait_ge(u_loaded[half], 16 * i + 16)
                        if not (first and half == 0):
                            pe.wait_ge(ulo_made, 2 * i + half)
                        for k in range(KT):
                            mm = pe.transpose(tb[:, k * P:(k + 1) * P], u[:, half, k * P:(k + 1) * P], const["ident"][:])
                        mm.then_inc(u_turned, 1)
                    if g == FROM:
                        pe.wait_ge(ulo_made, 2 * i + (half + 1))
                        if not (first and half == 0):
                            pe.wait_ge(gel_made, 2 * i + half)
                    if g >= FROM:
                        for m in range(SHARE * (g - FROM), min(SHARE * (g - FROM + 1), len(products))):
                            k, a, h = products[m]
                            mm = pe.matmul(ub[:], a[:, k], h[:, k], start=(m == 0), stop=(m == len(products) - 1))
                    if g == GROUPS - 1:
                        mm.then_inc(act_done, 1)

            turn(0, True)
            with pe.Fori(1, TURNS) as i:
                turn(i, False)

        @block.scalar
        def _(act):
            def turn(i, first):
                for n in range(PER):
                    half, g = n // GROUPS, n % GROUPS
                    if g == 0 and not first:
                        act.wait_ge(stored[half], 16 * i)
                    act.wait_ge(spread_done, PER * i + (n + 1))
                    nc.scalar.activation(wb[:, half, :, g * G:(g + 1) * G], banks[n % NP][:].rearrange("p t i -> p i t"),
                                         ACT.Copy).then_inc(taken, 1)
                    if g == 0:
                        act.wait_ge(u_turned, 2 * i + (half + 1))
                        if not (first and half == 0):
                            act.wait_ge(act_done, 2 * i + half)
                        nc.scalar.activation(uhi[:].rearrange("p k e -> p (k e)"), tb[:], ACT.Copy).then_inc(uhi_made, 1)
                        nc.scalar.activation(ut, tb[:], ACT.Copy).then_inc(ut_made, 1)
                    if g == GROUPS - 1:
                        act.wait_ge(act_done, 2 * i + (half + 1))
                        if not first:
                            act.wait_ge(gel_stored[half], 16 * i)
                        nc.scalar.activation(gel[:, half], ub[:], ACT.Gelu).then_inc(gel_made, 1)

            turn(0, True)
            with act.Fori(1, TURNS) as i:
                turn(i, False)

        @block.sync
        def _(sp):
            def load_u(half, turn):
                at = bass.ds((2 * turn + half) * P, P) if not isinstance(turn, int) else slice((2 * turn + half) * P, (2 * turn + half + 1) * P)
                sp.dma_start(u[:, half], u_tab[at, :]).then_inc(u_loaded[half], 16)

            def turn(i, last=False):
                for half in range(2):
                    if not last:
                        sp.wait_ge(u_turned, 2 * i + (half + 1))
                        hold(sp, spare)
                        load_u(half, i + 1)
                    sp.wait_ge(taken, PER * i + (half + 1) * GROUPS)
                    hold(sp, spare)
                    dst = w_dram[bass.ds(2 * i + half, 1)].rearrange("a j i t -> (a j) (i t)")
                    sp.dma_start(dst, wb[:, half].rearrange("p i t -> p (i t)")).then_inc(stored[half], 16)
                    sp.wait_ge(gel_made, 2 * i + (half + 1))
                    hold(sp, spare)
                    dst = gelu_dram[bass.ds(2 * i + half, 1)].rearrange("a j t -> (a j) t")
                    sp.dma_start(dst, gel[:, half]).then_inc(gel_stored[half], 16)

            for half in range(2):
                load_u(half, 0)
            with sp.Fori(0, TURNS - 1) as i:
                turn(i)
            turn(TURNS - 1, last=True)
            for half in range(2):
                sp.wait_ge(stored[half], 16 * TURNS)
                sp.wait_ge(gel_stored[half], 16 * TURNS)


def phase_experts(nc, const, arena, pe_t, name, u_tab, v_tab, w_dram, gelu_dram, load_norm):
    with ExitStack() as ctx:
        sem = signals(nc, ctx, name + "_")
        hhi, hlo, acc = pe_t["hhi"], pe_t["hlo"], pe_t["acc"]
        KT, S = hhi.shape[1], hhi.shape[2]
        D = KT * P
        TT = S // P
        ET = u_tab.shape[0] // P
        NBUF = 4
        TURNS = ET // NBUF
        READY = gelu_dram.shape[0]
        EARLY = READY // NBUF
        OUTS = TT * 2
        u, vr, wt = arena("u", [P, NBUF, D]), arena("v", [P, NBUF, D]), arena("wt", [P, NBUF, S])
        uhi, ulo = arena("uhi", [P, 2, KT, P], F32R), arena("ulo", [P, 2, KT, P], F32R)
        vhi, vlo = arena("vhi", [P, 2, 2, D], F32R), arena("vlo", [P, 2, 2, D], F32R)
        phi, plo = arena("phi", [P, 2, 2, S], F32R), arena("plo", [P, 2, 2, S], F32R)
        gel, pf = arena("gel", [P, 2, S]), arena("pf", [P, 2, S])
        tb = ctx.enter_context(nc.psum_tensor(f"{name}_tb", [P, KT, P], F32))
        ub = [ctx.enter_context(nc.psum_tensor(f"{name}_ub{i}", [P, S], F32)) for i in range(2)]
        vb = [ctx.enter_context(nc.psum_tensor(f"{name}_vb{i}", [P, 512], F32)) for i in range(4)]
        u_loaded = [sem(f"u{q}_loaded") for q in range(NBUF)]
        v_loaded = [sem(f"v{q}_loaded") for q in range(NBUF)]
        w_loaded = [sem(f"w{q}_loaded") for q in range(NBUF)]
        u_turned, uhi_made, ulo_made, act_done = sem("u_turned"), sem("uhi"), sem("ulo"), sem("act_done")
        gel_made, pf_made, phi_made, plo_made = sem("gel"), sem("pf"), sem("phi"), sem("plo")
        vhi_made, vlo_made, out_done, added = sem("vhi"), sem("vlo"), sem("out_done"), sem("added")
        zeroed, next_loaded, spare = sem("zeroed"), sem("next_loaded"), sem("spare")
        block = ctx.enter_context(nc.Block())

        @block.sync
        def _(sp):
            wt_v = lambda q: wt[:, q].rearrange("p (b t) -> p b t", b=w_dram.shape[0])

            def turn(i, first=False, ready=False, after_ready=False):
                for q in range(NBUF):
                    e = NBUF * i + q
                    last = NBUF * i + (q - NBUF + 1)
                    if not first:
                        if ready or after_ready:
                            sp.wait_ge(pf_made, last)
                        else:
                            sp.wait_ge(u_turned, NBUF * i + (q - NBUF + 1 - READY))
                        hold(sp, spare)
                    if ready:
                        sp.dma_start(u[:, q, 0:S], gelu_dram[e]).then_inc(u_loaded[q], 16)
                    else:
                        sp.dma_start(u[:, q], u_tab[bass.ds(e * P, P), :]).then_inc(u_loaded[q], 16)
                    if not first:
                        sp.wait_ge(pf_made, last)
                        hold(sp, spare)
                    sp.dma_start(wt_v(q), w_dram[:, :, bass.ds(e, 1)].rearrange("b j i t -> j b (i t)")).then_inc(w_loaded[q], 16)
                    if not first:
                        sp.wait_ge(vlo_made, last)
                        hold(sp, spare)
                    sp.dma_start(vr[:, q], v_tab[bass.ds(e * P, P), :]).then_inc(v_loaded[q], 16)

            turn(0, first=True, ready=True)
            load_norm(sp, next_loaded)
            sp.wait_ge(next_loaded, 48)
            for i in range(1, EARLY):
                turn(i, ready=True)
            turn(EARLY, after_ready=True)
            with sp.Fori(EARLY + 1, TURNS) as i:
                turn(i)

        @block.tensor
        def _(pe):
            def turn_u(q, turns, e, first=False):
                pe.wait_ge(u_loaded[q], 16 * turns)
                if not first:
                    pe.wait_ge(ulo_made, e)
                for k in range(KT):
                    mm = pe.transpose(tb[:, k], u[:, q, k * P:(k + 1) * P], const["ident"][:])
                mm.then_inc(u_turned, 1)

            def u_product(q, e, first=False):
                pe.wait_ge(ulo_made, e + 1)
                if not first:
                    pe.wait_ge(gel_made, e - 1)
                n = 0
                for k in range(KT):
                    for a, h in ((uhi, hhi), (uhi, hlo), (ulo, hhi)):
                        mm = pe.matmul(ub[q % 2][:], a[:, q % 2, k], h[:, k], start=(n == 0), stop=(n == 3 * KT - 1))
                        n += 1
                mm.then_inc(act_done, 1)

            def v_product(b, pair, first=False):
                pe.wait_ge(plo_made, 2 * pair + 2)
                pe.wait_ge(vlo_made, 2 * pair + 2)
                for o in range(OUTS):
                    if not first or o >= 4:
                        pe.wait_ge(added, OUTS * pair + (o - 3))
                    t, half = o // 2, o % 2
                    n = 0
                    for i in range(2):
                        for a, w in ((phi, vhi), (phi, vlo), (plo, vhi)):
                            mm = pe.matmul(vb[o % 4][:], a[:, b, i, t * P:(t + 1) * P], w[:, b, i, half * 512:(half + 1) * 512],
                                           start=(n == 0), stop=(n == 5))
                            n += 1
                    mm.then_inc(out_done, 1)

            def turn(i, first=False, ready=False, left_first=False, last=False):
                for q in range(NBUF):
                    left = NBUF * i + (q - READY)
                    if not ready:
                        u_product(q, left, left_first and q < 2)
                    if (not ready or left + 2 >= 0) and not (last and q >= 2):
                        turn_u((q + 2) % NBUF, i + 1 + (q >= 2), left + 2, ready and left + 2 == 0)
                    if q % 2 and not (first and q == 1):
                        v_product(((q // 2) + 1) % 2, 2 * i + (q // 2 - 1), first and q == 3)

            for i in range(EARLY):
                turn(i, first=(i == 0), ready=True)
            turn(EARLY, left_first=True)
            with pe.Fori(EARLY + 1, TURNS - 1) as i:
                turn(i)
            turn(TURNS - 1, last=True)
            v_product(1, 2 * TURNS - 1)

        @block.scalar
        def _(act):
            a = nc.scalar

            def take_u(q, e):
                act.wait_ge(u_turned, e + 1)
                a.activation(uhi[:, q % 2], tb[:], ACT.Copy).then_inc(uhi_made, 1)

            def turn(i, first=False, ready=False, last=False):
                for q in range(NBUF):
                    e = NBUF * i + q
                    left = NBUF * i + (q - READY)
                    b = q // 2
                    act.wait_ge(v_loaded[q], 16 * i + 16)
                    if not (first):
                        act.wait_ge(out_done, OUTS * (2 * i + (b - 1)))
                    a.activation(vhi[:, b, q % 2], vr[:, q], ACT.Copy).then_inc(vhi_made, 1)
                    if (not ready or left + 2 >= 0) and not (last and q >= 2):
                        take_u(q, left + 2)
                    if not ready:
                        act.wait_ge(act_done, left + 1)
                        act.wait_ge(pf_made, e - 1)
                        a.activation(gel[:, q % 2], ub[q % 2][:], ACT.Gelu).then_inc(gel_made, 1)
                    act.wait_ge(pf_made, e + 1)
                    a.activation(phi[:, b, q % 2], pf[:, q % 2], ACT.Copy).then_inc(phi_made, 1)

            for i in range(EARLY):
                turn(i, first=(i == 0), ready=True)
            with act.Fori(EARLY, TURNS - 1) as i:
                turn(i)
            turn(TURNS - 1, last=True)

        @block.gpsimd
        def _(pool):
            def turn(i, first=False):
                for q in range(NBUF):
                    e = NBUF * i + q
                    pool.wait_ge(vhi_made, e + 1)
                    nc.gpsimd.tensor_tensor(vlo[:, q // 2, q % 2], vr[:, q], vhi[:, q // 2, q % 2].bitcast(F32),
                                            ALU.subtract).then_inc(vlo_made, 1)

            with pool.Fori(0, TURNS) as i:
                turn(i)

        @block.vector
        def _(dve):
            v = nc.vector

            def low_u(q, e):
                dve.wait_ge(uhi_made, e + 1)
                v.tensor_tensor(ulo[:, q % 2], tb[:], uhi[:, q % 2].bitcast(F32), ALU.subtract).then_inc(ulo_made, 1)

            def add(pair, first=False):
                for o in range(OUTS):
                    t, half = o // 2, o % 2
                    dve.wait_ge(out_done, OUTS * pair + (o + 1))
                    if not first:
                        dve.wait_ge(added, OUTS * pair + (o - OUTS + 1))
                    piece = acc[:, t, half * 512:(half + 1) * 512]
                    v.tensor_tensor(piece, piece, vb[o % 4][:], ALU.add).then_inc(added, 1)

            def turn(i, first=False, ready=False, last=False):
                for q in range(NBUF):
                    e = NBUF * i + q
                    left = NBUF * i + (q - READY)
                    if (not ready or left + 2 >= 0) and not (last and q >= 2):
                        low_u(q, left + 2)
                    if ready:
                        dve.wait_ge(u_loaded[q], 16 * i + 16)
                    else:
                        dve.wait_ge(gel_made, left + 1)
                    dve.wait_ge(w_loaded[q], 16 * i + 16)
                    if not (first and q < 2):
                        dve.wait_ge(plo_made, e - 1)
                    g = u[:, q, 0:S] if ready else gel[:, q % 2]
                    v.tensor_tensor(pf[:, q % 2], g, wt[:, q], ALU.mult).then_inc(pf_made, 1)
                    dve.wait_ge(phi_made, e + 1)
                    v.tensor_tensor(plo[:, q // 2, q % 2], pf[:, q % 2], phi[:, q // 2, q % 2].bitcast(F32),
                                    ALU.subtract).then_inc(plo_made, 1)
                    if q % 2 and not (first and q == 1):
                        add(2 * i + (q // 2 - 1), first and q == 3)

            v.memset(acc[:], 0.0).then_inc(zeroed, 1)
            dve.wait_ge(zeroed, 1)
            for i in range(EARLY):
                turn(i, first=(i == 0), ready=True)
            with dve.Fori(EARLY, TURNS - 1) as i:
                turn(i)
            turn(TURNS - 1, last=True)
            add(2 * TURNS - 1)



def hybrid_trunk(nc, x, c, ada_w, ada_b, ln_g, ln_b, rw_mu, rw_w_rkv, rw_w0, rw_w1, rw_w2, rw_a0, rw_a1, rw_a2,
                 rw_g1, rw_g2, rw_k_k, rw_k_a, rw_r_k, rw_lnx_g, rw_lnx_b, rw_w_o,
                 pl_w_in, pl_w_grp, pl_scale, pl_w_out, pe_w_q, pe_keys, pe_u, pe_v, out):
    x, out = x[0], out[0]
    S, D = x.shape
    KT, TT = D // P, S // P
    dram = lambda name, shape: nc.dram_tensor(name, shape, F32, kind="Internal").ap()
    mod_rows = dram("mod_rows", [DEPTH * N_MOD * D])
    w_dram = dram("routing", [S // 64, P, P, 64])
    BESIDE_ROUTE = pe_keys.shape[1]
    gelu_dram = dram("activations", [BESIDE_ROUTE + S // w_dram.shape[3], P, S])
    base, end = (nc.sbuf_base + 31) // 32 * 32, nc.sbuf_usable_end
    fixed = Arena(nc, "const", base, end)
    const = dict(ident=fixed("ident", [P, P]), ones=fixed("ones", [P, P]), masks=fixed("masks", [P, 4 * P]),
                 blockones=fixed("blockones", [P, P]), level_masks=fixed("level_masks", [P, 6, P]),
                 pair_mask_T=fixed("pair_mask_T", [P, P]), iota=fixed("iota", [P, P]),
                 cond=fixed("cond", [P, KT]),
                 **{n: fixed(n, [P, DEPTH * N_MOD * KT]) for n in ("modT", "mod_raw", "biasT")})
    kept_at = (end - 4 * (S // P + 3) * D) // 32 * 32
    area = lambda prefix, offset=fixed.offset, end=end: Arena(nc, prefix, offset, end)
    late = lambda prefix, offset: area(prefix, offset, kept_at)

    phase_constants(nc, const, area("make"))
    phase_first_modulation(nc, const, area("mod"), c, ada_w, ada_b)

    rwa = area("rw")
    rw = {n: rwa(n, [P, KT, S]) for n in ("rT", "kT", "aT", "sT")}
    rw.update({n: rwa(n, [P, TT, D]) for n in ("v", "g")})
    rw["cols"] = rwa("cols", [P, 88])
    pr = dict(mu=rw_mu[0].rearrange("n d -> (n d)"), w0=rw_w0[0], a0=rw_a0[0], k_k=rw_k_k[0], k_a=rw_k_a[0],
              r_k=rw_r_k[0].rearrange("h n -> (h n)"), w_rkv=rw_w_rkv[0], w1=rw_w1[0], w2=rw_w2[0], a1=rw_a1[0],
              a2=rw_a2[0], g1=rw_g1[0], g2=rw_g2[0], lnx_g=rw_lnx_g[0], lnx_b=rw_lnx_b[0])
    phase_rwkv_products(nc, const, area("rwp", rwa.offset), rw, x, pr)
    phase_rwkv_scan(nc, const, area("scan", rwa.offset), rw, pr, ada_w, D, S)
    phase_last_modulation(nc, const, area("modl", rwa.offset), mod_rows)

    keep = area("kept", kept_at)
    kept = dict(x=keep("x", [P, TT, D]), **{n: keep(n, [P, D]) for n in ("gate", "g_row", "b_row")})
    norm_loads = lambda layer, which: lambda sp, loaded: load_norm_rows(sp, kept, layer, which, mod_rows, ln_g[layer, which],
                                                                        ln_b[layer, which], loaded)
    phase_mixer_out(nc, const, late("out0", rwa.offset), kept, "out0", y_rows=rw["g"], w_out=rw_w_o[0], x=x,
                    load_norm=norm_loads(0, 0))

    pea = late("peer", fixed.offset)
    pe_t = dict(hhi=pea("hhi", [P, KT, S], F32R), hlo=pea("hlo", [P, KT, S], F32R), slotT=pea("slotT", [P, 3, S]),
                acc=pea("acc", [P, TT, D]))

    def peer(layer, dst):
        n = f"peer{layer}"
        phase_route(nc, const, late(n + "r", pea.offset), kept, pe_t, n + "r", layer, pe_w_q[layer], pe_keys[layer],
                    pe_u[layer, 0:BESIDE_ROUTE * P], gelu_dram[0:BESIDE_ROUTE])
        phase_expand(nc, const, late(n + "w", pea.offset), pe_t, n + "w", w_dram, pe_u[layer, BESIDE_ROUTE * P:], gelu_dram[BESIDE_ROUTE:])
        phase_experts(nc, const, late(n + "e", pea.offset), pe_t, n + "e", pe_u[layer], pe_v[layer], w_dram, gelu_dram,
                      norm_loads(layer, 1))
        phase_mixer_out(nc, const, late(n + "o", pea.offset), kept, n + "o", y_rows=pe_t["acc"], out=dst)

    peer(0, None)
    pla = late("pl", fixed.offset)
    y2T, w_out = pla("y2T", [P, KT, S]), pla("w_out", [P, KT, D])
    pp = dict(w_in=pl_w_in[0], w_grp=pl_w_grp[0], scale=pl_scale[0], w_out=pl_w_out[0])
    phase_pool_products(nc, const, late("pool", pla.offset), kept, y2T, w_out, norm_loads(1, 0), pp)
    phase_mixer_out(nc, const, late("out1", pla.offset), kept, "out1", yT=y2T, w=w_out)
    peer(1, out)


_INS = ["x", "c", "ada_w", "ada_b", "ln_g", "ln_b", "rw_mu", "rw_w_rkv", "rw_w0", "rw_w1", "rw_w2", "rw_a0", "rw_a1",
        "rw_a2", "rw_g1", "rw_g2", "rw_k_k", "rw_k_a", "rw_r_k", "rw_lnx_g", "rw_lnx_b", "rw_w_o", "pl_w_in", "pl_w_grp",
        "pl_scale", "pl_w_out", "pe_w_q", "pe_keys", "pe_u", "pe_v"]


def kernel(**inputs):
    import numpy as np
    import concourse.bacc as bacc
    from concourse.bass_utils import run_bass_kernel_spmd

    nc = bacc.Bacc("TRN2", target_bir_lowering=False, num_devices=1)
    arrays, args = {}, []
    for name in _INS:
        a = np.ascontiguousarray(inputs[name])
        arrays[f"in_{name}"] = a
        args.append(nc.dram_tensor(f"in_{name}", a.shape, mybir.dt.from_np(a.dtype), kind="ExternalInput").ap())
    args.append(nc.dram_tensor("out", arrays["in_x"].shape, F32, kind="ExternalOutput").ap())
    hybrid_trunk(nc, *args)
    r = run_bass_kernel_spmd(nc, [arrays], core_ids=[0])
    return r.results[0]["out"]
```
